# Optimizing a Trainium2 kernel written in Bass

```python
import jax
import jax.numpy as jnp
from jax import lax
import numpy as np

D_MODEL = 1024
BATCH = 1
SEQ = 256
DEPTH = 2

CHUNK = 64
HEAD_DIM = 64
A_Q_HEADS = 6
A_KV_HEADS = 2
A_GROUP = A_Q_HEADS // A_KV_HEADS
A_WINDOW = 128
A_PREV = A_WINDOW // CHUNK - 1
B_GROUPS = 4
B_BLOCK = 128
C_HEADS = 6
C_PREV = 8
C_REL_CLIP = 256
C_REL_SIZE = CHUNK + C_REL_CLIP

A_WIDTH = A_Q_HEADS * HEAD_DIM
A_KV_WIDTH = A_KV_HEADS * HEAD_DIM
B_WIDTH = B_GROUPS * HEAD_DIM
C_WIDTH = C_HEADS * HEAD_DIM
MIX_WIDTH = A_WIDTH + B_WIDTH + C_WIDTH
_A_END = A_WIDTH + 2 * A_KV_WIDTH
_B_END = _A_END + 2 * B_WIDTH
IN_SPLITS = [A_WIDTH, A_WIDTH + A_KV_WIDTH, _A_END, _A_END + B_WIDTH, _B_END, _B_END + C_WIDTH, _B_END + 2 * C_WIDTH]
IN_WIDTH = _B_END + 3 * C_WIDTH

D_FF = 2816
N_EXPERTS = 8
TOP_K = 2
D_FF_EXPERT = 3584
N_DENSE = (DEPTH + 1) // 2
N_MOE = DEPTH // 2
EPS = 1e-6
NEG_INF = -1e30

kernel_name = 'hybrid_chunk_causal_head_groups_moe'

def rms_norm(x, g):
    xf = x.astype(jnp.float32)
    y = xf * lax.rsqrt(jnp.mean(xf * xf, axis=-1, keepdims=True) + EPS)
    return (y * g.astype(jnp.float32)).astype(x.dtype)

def layer_norm(x, g, b):
    xf = x.astype(jnp.float32)
    mu = jnp.mean(xf, axis=-1, keepdims=True)
    xc = xf - mu
    y = xc * lax.rsqrt(jnp.mean(xc * xc, axis=-1, keepdims=True) + EPS)
    return (y * g.astype(jnp.float32) + b.astype(jnp.float32)).astype(x.dtype)

def chunk_band(t, n_prev):
    nb, nc = t.shape[0], t.shape[1]
    tp = jnp.pad(t, ((0, 0), (n_prev, 0), (0, 0), (0, 0), (0, 0)))
    band = jnp.stack([tp[:, j:j + nc] for j in range(n_prev + 1)], axis=2)
    return band.reshape(nb, nc, (n_prev + 1) * CHUNK, t.shape[3], t.shape[4])

def band_valid(nc, n_prev):
    n = jnp.arange(nc)[:, None]
    kk = jnp.arange((n_prev + 1) * CHUNK)[None, :]
    return (n - n_prev + kk // CHUNK) >= 0

def band_rel(n_prev):
    qi = jnp.arange(CHUNK)[:, None]
    kk = jnp.arange((n_prev + 1) * CHUNK)[None, :]
    return qi + n_prev * CHUNK - kk

def mixer_a(q, k, v, qn_g, kn_g, sinks):
    nb, s_len = q.shape[0], q.shape[1]
    nc = s_len // CHUNK
    q = rms_norm(q, qn_g).reshape(nb, nc, CHUNK, A_KV_HEADS, A_GROUP, HEAD_DIM)
    k = chunk_band(rms_norm(k, kn_g).reshape(nb, nc, CHUNK, A_KV_HEADS, HEAD_DIM), A_PREV)
    v = chunk_band(v.reshape(nb, nc, CHUNK, A_KV_HEADS, HEAD_DIM), A_PREV)
    s = jnp.einsum('bnqhgd,bnkhd->bhgnqk', q, k).astype(jnp.float32) * (HEAD_DIM ** -0.5)
    slopes = jnp.exp2(-8.0 * jnp.arange(1, A_Q_HEADS + 1, dtype=jnp.float32) / A_Q_HEADS).reshape(A_KV_HEADS, A_GROUP)
    dist = jnp.abs(band_rel(A_PREV)).astype(jnp.float32)
    s = s - slopes[:, :, None, None, None] * dist
    s = jnp.where(band_valid(nc, A_PREV)[:, None, :], s, NEG_INF)
    sink = sinks.astype(jnp.float32).reshape(A_KV_HEADS, A_GROUP)[:, :, None, None, None]
    m = jnp.maximum(jnp.max(s, axis=-1, keepdims=True), sink)
    p = jnp.exp(s - m)
    p = p / (jnp.sum(p, axis=-1, keepdims=True) + jnp.exp(sink - m))
    o = jnp.einsum('bhgnqk,bnkhd->bnqhgd', p.astype(v.dtype), v)
    return o.reshape(nb, s_len, A_WIDTH)

def mixer_b(u, v, ln_g, ln_b, w_s, b_s):
    nb, s_len = u.shape[0], u.shape[1]
    nblk = s_len // B_BLOCK
    u = jax.nn.gelu(u, approximate=False)
    v = jax.nn.gelu(v, approximate=False).reshape(nb, s_len, B_GROUPS, HEAD_DIM)
    v = layer_norm(v, ln_g.reshape(B_GROUPS, HEAD_DIM), ln_b.reshape(B_GROUPS, HEAD_DIM))
    v = v.reshape(nb, nblk, B_BLOCK, B_GROUPS, HEAD_DIM)
    pos = jnp.arange(B_BLOCK) // CHUNK
    mask = pos[None, :] <= pos[:, None]
    w = jnp.where(mask, w_s, jnp.zeros_like(w_s))
    s = jnp.einsum('gij,bnjgd->bnigd', w, v) + b_s.T[:, :, None]
    return u * s.reshape(nb, s_len, B_WIDTH)

def mixer_c(q, k, v, qn_g, kn_g, rel_bias):
    nb, s_len = q.shape[0], q.shape[1]
    nc = s_len // CHUNK
    q = rms_norm(q, qn_g).reshape(nb, nc, CHUNK, C_HEADS, HEAD_DIM)
    k = chunk_band(rms_norm(k, kn_g).reshape(nb, nc, CHUNK, C_HEADS, HEAD_DIM), C_PREV)
    v = chunk_band(v.reshape(nb, nc, CHUNK, C_HEADS, HEAD_DIM), C_PREV)
    s = jnp.einsum('bnqhd,bnkhd->bhnqk', q, k).astype(jnp.float32) * (HEAD_DIM ** -0.5)
    idx = jnp.clip(band_rel(C_PREV), -(CHUNK - 1), C_REL_CLIP) + (CHUNK - 1)
    s = s + rel_bias.astype(jnp.float32)[:, idx][:, None]
    s = jnp.where(band_valid(nc, C_PREV)[:, None, :], s, NEG_INF)
    p = jax.nn.softmax(s, axis=-1)
    o = jnp.einsum('bhnqk,bnkhd->bnqhd', p.astype(v.dtype), v)
    return o.reshape(nb, s_len, C_WIDTH)

def swiglu(h, wg, wu, wd):
    return jnp.matmul(jax.nn.silu(jnp.matmul(h, wg)) * jnp.matmul(h, wu), wd)

def moe(h, w_router, wg, wu, wd):
    shape = h.shape
    t = h.reshape(-1, shape[-1])
    logits = jnp.matmul(t, w_router).astype(jnp.float32)
    top_v, top_i = lax.top_k(logits, TOP_K)
    gates = jax.nn.softmax(top_v, axis=-1)
    combine = jnp.sum(jax.nn.one_hot(top_i, N_EXPERTS, dtype=jnp.float32) * gates[..., None], axis=1)
    y = jnp.zeros_like(t)
    for e in range(N_EXPERTS):
        y = y + combine[:, e:e + 1].astype(t.dtype) * swiglu(t, wg[e], wu[e], wd[e])
    return y.reshape(shape)

def setup_inputs(seed: int = 0) -> dict:
    key = jax.random.key(seed)
    ks = jax.random.split(key, 24)

    def nrm(k, shape, scale):
        return jax.random.normal(k, shape, jnp.float32) * scale

    return {
        'x': nrm(ks[0], (BATCH, SEQ, D_MODEL), 1.0),
        'g_mix': 1.0 + nrm(ks[1], (DEPTH, D_MODEL), 0.02),
        'w_in': nrm(ks[2], (DEPTH, D_MODEL, IN_WIDTH), D_MODEL ** -0.5),
        'qn_a': 1.0 + nrm(ks[3], (DEPTH, HEAD_DIM), 0.02),
        'kn_a': 1.0 + nrm(ks[4], (DEPTH, HEAD_DIM), 0.02),
        'sinks_a': nrm(ks[5], (DEPTH, A_Q_HEADS), 1.0),
        'ln_b_g': 1.0 + nrm(ks[6], (DEPTH, B_WIDTH), 0.02),
        'ln_b_b': nrm(ks[7], (DEPTH, B_WIDTH), 0.02),
        'w_s': nrm(ks[8], (DEPTH, B_GROUPS, B_BLOCK, B_BLOCK), B_BLOCK ** -0.5),
        'b_s': 1.0 + nrm(ks[9], (DEPTH, B_GROUPS, B_BLOCK), 0.1),
        'qn_c': 1.0 + nrm(ks[10], (DEPTH, HEAD_DIM), 0.02),
        'kn_c': 1.0 + nrm(ks[11], (DEPTH, HEAD_DIM), 0.02),
        'rel_bias_c': nrm(ks[12], (DEPTH, C_HEADS, C_REL_SIZE), 0.5),
        'g_out': 1.0 + nrm(ks[13], (DEPTH, MIX_WIDTH), 0.02),
        'w_out': nrm(ks[14], (DEPTH, MIX_WIDTH, D_MODEL), MIX_WIDTH ** -0.5),
        'g_ffn': 1.0 + nrm(ks[15], (DEPTH, D_MODEL), 0.02),
        'w_gate_d': nrm(ks[16], (N_DENSE, D_MODEL, D_FF), D_MODEL ** -0.5),
        'w_up_d': nrm(ks[17], (N_DENSE, D_MODEL, D_FF), D_MODEL ** -0.5),
        'w_down_d': nrm(ks[18], (N_DENSE, D_FF, D_MODEL), D_FF ** -0.5),
        'w_router': nrm(ks[19], (N_MOE, D_MODEL, N_EXPERTS), D_MODEL ** -0.5),
        'w_gate_e': nrm(ks[20], (N_MOE, N_EXPERTS, D_MODEL, D_FF_EXPERT), D_MODEL ** -0.5),
        'w_up_e': nrm(ks[21], (N_MOE, N_EXPERTS, D_MODEL, D_FF_EXPERT), D_MODEL ** -0.5),
        'w_down_e': nrm(ks[22], (N_MOE, N_EXPERTS, D_FF_EXPERT, D_MODEL), D_FF_EXPERT ** -0.5),
    }

def reference(x, g_mix, w_in, qn_a, kn_a, sinks_a, ln_b_g, ln_b_b, w_s, b_s, qn_c, kn_c, rel_bias_c, g_out, w_out, g_ffn, w_gate_d, w_up_d, w_down_d, w_router, w_gate_e, w_up_e, w_down_e):
    nb, s_len = x.shape[0], x.shape[1]
    for l in range(DEPTH):
        h = rms_norm(x, g_mix[l])
        proj = jnp.matmul(h, w_in[l])
        aq, ak, av, bu, bv, cq, ck, cv = jnp.split(proj, IN_SPLITS, axis=-1)
        o_a = mixer_a(aq.reshape(nb, s_len, A_Q_HEADS, HEAD_DIM),
                      ak.reshape(nb, s_len, A_KV_HEADS, HEAD_DIM),
                      av.reshape(nb, s_len, A_KV_HEADS, HEAD_DIM),
                      qn_a[l], kn_a[l], sinks_a[l])
        o_b = mixer_b(bu, bv, ln_b_g[l], ln_b_b[l], w_s[l], b_s[l])
        o_c = mixer_c(cq.reshape(nb, s_len, C_HEADS, HEAD_DIM),
                      ck.reshape(nb, s_len, C_HEADS, HEAD_DIM),
                      cv.reshape(nb, s_len, C_HEADS, HEAD_DIM),
                      qn_c[l], kn_c[l], rel_bias_c[l])
        go = g_out[l]
        mix = jnp.concatenate([
            rms_norm(o_a, go[:A_WIDTH]),
            rms_norm(o_b, go[A_WIDTH:A_WIDTH + B_WIDTH]),
            rms_norm(o_c, go[A_WIDTH + B_WIDTH:]),
        ], axis=-1)
        x = x + jnp.matmul(mix, w_out[l])
        h = rms_norm(x, g_ffn[l])
        i = l // 2
        if l % 2 == 0:
            x = x + swiglu(h, w_gate_d[i], w_up_d[i], w_down_d[i])
        else:
            x = x + moe(h, w_router[i], w_gate_e[i], w_up_e[i], w_down_e[i])
    return x


_drawn_inputs = setup_inputs


def setup_inputs(seed=0):
    import zlib

    import numpy as np

    out = dict(_drawn_inputs(seed))
    spreads = {}
    factors = {'qn_a': 3.198,
     'kn_a': 2.995,
     'ln_b_g': 4.859,
     'ln_b_b': 4.976,
     'qn_c': 3.123,
     'kn_c': 3.328,
     'sinks_a': 50.184}
    for name, (base, spread) in spreads.items():
        noise = np.random.default_rng([zlib.crc32(name.encode()), seed]).standard_normal(out[name].shape)
        drawn = base * np.exp(spread * noise) if base else spread * noise
        out[name] = jnp.asarray(drawn.astype(out[name].dtype))
    for name, factor in factors.items():
        out[name] = (out[name] * factor).astype(out[name].dtype)
    return out
```

```python
from contextlib import ExitStack

import concourse.bass as bass
from concourse import mybir

F32 = mybir.dt.float32
F32R = mybir.dt.float32r
I32 = mybir.dt.int32
U32 = mybir.dt.uint32
ALU = mybir.AluOpType
ACT = mybir.ActivationFunctionType
AX_X = mybir.AxisListType.X

P = 128
TILES = 2
D = 1024
KD = D // P
CHUNK = 64
HEAD = 64
AQ, AKV, BG, CH = 6, 2, 4, 6
COL_AQ, COL_AK, COL_AV = 0, 384, 512
COL_BU, COL_BV = 640, 896
COL_CQ, COL_CK, COL_CV = 1152, 1536, 1920
IN_WIDTH = 2304
OUT_GROUPS = ((0, COL_AQ, 384), (384, COL_BU, 256), (640, COL_CQ, 384))
DFF = 2816
DFE = 3584
EXPERTS = 8
LAYERS = 2
EPS = 1e-6
NEG_INF = -1e30
FAR = 1e33
SCORES = 3 * P
LAST_REL = 255

SLOT = 2048
RAW = 6
SPLIT = 3
NARROW = SLOT // KD
IN_SLOTS = IN_WIDTH // NARROW
OUT_SLOTS = D // NARROW
FF_CHUNKS = DFF // NARROW
FF_SLOTS = 3 * FF_CHUNKS
DENSE_SLOTS = LAYERS * (IN_SLOTS + OUT_SLOTS) + FF_SLOTS
BASE_IN = (0, IN_SLOTS + OUT_SLOTS + FF_SLOTS)
BASE_OUT = (IN_SLOTS, BASE_IN[1] + IN_SLOTS)
BASE_FF = IN_SLOTS + OUT_SLOTS
WIDE = 512
EX_CHUNKS = DFE // WIDE
ITEM_SLOTS = 6 * EX_CHUNKS
MAX_OVER = 3
ITEMS = EXPERTS + MAX_OVER + 1
MARGIN_AT = 6
LANDING = 16

assert ITEM_SLOTS % RAW == 0 and ITEM_SLOTS % SPLIT == 0
RAW_SHIFT = -DENSE_SLOTS % RAW
SPLIT_SHIFT = -DENSE_SLOTS % SPLIT


def raw_place(j):
    return (j + RAW_SHIFT) % RAW


def split_place(j):
    return (j + SPLIT_SHIFT) % SPLIT


def landings(j):
    return (j - (raw_place(j) - RAW_SHIFT) % RAW) // RAW + 1


def ff_slots(c):
    gate = BASE_FF if c == 0 else BASE_FF + 3 * c - 1
    down = BASE_FF + (3 * c + 4 if c < FF_CHUNKS - 1 else FF_SLOTS - 1)
    return gate, gate + 1, down


def ex_slots(c):
    gate = 0 if c == 0 else 6 * c - 2
    down = 6 * c + 8 if c < EX_CHUNKS - 1 else ITEM_SLOTS - 2
    return gate, gate + 2, down


def hybrid_trunk(nc, x, g_mix, w_in, qk_gain, sinks, ln_g, ln_b, w_s, b_s, rel, g_out, w_out, g_ffn,
                 w_gate_d, w_up_d, w_down_d, w_router, w_gate_e, w_up_e, w_down_e, out):
    ctx = ExitStack()
    with ctx:
        def sb(name, shape, dt=F32):
            return ctx.enter_context(nc.sbuf_tensor(name, shape, dt))

        def sem(name):
            return ctx.enter_context(nc.semaphore(name))

        ps = ctx.enter_context(nc.psum_tensor("ps", [P, 8, 512], F32))

        raw = sb("raw", [P, RAW, SLOT])
        high = sb("high", [P, SPLIT, SLOT], F32R)
        low = sb("low", [P, SPLIT, SLOT], F32R)
        xr = sb("xr", [P, TILES, D])
        hn = sb("hn", [P, TILES, D])
        gain = sb("gain", [P, D])
        turned_h = sb("turned_h", [P, TILES * D], F32R)
        turned_l = sb("turned_l", [P, TILES * D], F32R)
        th = turned_h[:, :].rearrange("p (k n) -> p k n", k=KD)
        tl = turned_l[:, :].rearrange("p (k n) -> p k n", k=KD)
        rows_h = turned_h[:, :].rearrange("p (t n) -> p t n", t=TILES)
        rows_l = turned_l[:, :].rearrange("p (t n) -> p t n", t=TILES)
        proj = sb("proj", [P, TILES, IN_WIDTH])
        qkT = sb("qkT", [P, 10, TILES * P])
        work = sb("work", [P, 20 * P])
        S = work[:, 0:6 * SCORES].rearrange("p (h n) -> p h n", h=6)
        relb = sb("relb", [P, CH, SCORES])
        dist = sb("dist", [P, SCORES])
        PT = hn[:, 0, 0:2 * SCORES].rearrange("p (n c) -> p n c", n=2)
        paired = hn[:, 1, :].rearrange("p (t b a d) -> p t b a d", t=TILES, b=4, a=2)
        wsT = sb("wsT", [P, BG, P])
        lng = sb("lng", [P, BG * HEAD])
        lnb = sb("lnb", [P, BG * HEAD])
        small = sb("small", [P, 320])
        taken = [0]

        def cols(n):
            taken[0] += n
            assert taken[0] <= 320
            return small[:, taken[0] - n:taken[0]]

        bs = cols(BG)
        qkg = cols(4)
        sink = cols(AQ)
        ss_x = cols(2 * LAYERS * TILES)
        ms_x = cols(2 * LAYERS * TILES)
        rs_x = cols(2 * LAYERS * TILES)
        ss_q = cols(40)
        rs_q = cols(40)
        mean_b = cols(8)
        var_b = cols(8)
        rs_b = cols(8)
        mx = cols(24).rearrange("p (n t) -> p n t", t=TILES)
        nm = cols(24).rearrange("p (n t) -> p n t", t=TILES)
        total = cols(24).rearrange("p (n t) -> p n t", t=TILES)
        esink = cols(12).rearrange("p (n t) -> p n t", t=TILES)
        ss_g = cols(6)
        rs_g = cols(6)
        inv_n = cols(6)
        halves = cols(40)
        ident = sb("ident", [P, P])
        ident_r = sb("ident_r", [P, P], F32R)
        count_up = sb("count_up", [P, P])
        before = sb("before", [P, P])
        ones = sb("ones", [P, P])
        silu = work[:, 0:512]
        acted = work[:, 512:1024]
        part_h = sb("part_h", [P, D], F32R)
        part_l = sb("part_l", [P, D], F32R)
        wr = sb("wr", [P, KD * EXPERTS])
        wr_h = sb("wr_h", [P, KD * EXPERTS], F32R)
        wr_l = sb("wr_l", [P, KD * EXPERTS], F32R)
        route = work[:, 2304:2560]
        used = [0]

        def rcols(n, **kw):
            used[0] += n
            assert used[0] <= 256
            a = route[:, used[0] - n:used[0]]
            return a.rearrange("p (t e) -> p t e", **kw) if kw else a

        logits = rcols(16, t=2)
        best = rcols(16, t=2)
        best_at = rcols(4, t=2)
        margin = rcols(2)
        emargin = rcols(2)
        gate1 = rcols(2)
        gate2 = rcols(2)
        first = rcols(16, t=2)
        second = rcols(16, t=2)
        chosen = rcols(16, t=2)
        ranks = rcols(24)
        over = rcols(8)
        over_at = rcols(8)
        pick = rcols(8)
        picked = rcols(16, t=2)
        spare = rcols(4)
        item_rank = rcols(2 * ITEMS, t=2)
        item_gate = rcols(2 * ITEMS, t=2)
        best_index = sb("best_index", [P, 2, 8], U32)
        plan = sb("plan", [P, 4], I32)
        hot = sb("hot", [P, TILES, P], F32R)
        hotT = sb("hotT", [P, TILES, P], F32R)
        item_h = sb("item_h", [P, KD, P], F32R)
        item_l = sb("item_l", [P, KD, P], F32R)

        s = {}

        def sems(*names):
            for n in names:
                s[n] = sem(n)

        landed = [sem(f"landed{r}") for r in range(RAW)]
        sems("high_ready", "slot_split", "slot_used", "tile0_done")
        sems("x0_loaded", "x1_loaded", "gain_loaded", "param_loaded", "router_loaded")
        sems("const_made", "const_chain", "dist_made", "masked", "ident_r_made", "router_high", "router_split", "qkg_scaled")
        sems("x_squared", "x_ms", "x_rs", "hn_ready", "turned", "turned_high", "turned_ready", "x_updated")
        sems("evac_a", "evac_d", "qk_squared", "qk_sum", "qk_rs", "qk_normed", "pool_chain")
        sems("gelu_done", "b_chain", "b_var", "b_rs", "b_normed", "b_psum", "b_out")
        sems("qk_turned", "qkT_a", "qkT_d", "scored", "score_in", "max_chain", "nm_ready", "p_ready", "esink_ready")
        sems("p_turned", "PT_a", "PT_d", "pv_done", "den_chain", "o_ready", "group_squared", "group_rs")
        sems("ff_silu", "ff_acted", "ff_turned", "ff_high", "ff_ready")
        sems("logits_psum", "route_chain", "emargin_ready", "chosen_ready", "ranks_psum", "ranks_read", "rows_high", "rows_ready", "plan_ready")
        sems("hot_ready", "m_hotT_psum", "m_hotT_ready", "m_item_psum", "m_item_high", "m_item_ready")
        sems("m_silu", "m_acted", "m_turned", "m_part_high", "m_part_ready", "m_res_high", "m_res_ready", "m_scattered", "m_added")
        sems("x_stored")

        def rms_index(l, ffn):
            return 2 * l + ffn

        block = ctx.enter_context(nc.Block())

        @block.sync
        def _(sp):
            narrow = lambda w: w.rearrange("(k p) n -> p k n", p=P)
            eight = lambda r: raw[:, r, :].rearrange("p (k n) -> p k n", k=KD)
            four = lambda r: raw[:, r, :].rearrange("p (k n) -> p k n", k=4)
            two = lambda r: raw[:, r, :].rearrange("p (k n) -> p k n", k=2)

            def send(j, to, src):
                if j >= RAW:
                    sp.wait_ge(s["slot_split"], j - RAW + 1)
                sp.dma_start(to(raw_place(j)), src).then_inc(landed[raw_place(j)], LANDING)

            for t in range(TILES):
                sp.dma_start(xr[:, t, :], x[t * P:(t + 1) * P, :]).then_inc(s[f"x{t}_loaded"], LANDING)
            for l in range(LAYERS):
                for c in range(IN_SLOTS):
                    send(BASE_IN[l] + c, eight, narrow(w_in[l])[:, :, c * NARROW:(c + 1) * NARROW])
                for c in range(OUT_SLOTS):
                    send(BASE_OUT[l] + c, eight, narrow(w_out[l])[:, :, c * NARROW:(c + 1) * NARROW])
                if l == 0:
                    for c in range(FF_CHUNKS + 1):
                        if c < FF_CHUNKS:
                            cut = slice(c * NARROW, (c + 1) * NARROW)
                            send(ff_slots(c)[0], eight, narrow(w_gate_d[0])[:, :, cut])
                            send(ff_slots(c)[1], eight, narrow(w_up_d[0])[:, :, cut])
                        if c > 0:
                            send(ff_slots(c - 1)[2], two, narrow(w_down_d[0])[:, 2 * (c - 1):2 * c, :])

            up_view = lambda w: w[0].rearrange("e (k p) n -> e p k n", p=P)

            def send_item(i, e):
                def put(m, to, src):
                    j = DENSE_SLOTS + m
                    sp.wait_ge(s["slot_split"], i * ITEM_SLOTS + (j - RAW + 1))
                    sp.dma_start(to(raw_place(j)), src).then_inc(landed[raw_place(j)], LANDING)

                for c in range(EX_CHUNKS + 1):
                    for a in range(2):
                        if c < EX_CHUNKS:
                            cut = slice(c * WIDE, (c + 1) * WIDE)
                            put(ex_slots(c)[0] + a, four, up_view(w_gate_e)[e, :, 4 * a:4 * a + 4, cut])
                    for a in range(2):
                        if c < EX_CHUNKS:
                            put(ex_slots(c)[1] + a, four, up_view(w_up_e)[e, :, 4 * a:4 * a + 4, cut])
                    for a in range(2):
                        if c > 0:
                            k = 4 * (c - 1) + 2 * a
                            put(ex_slots(c - 1)[2] + a, two, up_view(w_down_e)[e, :, k:k + 2, :])

            with sp.Fori(0, EXPERTS) as i:
                send_item(i, i)
            sp.wait_ge(s["plan_ready"], 2)
            extra = sp.value_load(plan[0:1, 0:1], min_val=0, max_val=MAX_OVER)
            with sp.If(extra > 0):
                with sp.Fori(0, extra) as v:
                    e = sp.value_load(plan[0:1, bass.ds(v + 1, 1)], min_val=0, max_val=EXPERTS - 1)
                    send_item(v + EXPERTS, e)
            for m in range(SPLIT):
                j = DENSE_SLOTS + m
                sp.wait_ge(s["slot_split"], (extra + EXPERTS) * ITEM_SLOTS + (j - RAW + 1))
                sp.dma_start(four(raw_place(j)), up_view(w_gate_e)[0, :, 0:4, 0:WIDE]).then_inc(landed[raw_place(j)], LANDING)
            sp.wait_ge(s["m_added"], (extra + EXPERTS) * 4 + 1)
            for t in range(TILES):
                sp.dma_start(out[t * P:(t + 1) * P, :], xr[:, t, :]).then_inc(s["x_stored"], LANDING)
            sp.wait_ge(s["x_stored"], TILES * LANDING)

        @block.gpsimd
        def _(pool):
            loads = [0]

            def load_gain(n):
                row = (g_mix, g_out, g_ffn)[n % 3][n // 3]
                pool.dma_start(gain[:, :], row.partition_broadcast(P)).then_inc(s["gain_loaded"], LANDING)

            def load_params(l):
                for to, src in ((relb[:, :, :], rel[l]), (wsT[:, :, :], w_s[l]), (bs, b_s[l]), (qkg, qk_gain[l]),
                                (lng[:, :], ln_g[l].partition_broadcast(P)), (lnb[:, :], ln_b[l].partition_broadcast(P)),
                                (sink, sinks[l].partition_broadcast(P))):
                    pool.dma_start(to, src).then_inc(s["param_loaded"], LANDING)
                    loads[0] += LANDING
                pool.wait_ge(s["param_loaded"], loads[0])
                pool.wait_ge(s["x_rs"], TILES * (2 * l + 1))
                nc.gpsimd.memset(relb[0:CHUNK, :, CHUNK:P], NEG_INF).then_inc(s["masked"], 1)
                nc.gpsimd.memset(relb[0:CHUNK, :, SCORES - CHUNK:SCORES], NEG_INF).then_inc(s["masked"], 1)
                nc.gpsimd.memset(wsT[CHUNK:P, :, 0:CHUNK], 0.0).then_inc(s["masked"], 1)
                pool.wait_ge(s["masked"], 3 * (l + 1))

            load_gain(0)
            nc.gpsimd.memset(halves, -0.5).then_inc(s["const_made"], 1)
            nc.gpsimd.memset(ident[:, :], 0.0).then_inc(s["const_chain"], 1)
            pool.wait_ge(s["const_chain"], 1)
            nc.gpsimd.affine_select(out=ident[:, :], in_=ident[:, :], compare_op=ALU.not_equal, fill=1.0, base=0,
                                    pattern=[[-1, P]], channel_multiplier=1).then_inc(s["const_made"], 1)
            nc.gpsimd.iota(count_up[:, :], [[1, P]], base=0, channel_multiplier=0,
                           allow_small_or_imprecise_dtypes=True).then_inc(s["const_made"], 1)
            nc.gpsimd.iota(before[:, :], [[1, P]], base=0, channel_multiplier=-1,
                           allow_small_or_imprecise_dtypes=True).then_inc(s["const_made"], 1)
            nc.gpsimd.iota(dist[:, 0:P], [[-1, P]], base=0, channel_multiplier=1,
                           allow_small_or_imprecise_dtypes=True).then_inc(s["const_made"], 1)
            nc.gpsimd.iota(dist[:, P:SCORES], [[-1, 2 * P]], base=P, channel_multiplier=1,
                           allow_small_or_imprecise_dtypes=True).then_inc(s["const_made"], 1)
            nc.gpsimd.memset(ones[:, :], 1.0).then_inc(s["const_made"], 1)
            for t in range(TILES):
                for g, (_, _, width) in enumerate(OUT_GROUPS):
                    nc.gpsimd.memset(inv_n[:, 3 * t + g:3 * t + g + 1], 1.0 / width).then_inc(s["const_made"], 1)
            pool.dma_start(wr[:, :], w_router).then_inc(s["router_loaded"], LANDING)
            chain = [0]

            def power(out_, ms, done):
                pool.wait_ge(s["pool_chain"], chain[0])
                nc.gpsimd.tensor_tensor(out_, ms, halves[:, 0:out_.shape[1]], ALU.pow).then_inc(s[done], 1)

            def mean_eps(to, sums, scale):
                nc.gpsimd.tensor_scalar(to, sums, scale, EPS, ALU.mult, ALU.add).then_inc(s["pool_chain"], 1)
                chain[0] += 1

            def rms_rows(n):
                for t in range(TILES):
                    c = slice(TILES * n + t, TILES * n + t + 1)
                    pool.wait_ge(s["x_squared"], TILES * n + t + 1)
                    mean_eps(ms_x[:, c], ss_x[:, c], 1.0 / D)
                    power(rs_x[:, c], ms_x[:, c], "x_rs")

            def next_gain(n):
                pool.wait_ge(s["hn_ready"], TILES * n)
                load_gain(n)

            for l in range(LAYERS):
                rms_rows(2 * l)
                load_params(l)
                next_gain(3 * l + 1)
                for part, lo, n in (("a", 0, 16), ("b", 0, 8), ("c", 16, 24)):
                    if part == "b":
                        pool.wait_ge(s["b_var"], l + 1)
                        mean_eps(var_b, var_b, 1.0 / HEAD)
                        power(rs_b, var_b, "b_rs")
                    else:
                        pool.wait_ge(s["qk_sum"], 2 * l + (1 if part == "a" else 2))
                        mean_eps(ss_q[:, lo:lo + n], ss_q[:, lo:lo + n], 1.0 / HEAD)
                        power(rs_q[:, lo:lo + n], ss_q[:, lo:lo + n], "qk_rs")
                pool.wait_ge(s["group_squared"], 6 * (l + 1))
                nc.gpsimd.tensor_tensor(ss_g, ss_g, inv_n, ALU.mult).then_inc(s["pool_chain"], 1)
                chain[0] += 1
                pool.wait_ge(s["pool_chain"], chain[0])
                mean_eps(ss_g, ss_g, 1.0)
                power(rs_g, ss_g, "group_rs")
                next_gain(3 * l + 2)
                rms_rows(2 * l + 1)
                if l + 1 < LAYERS:
                    next_gain(3 * l + 3)

        @block.scalar
        def _(act):
            at = [0]

            def high_to(m):
                for j in range(at[0], m + 1):
                    act.wait_ge(landed[raw_place(j)], LANDING * landings(j))
                    if j >= SPLIT:
                        act.wait_ge(s["slot_used"], j - SPLIT + 1)
                    nc.scalar.activation(high[:, split_place(j), :], raw[:, raw_place(j), :], ACT.Copy)\
                        .then_inc(s["high_ready"], 1)
                at[0] = max(at[0], m + 1)

            def square_rows(n, need):
                for t in range(TILES):
                    need(t)
                    c = TILES * n + t
                    nc.scalar.activation(work[:, t * D:(t + 1) * D], xr[:, t, :], ACT.Square,
                                         accum_out=ss_x[:, c:c + 1]).then_inc(s["x_squared"], 1)

            def turn_high(u):
                t = u % TILES
                for q in range(2):
                    act.wait_ge(s["turned"], 2 * u + q + 1)
                    bank = (u % 2) * 2 + q
                    nc.scalar.activation(th[:, 4 * q:4 * q + 4, t * P:(t + 1) * P],
                                         ps[:, bank, :].rearrange("p (k n) -> p k n", k=4), ACT.Copy)\
                        .then_inc(s["turned_high"], 1)

            act.sem_inc(s["evac_a"], SPLIT)
            for name in ("m_silu", "m_part_high", "m_item_high", "m_res_high"):
                act.sem_inc(s[name], 1)
            square_rows(0, lambda t: act.wait_ge(s[f"x{t}_loaded"], LANDING))
            act.wait_ge(s["const_made"], 13)
            nc.scalar.activation(ident_r[:, :], ident[:, :], ACT.Copy).then_inc(s["ident_r_made"], 1)
            act.wait_ge(s["router_loaded"], LANDING)
            nc.scalar.activation(wr_h[:, :], wr[:, :], ACT.Copy).then_inc(s["router_high"], 1)

            for l in range(LAYERS):
                base, after = BASE_IN[l], BASE_OUT[l]
                high_to(base + SPLIT - 1)
                for t in range(TILES):
                    turn_high(6 * l + t)
                for c in range(IN_SLOTS):
                    high_to(base + c + SPLIT)
                    act.wait_ge(s["tile0_done"], base + c + 1)
                    nc.scalar.activation(proj[:, 0, c * NARROW:(c + 1) * NARROW], ps[:, 2 * (c % 3), 0:NARROW], ACT.Copy)\
                        .then_inc(s["evac_a"], 1)
                    if c in (2, 5, 8):
                        act.wait_ge(s["evac_a"], SPLIT + IN_SLOTS * l + c)
                        act.wait_ge(s["evac_d"], SPLIT + IN_SLOTS * l + c)
                    if c == 2:
                        for t in range(TILES):
                            nc.scalar.activation(work[:, 512 * t:512 * t + 512], proj[:, t, COL_AQ:COL_AV], ACT.Square)\
                                .then_inc(s["qk_squared"], 1)
                    if c == 5:
                        for t in range(TILES):
                            nc.scalar.activation(proj[:, t, COL_BU:COL_CQ], proj[:, t, COL_BU:COL_CQ], ACT.Gelu)\
                                .then_inc(s["gelu_done"], 1)
                    if c == 8:
                        for t in range(TILES):
                            nc.scalar.activation(work[:, 1024 + 768 * t:1792 + 768 * t], proj[:, t, COL_CQ:COL_CV], ACT.Square)\
                                .then_inc(s["qk_squared"], 1)
                act.wait_ge(s["qkg_scaled"], l + 1)
                for bank, g in ((0, 0), (2, 2), (4, 3)):
                    act.wait_ge(s["qk_turned"], 10 * l + 2 * bank + 2)
                    nc.scalar.activation(qkT[:, 2 * bank:2 * bank + 2, :], ps[:, bank, :].rearrange("p (a n) -> p a n", a=2),
                                         ACT.Copy, scale=qkg[:, g:g + 1]).then_inc(s["qkT_a"], 1)

                def pt_copy(n):
                    act.wait_ge(s["p_turned"], 12 * l + n + 1)
                    if n >= 2:
                        act.wait_ge(s["pv_done"], 12 * l + n - 1)
                    nc.scalar.activation(PT[:, n % 2, :], ps[:, 4 + n % 2, 0:SCORES], ACT.Copy).then_inc(s["PT_a"], 1)

                for n in range(AQ + CH):
                    if n in (0, AQ):
                        act.wait_ge(s["nm_ready"], 2 * l + (1 if n == 0 else 2))
                    for t, (lo, hi) in enumerate(((0, P), (P, SCORES))):
                        e = nc.scalar.activation(S[:, n % 6, lo:hi], S[:, n % 6, lo:hi], ACT.Exp,
                                                 bias=nm[:, n, t:t + 1], accum_out=total[:, n, t:t + 1])
                    e.then_inc(s["p_ready"], 1)
                    if n == AQ - 1:
                        nc.scalar.activation(esink, esink, ACT.Exp).then_inc(s["esink_ready"], 1)
                    if n >= 2 and n % 2 == 0:
                        pt_copy(n - 2)
                pt_copy(10)
                act.wait_ge(s["b_out"], 4 * (l + 1))
                act.wait_ge(s["o_ready"], 4 * (l + 1))
                for t in range(TILES):
                    for g, (to, col, width) in enumerate(OUT_GROUPS):
                        nc.scalar.activation(work[:, t * D + to:t * D + to + width], proj[:, t, col:col + width], ACT.Square,
                                             accum_out=ss_g[:, 3 * t + g:3 * t + g + 1]).then_inc(s["group_squared"], 1)
                for t in range(TILES):
                    turn_high(6 * l + 2 + t)
                high_to(after + OUT_SLOTS + SPLIT - 1)
                done = (8 if l == 0 else 20)
                square_rows(2 * l + 1, lambda t: act.wait_ge(s["x_updated"], done - 1 + t))
                for t in range(TILES):
                    turn_high(6 * l + 4 + t)
                if l == 0:
                    def ff_silu(c):
                        up = ff_slots(c)[1]
                        for t in range(TILES):
                            act.wait_ge(s["tile0_done" if t == 0 else "slot_used"], up + 1)
                            if c > 0:
                                act.wait_ge(s["ff_acted"], 2 * (c - 1) + t + 1)
                            nc.scalar.activation(silu[:, 256 * t:256 * t + 256], ps[:, t, 0:NARROW], ACT.Silu)\
                                .then_inc(s["ff_silu"], 1)

                    def ff_high(c):
                        for t in range(TILES):
                            act.wait_ge(s["ff_turned"], 2 * c + t + 1)
                            if c > 0:
                                act.wait_ge(s["slot_used"], ff_slots(c - 1)[2] + 1)
                            nc.scalar.activation(part_h[:, 256 * t:256 * t + 256], ps[:, 6 + t, 0:256], ACT.Copy)\
                                .then_inc(s["ff_high"], 1)

                    for c in range(FF_CHUNKS):
                        if c > 0:
                            high_to(ff_slots(c - 1)[1] + 5)
                            ff_high(c - 1)
                        high_to(ff_slots(c)[1] + SPLIT)
                        ff_silu(c)
                    high_to(ff_slots(FF_CHUNKS - 1)[1] + 4)
                    ff_high(FF_CHUNKS - 1)
                    square_rows(2, lambda t: act.wait_ge(s["x_updated"], 8 + 2 * (t + 1)))

            act.wait_ge(s["logits_psum"], 1)
            for t in range(TILES):
                nc.scalar.activation(rows_h[:, t, :], hn[:, t, :], ACT.Copy).then_inc(s["rows_high"], 1)
            act.wait_ge(s["route_chain"], MARGIN_AT)
            nc.scalar.activation(emargin, margin, ACT.Exp).then_inc(s["emargin_ready"], 1)

            def item_high(i):
                for q in range(2):
                    act.wait_ge(s["m_item_psum"], i * 2 + q + 1)
                    nc.scalar.activation(item_h[:, 4 * q:4 * q + 4, :], ps[:, 2 + q, :].rearrange("p (k n) -> p k n", k=4),
                                         ACT.Copy).then_inc(s["m_item_high"], 1)

            def hotT_copy(i):
                act.wait_ge(s["m_hotT_psum"], i + 1)
                nc.scalar.activation(hotT[:, :, :].rearrange("p t n -> p (t n)"), ps[:, 7, 256:512], ACT.Copy)\
                    .then_inc(s["m_hotT_ready"], 1)

            item_high(0)
            hotT_copy(0)

            def item_body(i):
                def high_item(m):
                    j = DENSE_SLOTS + m
                    act.wait_ge(landed[raw_place(j)], i * (ITEM_SLOTS // RAW * LANDING) + LANDING * landings(j))
                    act.wait_ge(s["slot_used"], i * ITEM_SLOTS + (j - SPLIT + 1))
                    nc.scalar.activation(high[:, split_place(j), :], raw[:, raw_place(j), :], ACT.Copy)\
                        .then_inc(s["high_ready"], 1)

                def silu_of(c):
                    act.wait_ge(s["slot_used"], i * ITEM_SLOTS + (DENSE_SLOTS + ex_slots(c)[0] + 2))
                    act.wait_ge(s["m_acted"], i * EX_CHUNKS + c + 1)
                    nc.scalar.activation(silu, ps[:, 2 * (c % 2), :], ACT.Silu).then_inc(s["m_silu"], 1)

                def part_high(c):
                    act.wait_ge(s["m_turned"], i * EX_CHUNKS + c + 2)
                    if c > 0:
                        act.wait_ge(s["slot_used"], i * ITEM_SLOTS + (DENSE_SLOTS + ex_slots(c - 1)[2] + 2))
                    else:
                        act.wait_ge(s["m_scattered"], i * 4 + 1)
                    nc.scalar.activation(part_h[:, 0:512], ps[:, 6, :], ACT.Copy).then_inc(s["m_part_high"], 1)

                for m in range(SPLIT, ITEM_SLOTS + SPLIT):
                    high_item(m)
                    for c in range(EX_CHUNKS):
                        if m == ex_slots(c)[0] + 1 + SPLIT:
                            silu_of(c)
                    for c in range(EX_CHUNKS):
                        if m == (6 * c + 8 if c < EX_CHUNKS - 1 else ITEM_SLOTS):
                            part_high(c)
                    if m == ITEM_SLOTS:
                        item_high(i + 1)
                act.wait_ge(s["slot_used"], i * ITEM_SLOTS + (DENSE_SLOTS + ITEM_SLOTS))
                for q in range(2):
                    nc.scalar.activation(part_h[:, 512 * q:512 * q + 512], ps[:, 4 + q, :], ACT.Copy)\
                        .then_inc(s["m_res_high"], 1)
                hotT_copy(i + 1)

            with act.Fori(0, EXPERTS) as i:
                item_body(i)
            act.wait_ge(s["plan_ready"], 2)
            extra = act.value_load(plan[0:1, 0:1], min_val=0, max_val=MAX_OVER)
            with act.If(extra > 0):
                with act.Fori(0, extra) as v:
                    item_body(v + EXPERTS)

        @block.vector
        def _(dve):
            at = [0]
            chains = {}

            def link(name, ins):
                chains[name] = chains.get(name, 0) + 1
                ins.then_inc(s[name], 1)
                dve.wait_ge(s[name], chains[name])

            def low_to(m):
                for j in range(at[0], m + 1):
                    dve.wait_ge(s["high_ready"], j + 1)
                    nc.vector.tensor_tensor(low[:, split_place(j), :], raw[:, raw_place(j), :],
                                            high[:, split_place(j), :].bitcast(F32), ALU.subtract)\
                        .then_inc(s["slot_split"], 1)
                at[0] = max(at[0], m + 1)

            def normed_rows(n, u, gains):
                for t in range(TILES):
                    dve.wait_ge(s["x_rs"], TILES * n + t + 1)
                    dve.wait_ge(s["gain_loaded"], LANDING * gains)
                    c = TILES * n + t
                    nc.vector.scalar_tensor_tensor(hn[:, t, :], xr[:, t, :], rs_x[:, c:c + 1], gain[:, :],
                                                   ALU.mult, ALU.mult).then_inc(s["hn_ready"], 1)

            def turn_low(u):
                t = u % TILES
                for q in range(2):
                    dve.wait_ge(s["turned_high"], 2 * u + q + 1)
                    bank = (u % 2) * 2 + q
                    cut = (slice(None), slice(4 * q, 4 * q + 4), slice(t * P, (t + 1) * P))
                    nc.vector.tensor_tensor(tl[cut], ps[:, bank, :].rearrange("p (k n) -> p k n", k=4),
                                            th[cut].bitcast(F32), ALU.subtract).then_inc(s["turned_ready"], 1)

            dve.sem_inc(s["evac_d"], SPLIT)
            for name in ("m_acted", "m_part_ready", "m_item_ready", "m_res_ready", "m_added"):
                dve.sem_inc(s[name], 1)
            dve.wait_ge(s["const_made"], 13)
            link("dist_made", nc.vector.scalar_tensor_tensor(dist[:, :], dist[:, :], -1.0, dist[:, :], ALU.mult, ALU.max))
            for rows, lo, hi in (((0, CHUNK), CHUNK, P), ((0, CHUNK), P, P + CHUNK), ((0, CHUNK), SCORES - CHUNK, SCORES),
                                 ((CHUNK, P), P, 2 * P)):
                link("dist_made", nc.vector.memset(dist[rows[0]:rows[1], lo:hi], FAR))
            link("dist_made", nc.vector.tensor_scalar(before[:, :], before[:, :], 0.0, None, ALU.is_gt))
            dve.wait_ge(s["router_high"], 1)
            nc.vector.tensor_tensor(wr_l[:, :], wr[:, :], wr_h[:, :].bitcast(F32), ALU.subtract)\
                .then_inc(s["router_split"], 1)

            for l in range(LAYERS):
                base, after = BASE_IN[l], BASE_OUT[l]
                normed_rows(2 * l, 6 * l, 3 * l + 1)
                for t in range(TILES):
                    turn_low(6 * l + t)
                low_to(base + SPLIT - 1)

                def scale_a():
                    dve.wait_ge(s["qk_rs"], 2 * l + 1)
                    for t in range(TILES):
                        r = rs_q[:, 8 * t:8 * t + 8]
                        for half in range(2):
                            cut = slice(3 * half, 3 * half + 3)
                            q = proj[:, t, COL_AQ + 192 * half:COL_AQ + 192 * half + 192].rearrange("p (h d) -> p h d", d=HEAD)
                            nc.vector.tensor_tensor(paired[:, t, 0:3, half, :], q,
                                                    r[:, cut].unsqueeze(2).broadcast_to([P, 3, HEAD]), ALU.mult)
                        k = proj[:, t, COL_AK:COL_AV].rearrange("p (h d) -> p h d", d=HEAD)
                        nc.vector.tensor_tensor(paired[:, t, 3, :, :], k, r[:, AQ:].unsqueeze(2).broadcast_to([P, AKV, HEAD]),
                                                ALU.mult).then_inc(s["qk_normed"], 1)

                def scale_c():
                    dve.wait_ge(s["qk_rs"], 2 * l + 2)
                    for t in range(TILES):
                        v = proj[:, t, COL_CQ:COL_CV].rearrange("p (h d) -> p h d", d=HEAD)
                        r = rs_q[:, 16 + 12 * t:28 + 12 * t].unsqueeze(2).broadcast_to([P, 2 * CH, HEAD])
                        nc.vector.tensor_tensor(v, v, r, ALU.mult).then_inc(s["qk_normed"], 1)

                bv = proj[:, :, COL_BV:COL_CQ].rearrange("p t (g d) -> p t g d", d=HEAD)
                bsq = work[:, 1024:1536]
                for c in range(IN_SLOTS):
                    low_to(base + c + SPLIT)
                    dve.wait_ge(s["slot_used"], base + c + 1)
                    nc.vector.tensor_copy(proj[:, 1, c * NARROW:(c + 1) * NARROW], ps[:, 2 * (c % 3) + 1, 0:NARROW])\
                        .then_inc(s["evac_d"], 1)
                    if c == 1:
                        dve.wait_ge(s["param_loaded"], 7 * LANDING * (l + 1))
                        nc.vector.tensor_scalar(qkg[:, 0:4:2], qkg[:, 0:4:2], HEAD ** -0.5, None, ALU.mult)\
                            .then_inc(s["qkg_scaled"], 1)
                    if c == 3:
                        dve.wait_ge(s["qk_squared"], 4 * l + 2)
                        nc.vector.tensor_reduce(ss_q[:, 0:16], work[:, 0:1024].rearrange("p (h d) -> p h d", d=HEAD),
                                                AX_X, ALU.add).then_inc(s["qk_sum"], 1)
                    if c == 4:
                        scale_a()
                    if c == 6:
                        dve.wait_ge(s["gelu_done"], 2 * (l + 1))
                        m4 = mean_b.rearrange("p (t g) -> p t g", t=TILES)
                        link("b_chain", nc.vector.tensor_reduce(m4, bv, AX_X, ALU.add))
                        link("b_chain", nc.vector.tensor_scalar(mean_b, mean_b, 1.0 / HEAD, None, ALU.mult))
                        link("b_chain", nc.vector.tensor_tensor(bv, bv, m4.unsqueeze(3).broadcast_to([P, TILES, BG, HEAD]),
                                                                ALU.subtract))
                        b4 = bsq.rearrange("p (t g d) -> p t g d", t=TILES, d=HEAD)
                        link("b_chain", nc.vector.tensor_tensor(b4, bv, bv, ALU.mult))
                        nc.vector.tensor_reduce(var_b, bsq.rearrange("p (g d) -> p g d", d=HEAD), AX_X, ALU.add)\
                            .then_inc(s["b_var"], 1)
                    if c == 7:
                        dve.wait_ge(s["b_rs"], l + 1)
                        dve.wait_ge(s["param_loaded"], 7 * LANDING * (l + 1))
                        r4 = rs_b.rearrange("p (t g) -> p t g", t=TILES)
                        link("b_chain", nc.vector.tensor_tensor(bv, bv, r4.unsqueeze(3).broadcast_to([P, TILES, BG, HEAD]),
                                                                ALU.mult))
                        flat = proj[:, :, COL_BV:COL_CQ]
                        link("b_chain", nc.vector.tensor_tensor(flat, flat, lng[:, :].unsqueeze(1).broadcast_to([P, TILES, 256]),
                                                                ALU.mult))
                        nc.vector.tensor_tensor(flat, flat, lnb[:, :].unsqueeze(1).broadcast_to([P, TILES, 256]), ALU.add)\
                            .then_inc(s["b_normed"], 1)
                dve.wait_ge(s["qk_squared"], 4 * l + 4)
                nc.vector.tensor_reduce(ss_q[:, 16:40], work[:, 1024:2560].rearrange("p (h d) -> p h d", d=HEAD),
                                        AX_X, ALU.add).then_inc(s["qk_sum"], 1)

                def qk_copy(bank, g):
                    dve.wait_ge(s["qk_turned"], 10 * l + 2 * bank + 2)
                    for a in range(2):
                        i = nc.vector.tensor_scalar(qkT[:, 2 * bank + a, :], ps[:, bank, 256 * a:256 * a + 256],
                                                    qkg[:, g + a:g + a + 1], None, ALU.mult)
                    i.then_inc(s["qkT_d"], 1)

                dve.wait_ge(s["qkg_scaled"], l + 1)
                qk_copy(1, 0)
                scale_c()
                qk_copy(3, 2)

                def score_a(h):
                    dve.wait_ge(s["scored"], 12 * l + h + 1)
                    slope = 2.0 ** (-8.0 * (h + 1) / AQ)
                    link("max_chain", nc.vector.scalar_tensor_tensor(S[:, h, :], dist[:, :], -slope, ps[:, h % 4, 0:SCORES],
                                                                     ALU.mult, ALU.add))
                    nc.vector.tensor_reduce(mx[:, h, 0:1], S[:, h, 0:P], AX_X, ALU.max)
                    nc.vector.tensor_reduce(mx[:, h, 1:2], S[:, h, P:SCORES], AX_X, ALU.max).then_inc(s["score_in"], 1)

                def score_c(h):
                    n = AQ + h
                    dve.wait_ge(s["scored"], 12 * l + n + 1)
                    dve.wait_ge(s["p_turned"], 12 * l + h + 1)
                    for t, (lo, hi) in enumerate(((0, P), (P, SCORES))):
                        i = nc.vector.tensor_tensor_reduce(S[:, h, lo:hi], ps[:, n % 4, lo:hi], relb[:, h, lo:hi], 1.0, -3e38,
                                                           ALU.add, ALU.max, mx[:, n, t:t + 1])
                    i.then_inc(s["score_in"], 1)

                def pt_copy(n):
                    dve.wait_ge(s["p_turned"], 12 * l + n + 1)
                    if n >= 2:
                        dve.wait_ge(s["pv_done"], 12 * l + n - 1)
                    nc.vector.tensor_copy(PT[:, n % 2, :], ps[:, 4 + n % 2, 0:SCORES]).then_inc(s["PT_d"], 1)

                def weigh(n0, col, order):
                    dve.wait_ge(s["pv_done"], 12 * l + n0 + 6)
                    for t in range(TILES):
                        v = proj[:, t, col:col + 384].rearrange("p (h d) -> p h d", d=HEAD)
                        r = total[:, n0:n0 + 6, t:t + 1].broadcast_to([P, 6, HEAD])
                        nc.vector.tensor_tensor(v, ps[:, 6 + t, 0:384].rearrange("p (h d) -> p h d", d=HEAD), r, ALU.mult)\
                            .then_inc(s["o_ready"], 1)

                for h in range(AQ):
                    score_a(h)
                dve.wait_ge(s["score_in"], 12 * l + AQ)
                sinks2 = sink.unsqueeze(2).broadcast_to([P, AQ, TILES])
                link("max_chain", nc.vector.tensor_tensor(mx[:, 0:AQ, :], mx[:, 0:AQ, :], sinks2, ALU.max))
                link("max_chain", nc.vector.tensor_scalar(nm[:, 0:AQ, :], mx[:, 0:AQ, :], -1.0, None, ALU.mult))
                nc.vector.tensor_tensor(esink, sinks2, nm[:, 0:AQ, :], ALU.add).then_inc(s["nm_ready"], 1)
                dve.wait_ge(s["b_psum"], l + 1)
                for g in range(BG):
                    u = proj[:, :, COL_BU + g * HEAD:COL_BU + (g + 1) * HEAD]
                    nc.vector.scalar_tensor_tensor(u, ps[:, 5, :].rearrange("p (t c) -> p t c", t=TILES)[:, :, g * HEAD:(g + 1) * HEAD],
                                                   bs[:, g:g + 1], u, ALU.add, ALU.mult).then_inc(s["b_out"], 1)
                dve.wait_ge(s["masked"], 3 * (l + 1))
                for h in range(CH):
                    score_c(h)
                    if h in (1, 3):
                        pt_copy(h)
                dve.wait_ge(s["score_in"], 12 * (l + 1))
                nc.vector.tensor_scalar(nm[:, AQ:, :], mx[:, AQ:, :], -1.0, None, ALU.mult).then_inc(s["nm_ready"], 1)
                pt_copy(5)
                dve.wait_ge(s["esink_ready"], l + 1)
                link("den_chain", nc.vector.tensor_tensor(total[:, 0:AQ, :], total[:, 0:AQ, :], esink, ALU.add))
                link("den_chain", nc.vector.reciprocal(total[:, 0:AQ, :], total[:, 0:AQ, :]))
                weigh(0, COL_AQ, 0)
                for n in (7, 9, 11):
                    pt_copy(n)
                dve.wait_ge(s["p_ready"], 12 * (l + 1))
                link("den_chain", nc.vector.reciprocal(total[:, AQ:, :], total[:, AQ:, :]))
                weigh(AQ, COL_CQ, 1)
                dve.wait_ge(s["group_rs"], l + 1)
                dve.wait_ge(s["gain_loaded"], LANDING * (3 * l + 2))
                for t in range(TILES):
                    for g, (to, col, width) in enumerate(OUT_GROUPS):
                        i = nc.vector.scalar_tensor_tensor(hn[:, t, to:to + width], proj[:, t, col:col + width],
                                                           rs_g[:, 3 * t + g:3 * t + g + 1], gain[:, to:to + width],
                                                           ALU.mult, ALU.mult)
                    i.then_inc(s["hn_ready"], 1)
                for t in range(TILES):
                    turn_low(6 * l + 2 + t)
                for c in range(OUT_SLOTS):
                    low_to(after + c + SPLIT)
                    for t in range(TILES):
                        dve.wait_ge(s["tile0_done" if t == 0 else "slot_used"], after + c + 1)
                        v = xr[:, t, c * NARROW:(c + 1) * NARROW]
                        nc.vector.tensor_tensor(v, v, ps[:, 4 + 2 * (c % 2) + t, 0:NARROW], ALU.add)\
                            .then_inc(s["x_updated"], 1)
                normed_rows(2 * l + 1, 6 * l + 4, 3 * l + 3)
                for t in range(TILES):
                    turn_low(6 * l + 4 + t)
                if l == 0:
                    def ff_mul(c):
                        up = ff_slots(c)[1]
                        for t in range(TILES):
                            dve.wait_ge(s["tile0_done" if t == 0 else "slot_used"], up + 1)
                            dve.wait_ge(s["ff_silu"], 2 * c + t + 1)
                            if c > 0:
                                dve.wait_ge(s["ff_turned"], 2 * (c - 1) + t + 1)
                            nc.vector.tensor_tensor(acted[:, 256 * t:256 * t + 256], silu[:, 256 * t:256 * t + 256],
                                                    ps[:, t, NARROW:2 * NARROW], ALU.mult).then_inc(s["ff_acted"], 1)

                    def ff_low(c):
                        for t in range(TILES):
                            dve.wait_ge(s["ff_high"], 2 * c + t + 1)
                            nc.vector.tensor_tensor(part_l[:, 256 * t:256 * t + 256], ps[:, 6 + t, 0:256],
                                                    part_h[:, 256 * t:256 * t + 256].bitcast(F32), ALU.subtract)\
                                .then_inc(s["ff_ready"], 1)

                    for c in range(FF_CHUNKS):
                        low_to(ff_slots(c)[1] + SPLIT)
                        ff_mul(c)
                        if c + 1 < FF_CHUNKS:
                            low_to(ff_slots(c)[1] + 5)
                        else:
                            low_to(ff_slots(c)[1] + 4)
                        ff_low(c)
                    for t in range(TILES):
                        dve.wait_ge(s["tile0_done" if t == 0 else "slot_used"], BASE_FF + FF_SLOTS)
                        for q in range(2):
                            v = xr[:, t, 512 * q:512 * q + 512]
                            nc.vector.tensor_tensor(v, v, ps[:, 2 + 2 * t + q, :], ALU.add).then_inc(s["x_updated"], 1)

            r = lambda ins: link("route_chain", ins)
            dve.wait_ge(s["logits_psum"], 1)
            r(nc.vector.tensor_copy(logits, ps[:, 7, 0:16].rearrange("p (t e) -> p t e", t=TILES)))
            for t in range(TILES):
                r(nc.vector.max(best[:, t, :], logits[:, t, :]))
            for t in range(TILES):
                r(nc.vector.max_index(best_index[:, t, :], best[:, t, :], logits[:, t, :]))
            r(nc.vector.tensor_tensor(margin, best[:, :, 1], best[:, :, 0], ALU.subtract))
            assert chains["route_chain"] == MARGIN_AT
            r(nc.vector.tensor_copy(best_at, best_index[:, :, 0:2]))
            for t in range(TILES):
                for k, hit in enumerate((first, second)):
                    r(nc.vector.tensor_scalar(hit[:, t, :], count_up[:, 0:EXPERTS], best_at[:, t, k:k + 1], None, ALU.is_equal))
            nc.vector.tensor_tensor(chosen, first, second, ALU.add).then_inc(s["chosen_ready"], 1)
            dve.wait_ge(s["ranks_psum"], 1)
            nc.vector.tensor_copy(ranks, ps[:, 7, 64:88]).then_inc(s["ranks_read"], 1)
            dve.wait_ge(s["emargin_ready"], 1)
            r(nc.vector.tensor_scalar(gate1, emargin, 1.0, None, ALU.add))
            r(nc.vector.reciprocal(gate1, gate1))
            r(nc.vector.tensor_tensor(gate2, gate1, emargin, ALU.mult))
            for t in range(TILES):
                r(nc.vector.tensor_scalar(first[:, t, :], first[:, t, :], gate1[:, t:t + 1], None, ALU.mult))
                r(nc.vector.scalar_tensor_tensor(item_gate[:, t, 0:EXPERTS], second[:, t, :], gate2[:, t:t + 1], first[:, t, :],
                                                 ALU.mult, ALU.add))
            dve.wait_ge(s["ranks_read"], 1)
            rank = ranks[:, 0:16].rearrange("p (t e) -> p t e", t=TILES)
            counts = ranks[:, 16:24]
            r(nc.vector.scalar_tensor_tensor(item_rank[:, :, 0:EXPERTS], rank, 1.0, chosen, ALU.add, ALU.mult))
            r(nc.vector.tensor_scalar(item_rank[:, :, 0:EXPERTS], item_rank[:, :, 0:EXPERTS], -1.0, None, ALU.add))

            def make_hot(i):
                for t in range(TILES):
                    col = item_rank[:, t, 0:1] if isinstance(i, int) else item_rank[:, t, bass.ds(i, 1)]
                    h = nc.vector.tensor_scalar(hot[:, t, :], count_up[:, :], col, None, ALU.is_equal)
                h.then_inc(s["hot_ready"], 1)

            make_hot(0)
            for t in range(TILES):
                dve.wait_ge(s["rows_high"], t + 1)
                nc.vector.tensor_tensor(rows_l[:, t, :], hn[:, t, :], rows_h[:, t, :].bitcast(F32), ALU.subtract)\
                    .then_inc(s["rows_ready"], 1)

            def item_low(i):
                for q in range(2):
                    dve.wait_ge(s["m_item_high"], i * 2 + q + 2)
                    nc.vector.tensor_tensor(item_l[:, 4 * q:4 * q + 4, :], ps[:, 2 + q, :].rearrange("p (k n) -> p k n", k=4),
                                            item_h[:, 4 * q:4 * q + 4, :].bitcast(F32), ALU.subtract)\
                        .then_inc(s["m_item_ready"], 1)

            item_low(0)
            r(nc.vector.tensor_scalar(over, counts, float(P), None, ALU.is_gt))
            r(nc.vector.memset(over_at[:, 0:1], 0.0))
            for e in range(1, EXPERTS):
                r(nc.vector.tensor_tensor(over_at[:, e:e + 1], over_at[:, e - 1:e], over[:, e - 1:e], ALU.add))
            r(nc.vector.tensor_reduce(spare[:, 0:1], over, AX_X, ALU.add))
            r(nc.vector.memset(item_rank[:, :, ITEMS - 1:ITEMS], -1.0))
            for v in range(MAX_OVER):
                r(nc.vector.scalar_tensor_tensor(pick, over_at, float(v), over, ALU.is_equal, ALU.mult))
                both = pick.unsqueeze(1).broadcast_to([P, TILES, EXPERTS])
                for table, less in ((item_rank, float(P)), (item_gate, 0.0)):
                    r(nc.vector.tensor_tensor(picked, table[:, :, 0:EXPERTS], both, ALU.mult))
                    col = table[:, :, EXPERTS + v]
                    r(nc.vector.tensor_reduce(col, picked, AX_X, ALU.add))
                    if less:
                        r(nc.vector.tensor_scalar(col, col, -less, None, ALU.add))
                r(nc.vector.tensor_tensor(pick, pick, count_up[:, 0:EXPERTS], ALU.mult))
                r(nc.vector.tensor_reduce(spare[:, 1 + v:2 + v], pick, AX_X, ALU.add))
            nc.vector.tensor_copy(plan[:, 0:1], spare[:, 0:1]).then_inc(s["plan_ready"], 1)
            nc.vector.tensor_copy(plan[:, 1:4], spare[:, 1:4]).then_inc(s["plan_ready"], 1)

            def item_body(i):
                def low_item(m):
                    j = DENSE_SLOTS + m
                    dve.wait_ge(s["high_ready"], i * ITEM_SLOTS + (j + 1))
                    nc.vector.tensor_tensor(low[:, split_place(j), :], raw[:, raw_place(j), :],
                                            high[:, split_place(j), :].bitcast(F32), ALU.subtract)\
                        .then_inc(s["slot_split"], 1)

                def mul_of(c):
                    dve.wait_ge(s["slot_used"], i * ITEM_SLOTS + (DENSE_SLOTS + ex_slots(c)[1] + 2))
                    dve.wait_ge(s["m_silu"], i * EX_CHUNKS + c + 2)
                    dve.wait_ge(s["m_turned"], i * EX_CHUNKS + c + 1)
                    nc.vector.tensor_tensor(acted, silu, ps[:, 2 * (c % 2) + 1, :], ALU.mult).then_inc(s["m_acted"], 1)

                def part_low(c):
                    dve.wait_ge(s["m_part_high"], i * EX_CHUNKS + c + 2)
                    nc.vector.tensor_tensor(part_l[:, 0:512], ps[:, 6, :], part_h[:, 0:512].bitcast(F32), ALU.subtract)\
                        .then_inc(s["m_part_ready"], 1)

                for m in range(SPLIT, ITEM_SLOTS + SPLIT):
                    low_item(m)
                    for c in range(EX_CHUNKS):
                        if m == ex_slots(c)[1] + 1 + SPLIT:
                            mul_of(c)
                    for c in range(EX_CHUNKS):
                        if m == (6 * c + 8 if c < EX_CHUNKS - 1 else ITEM_SLOTS):
                            part_low(c)
                    if m == 15:
                        dve.wait_ge(s["m_hotT_psum"], i + 1)
                        make_hot(i + 1)
                    if m == ITEM_SLOTS:
                        item_low(i + 1)
                for q in range(2):
                    dve.wait_ge(s["m_res_high"], i * 2 + q + 2)
                    nc.vector.tensor_tensor(part_l[:, 512 * q:512 * q + 512], ps[:, 4 + q, :],
                                            part_h[:, 512 * q:512 * q + 512].bitcast(F32), ALU.subtract)\
                        .then_inc(s["m_res_ready"], 1)
                for q in range(2):
                    for t in range(TILES):
                        dve.wait_ge(s["m_scattered"], i * 4 + 2 * q + t + 2)
                        v = xr[:, t, 512 * q:512 * q + 512]
                        nc.vector.scalar_tensor_tensor(v, ps[:, 2 * t + q, :], item_gate[:, t, bass.ds(i, 1)], v,
                                                       ALU.mult, ALU.add).then_inc(s["m_added"], 1)

            with dve.Fori(0, EXPERTS) as i:
                item_body(i)
            dve.wait_ge(s["plan_ready"], 2)
            extra = dve.value_load(plan[0:1, 0:1], min_val=0, max_val=MAX_OVER)
            with dve.If(extra > 0):
                with dve.Fori(0, extra) as v:
                    item_body(v + EXPERTS)

        @block.tensor
        def _(pe):
            eight = lambda t_, j: t_[:, split_place(j), :].rearrange("p (k n) -> p k n", k=KD)
            four = lambda t_, j: t_[:, split_place(j), :].rearrange("p (k n) -> p k n", k=4)
            two = lambda t_, j: t_[:, split_place(j), :].rearrange("p (k n) -> p k n", k=2)

            def three(out_, xh, xl, wh, wl, start, stop):
                nc.tensor.matmul(out_, xh, wh, start=start, stop=False)
                nc.tensor.matmul(out_, xh, wl, start=False, stop=False)
                return nc.tensor.matmul(out_, xl, wh, start=False, stop=stop)

            def turn(u):
                pe.wait_ge(s["hn_ready"], u + 1)
                for q in range(2):
                    for k in range(4):
                        c = (4 * q + k) * P
                        m = nc.tensor.transpose(ps[:, (u % 2) * 2 + q, k * P:(k + 1) * P], hn[:, u % TILES, c:c + P], ident[:, :])
                    m.then_inc(s["turned"], 1)

            def project(j, places, free=None, counts=None):
                for t in range(TILES):
                    if counts:
                        pe.wait_ge(s[free], counts[t])
                    for k in range(KD):
                        rows = slice(t * P, (t + 1) * P)
                        m = three(places[t], th[:, k, rows], tl[:, k, rows], eight(high, j)[:, k, :], eight(low, j)[:, k, :],
                                  k == 0, k == KD - 1)
                    m.then_inc(s["tile0_done" if t == 0 else "slot_used"], 1)

            pe.sem_inc(s["m_turned"], 1)
            pe.sem_inc(s["m_scattered"], 1)
            pe.wait_ge(s["const_made"], 13)
            for l in range(LAYERS):
                base, after = BASE_IN[l], BASE_OUT[l]
                for t in range(TILES):
                    turn(6 * l + t)
                pe.wait_ge(s["turned_ready"], 4 * (3 * l) + 4)
                with pe.Fori(0, IN_SLOTS // SPLIT) as trip:
                    for c in range(SPLIT):
                        pe.wait_ge(s["slot_split"], trip * SPLIT + (base + c + 1))
                        pe.wait_ge(s["evac_a"], trip * SPLIT + (IN_SLOTS * l + c + 1))
                        pe.wait_ge(s["evac_d"], trip * SPLIT + (IN_SLOTS * l + c + 1))
                        project(base + c, [ps[:, 2 * c + t, 0:NARROW] for t in range(TILES)])
                pe.wait_ge(s["evac_a"], SPLIT + IN_SLOTS * (l + 1))
                pe.wait_ge(s["evac_d"], SPLIT + IN_SLOTS * (l + 1))
                for pair in range(10):
                    pe.wait_ge(s["qk_normed"], 4 * l + (2 if pair < 4 else 4))
                    for t in range(TILES):
                        if pair < 4:
                            src = paired[:, t, pair, :, :].rearrange("p a d -> p (a d)")
                        else:
                            src = proj[:, t, COL_CQ + (pair - 4) * P:COL_CQ + (pair - 3) * P]
                        m = nc.tensor.transpose(ps[:, pair // 2, (pair % 2) * 256 + t * P:(pair % 2) * 256 + (t + 1) * P],
                                                src, ident[:, :])
                    m.then_inc(s["qk_turned"], 1)
                    if pair == 3:
                        pe.wait_ge(s["b_normed"], l + 1)
                        pe.wait_ge(s["masked"], 3 * (l + 1))
                        for t in range(TILES):
                            for g in range(BG):
                                m = nc.tensor.matmul(ps[:, 5, t * 256 + g * HEAD:t * 256 + (g + 1) * HEAD], wsT[:, g, :],
                                                     proj[:, t, COL_BV + g * HEAD:COL_BV + (g + 1) * HEAD], start=True, stop=True)
                        m.then_inc(s["b_psum"], 1)

                def score(n):
                    if n < AQ:
                        half, q, k = n // 3, n % 3, 3
                    else:
                        half, q, k = (n - AQ) % 2, 4 + (n - AQ) // 2, 7 + (n - AQ) // 2
                    pe.wait_ge(s["qkT_a"], 3 * l + (1 if n < 2 else 2 if n < AQ else 3))
                    pe.wait_ge(s["qkT_d"], 2 * l + (1 if n < 3 else 2))
                    if n >= 4:
                        pe.wait_ge(s["score_in"], 12 * l + n - 3)
                    rows = slice(half * HEAD, (half + 1) * HEAD)
                    nc.tensor.matmul(ps[:, n % 4, 0:P], qkT[rows, q, 0:P], qkT[rows, k, 0:P], start=True, stop=True)
                    nc.tensor.matmul(ps[:, n % 4, P:SCORES], qkT[rows, q, P:2 * P], qkT[rows, k, :], start=True, stop=True)\
                        .then_inc(s["scored"], 1)

                def turn_p(n):
                    pe.wait_ge(s["p_ready"], 12 * l + n + 1)
                    if n == 1:
                        pe.wait_ge(s["b_out"], 4 * (l + 1))
                    if n >= 2:
                        pe.wait_ge(s["PT_a" if n % 2 == 0 else "PT_d"], 6 * l + n // 2)
                    for b in range(3):
                        m = nc.tensor.transpose(ps[:, 4 + n % 2, b * P:(b + 1) * P], S[:, n % 6, b * P:(b + 1) * P], ident[:, :])
                    m.then_inc(s["p_turned"], 1)

                def values(n):
                    h = n if n < AQ else n - AQ
                    col = COL_AV + (h // 3) * HEAD if n < AQ else COL_CV + h * HEAD
                    if n == AQ:
                        pe.wait_ge(s["o_ready"], 4 * l + 2)
                    pe.wait_ge(s["PT_a" if n % 2 == 0 else "PT_d"], 6 * l + n // 2 + 1)
                    to = slice(h * HEAD, (h + 1) * HEAD)
                    nc.tensor.matmul(ps[:, 6, to], PT[:, n % 2, 0:P], proj[:, 0, col:col + HEAD], start=True, stop=True)
                    for b in range(2):
                        m = nc.tensor.matmul(ps[:, 7, to], PT[:, n % 2, (b + 1) * P:(b + 2) * P], proj[:, b, col:col + HEAD],
                                             start=b == 0, stop=b == 1)
                    m.then_inc(s["pv_done"], 1)

                for n in range(10):
                    score(n)
                for n in range(AQ + CH):
                    turn_p(n)
                    if n < 2:
                        score(10 + n)
                    if n >= 1:
                        values(n - 1)
                values(AQ + CH - 1)

                for t in range(TILES):
                    turn(6 * l + 2 + t)
                pe.wait_ge(s["turned_ready"], 4 * (3 * l + 1) + 4)
                for c in range(OUT_SLOTS):
                    pe.wait_ge(s["slot_split"], after + c + 1)
                    if c >= 2:
                        pe.wait_ge(s["x_updated"], 12 * l + 2 * (c - 1))
                    project(after + c, [ps[:, 4 + 2 * (c % 2) + t, 0:NARROW] for t in range(TILES)])
                for t in range(TILES):
                    turn(6 * l + 4 + t)
                pe.wait_ge(s["turned_ready"], 4 * (3 * l + 2) + 4)

                if l == 0:
                    def ff_gate(j, acted_n):
                        pe.wait_ge(s["slot_split"], j[0])
                        project(j[1], [ps[:, t, 0:NARROW] for t in range(TILES)], "ff_acted", acted_n)

                    def ff_up(j):
                        pe.wait_ge(s["slot_split"], j[0])
                        project(j[1], [ps[:, t, NARROW:2 * NARROW] for t in range(TILES)])

                    def ff_turn(acted_n, evac_n):
                        for t in range(TILES):
                            pe.wait_ge(s["ff_acted"], acted_n[t])
                            if evac_n is not None:
                                pe.wait_ge(s["ff_ready"], evac_n[t])
                            for k in range(2):
                                m = nc.tensor.transpose(ps[:, 6 + t, k * P:(k + 1) * P],
                                                        acted[:, 256 * t + k * P:256 * t + (k + 1) * P], ident[:, :])
                            m.then_inc(s["ff_turned"], 1)

                    def ff_down(j, ready_n, start, stop):
                        pe.wait_ge(s["slot_split"], j[0])
                        for t in range(TILES):
                            pe.wait_ge(s["ff_ready"], ready_n[t])
                            for q in range(2):
                                for k in range(2):
                                    rows = slice(256 * t + k * P, 256 * t + (k + 1) * P)
                                    cut = slice(512 * q, 512 * q + 512)
                                    m = three(ps[:, 2 + 2 * t + q, :], part_h[:, rows], part_l[:, rows],
                                              two(high, j[1])[:, k, cut], two(low, j[1])[:, k, cut],
                                              start and k == 0, stop and k == 1)
                            m.then_inc(s["tile0_done" if t == 0 else "slot_used"], 1)

                    g, u, _ = ff_slots(0)
                    ff_gate((g + 1, g), None)
                    ff_up((u + 1, u))
                    def ff_step(c, first):
                        const = 1
                        g, u, _ = ff_slots(const)
                        d = ff_slots(const - 1)[2]
                        away = (c - const) * 3
                        ff_gate((away + (g + 1), g), [c * 2 - 1, c * 2])
                        ff_turn([c * 2 - 1, c * 2], None if first else [(c - 1) * 2 - 1, (c - 1) * 2])
                        ff_up((away + (u + 1), u))
                        ff_down((away + (d + 1), d), [c * 2 - 1, c * 2], first, False)

                    ff_step(1, True)
                    with pe.Fori(2, FF_CHUNKS) as c:
                        ff_step(c, False)
                    last = FF_CHUNKS
                    ff_turn([2 * last - 1, 2 * last], [2 * last - 3, 2 * last - 2])
                    d = ff_slots(last - 1)[2]
                    ff_down((d + 1, d), [2 * last - 1, 2 * last], False, True)

            wrh = wr_h[:, :].rearrange("p (k e) -> p k e", k=KD)
            wrl = wr_l[:, :].rearrange("p (k e) -> p k e", k=KD)
            pe.wait_ge(s["router_split"], 1)
            pe.wait_ge(s["ident_r_made"], 1)
            for t in range(TILES):
                rows = slice(t * P, (t + 1) * P)
                to = ps[:, 7, t * EXPERTS:(t + 1) * EXPERTS]
                for k in range(KD):
                    three(to, th[:, k, rows], tl[:, k, rows], wrh[:, k, :], wrl[:, k, :], k == 0, False)
                    m = nc.tensor.matmul(to, tl[:, k, rows], wrl[:, k, :], start=False, stop=k == KD - 1)
            m.then_inc(s["logits_psum"], 1)
            pe.wait_ge(s["chosen_ready"], 1)
            pe.wait_ge(s["dist_made"], 6)
            nc.tensor.matmul(ps[:, 7, 64:72], before[:, :], chosen[:, 0, :], start=True, stop=True)
            nc.tensor.matmul(ps[:, 7, 72:80], before[:, :], chosen[:, 1, :], start=True, stop=False)
            nc.tensor.matmul(ps[:, 7, 72:80], ones[:, :], chosen[:, 0, :], start=False, stop=True)
            nc.tensor.matmul(ps[:, 7, 80:88], ones[:, :], chosen[:, 0, :], start=True, stop=False)
            nc.tensor.matmul(ps[:, 7, 80:88], ones[:, :], chosen[:, 1, :], start=False, stop=True).then_inc(s["ranks_psum"], 1)

            def gather(i):
                pe.wait_ge(s["hot_ready"], i + 1)
                for q in range(2):
                    for k in range(4):
                        c = slice((4 * q + k) * P, (4 * q + k + 1) * P)
                        to = ps[:, 2 + q, k * P:(k + 1) * P]
                        nc.tensor.matmul(to, rows_h[:, 0, c], hot[:, 0, :], start=True, stop=False)
                        nc.tensor.matmul(to, rows_l[:, 0, c], hot[:, 0, :], start=False, stop=False)
                        nc.tensor.matmul(to, rows_h[:, 1, c], hot[:, 1, :], start=False, stop=False)
                        m = nc.tensor.matmul(to, rows_l[:, 1, c], hot[:, 1, :], start=False, stop=True)
                    m.then_inc(s["m_item_psum"], 1)

            def turn_hot(i):
                for t in range(TILES):
                    m = nc.tensor.matmul(ps[:, 7, 256 + t * P:256 + (t + 1) * P], hot[:, t, :], ident_r[:, :], start=True, stop=True)
                m.then_inc(s["m_hotT_psum"], 1)

            pe.wait_ge(s["rows_ready"], TILES)
            gather(0)
            pe.wait_ge(s["ranks_read"], 1)
            turn_hot(0)

            def item_body(i):
                at_slot = i * ITEM_SLOTS

                def columns(first, bank, away):
                    for a in range(2):
                        j = DENSE_SLOTS + first + a
                        pe.wait_ge(s["slot_split"], away + (j + 1))
                        for k in range(4):
                            m = three(ps[:, bank, :], item_h[:, 4 * a + k, :], item_l[:, 4 * a + k, :],
                                      four(high, j)[:, k, :], four(low, j)[:, k, :], a + k == 0, a == 1 and k == 3)
                        m.then_inc(s["slot_used"], 1)

                def turn_acted(n):
                    pe.wait_ge(s["m_acted"], n + 2)
                    pe.wait_ge(s["m_part_ready"], n + 1)
                    for k in range(4):
                        m = nc.tensor.transpose(ps[:, 6, k * P:(k + 1) * P], acted[:, k * P:(k + 1) * P], ident[:, :])
                    m.then_inc(s["m_turned"], 1)

                def down(first, away, n, start, stop):
                    pe.wait_ge(s["m_part_ready"], n + 2)
                    for a in range(2):
                        j = DENSE_SLOTS + first + a
                        pe.wait_ge(s["slot_split"], away + (j + 1))
                        for k in range(2):
                            rows = slice((2 * a + k) * P, (2 * a + k + 1) * P)
                            for q in range(2):
                                cut = slice(512 * q, 512 * q + 512)
                                m = three(ps[:, 4 + q, :], part_h[:, rows], part_l[:, rows], two(high, j)[:, k, cut],
                                          two(low, j)[:, k, cut], start and a + k == 0, stop and a == 1 and k == 1)
                        m.then_inc(s["slot_used"], 1)

                pe.wait_ge(s["m_added"], i * 4 + 1)
                pe.wait_ge(s["m_item_ready"], i * 2 + 3)
                columns(ex_slots(0)[0], 0, at_slot)
                columns(ex_slots(0)[1], 1, at_slot)
                pe.wait_ge(s["m_res_ready"], i * 2 + 1)

                def step(c, away, done, start):
                    if c >= 2 or not start:
                        pe.wait_ge(s["m_acted"], done)
                    bank = 2 * (c % 2)
                    columns(ex_slots(c)[0], bank, away)
                    turn_acted(done - 1)
                    columns(ex_slots(c)[1], bank + 1, away)
                    down(ex_slots(c - 1)[2], away, done - 1, start, False)

                first = i * EX_CHUNKS
                step(1, at_slot, first + 1, True)
                step(2, at_slot, first + 2, False)
                with pe.Fori(0, (EX_CHUNKS - 3) // 2) as trip:
                    step(3, at_slot + trip * 12, first + trip * 2 + 3, False)
                    step(4, at_slot + trip * 12, first + trip * 2 + 4, False)
                turn_acted(first + EX_CHUNKS - 1)
                gather(i + 1)
                down(ex_slots(EX_CHUNKS - 1)[2], at_slot, first + EX_CHUNKS - 1, False, True)
                pe.wait_ge(s["m_hotT_ready"], i + 1)
                pe.wait_ge(s["m_item_ready"], i * 2 + 5)
                for q in range(2):
                    pe.wait_ge(s["m_res_ready"], i * 2 + q + 2)
                    for t in range(TILES):
                        to = ps[:, 2 * t + q, :]
                        cut = slice(512 * q, 512 * q + 512)
                        nc.tensor.matmul(to, hotT[:, t, :], part_h[:, cut], start=True, stop=False)
                        nc.tensor.matmul(to, hotT[:, t, :], part_l[:, cut], start=False, stop=True).then_inc(s["m_scattered"], 1)
                turn_hot(i + 1)

            with pe.Fori(0, EXPERTS) as i:
                item_body(i)
            pe.wait_ge(s["plan_ready"], 2)
            extra = pe.value_load(plan[0:1, 0:1], min_val=0, max_val=MAX_OVER)
            with pe.If(extra > 0):
                with pe.Fori(0, extra) as v:
                    item_body(v + EXPERTS)


def kernel(x, g_mix, w_in, qn_a, kn_a, sinks_a, ln_b_g, ln_b_b, w_s, b_s, qn_c, kn_c, rel_bias_c, g_out, w_out,
           g_ffn, w_gate_d, w_up_d, w_down_d, w_router, w_gate_e, w_up_e, w_down_e):
    import numpy as np
    import concourse.bacc as bacc
    from concourse.bass_utils import run_bass_kernel_spmd

    n = lambda a: np.ascontiguousarray(a)
    qk = np.stack([np.asarray(a) for a in (qn_a, kn_a, qn_c, kn_c)], axis=-1)
    qk = np.concatenate([qk, qk], axis=1)
    line = np.asarray(rel_bias_c)[:, :, :LAST_REL + CHUNK][:, :, ::-1]
    line = np.concatenate([line, line[:, :, -1:].repeat(CHUNK, axis=2)], axis=2)
    rel = np.stack([np.concatenate([line[:, :, LAST_REL - q:LAST_REL - q + P],
                                    line[:, :, LAST_REL - P - q:LAST_REL + P - q]], axis=2) for q in range(P)], axis=1)
    ins = {
        "x": np.asarray(x)[0], "g_mix": g_mix, "w_in": w_in, "qk_gain": qk, "sinks": sinks_a, "ln_g": ln_b_g, "ln_b": ln_b_b,
        "w_s": np.transpose(np.asarray(w_s), (0, 3, 1, 2)), "b_s": np.transpose(np.asarray(b_s), (0, 2, 1)), "rel": rel,
        "g_out": g_out, "w_out": w_out, "g_ffn": g_ffn, "w_gate_d": w_gate_d, "w_up_d": w_up_d, "w_down_d": w_down_d,
        "w_router": np.asarray(w_router)[0].reshape(KD, P, EXPERTS).transpose(1, 0, 2).reshape(P, KD * EXPERTS), "w_gate_e": w_gate_e, "w_up_e": w_up_e, "w_down_e": w_down_e,
    }
    nc = bacc.Bacc("TRN2", target_bir_lowering=False, num_devices=1)
    arrays, args = {}, {}
    for name, a in ins.items():
        arrays[f"in_{name}"] = n(a)
        args[name] = nc.dram_tensor(f"in_{name}", arrays[f"in_{name}"].shape, F32, kind="ExternalInput").ap()
    args["out"] = nc.dram_tensor("out_x", (TILES * P, D), F32, kind="ExternalOutput").ap()
    hybrid_trunk(nc, **args)
    r = run_bass_kernel_spmd(nc, [arrays], core_ids=[0])
    return r.results[0]["out_x"].reshape(1, TILES * P, D)
```

```python
from contextlib import ExitStack

import concourse.bass as bass
from concourse import mybir

F32 = mybir.dt.float32
F32R = mybir.dt.float32r
I32 = mybir.dt.int32
U32 = mybir.dt.uint32
ALU = mybir.AluOpType
ACT = mybir.ActivationFunctionType
AX_X = mybir.AxisListType.X

P = 128
TILES = 2
D = 1024
KD = D // P
CHUNK = 64
HEAD = 64
AQ, AKV, BG, CH = 6, 2, 4, 6
COL_AQ, COL_AK, COL_AV = 0, 384, 512
COL_BU, COL_BV = 640, 896
COL_CQ, COL_CK, COL_CV = 1152, 1536, 1920
IN_WIDTH = 2304
OUT_GROUPS = ((0, COL_AQ, 384), (384, COL_BU, 256), (640, COL_CQ, 384))
DFF = 2816
DFE = 3584
EXPERTS = 8
LAYERS = 2
EPS = 1e-6
NEG_INF = -1e30
FAR = 1e33
SCORES = 3 * P
LAST_REL = 255

SLOT = 2048
RAW = 6
SPLIT = 3
NARROW = SLOT // KD
IN_SLOTS = IN_WIDTH // NARROW
OUT_SLOTS = D // NARROW
FF_CHUNKS = DFF // NARROW
FF_SLOTS = 3 * FF_CHUNKS
DENSE_SLOTS = LAYERS * (IN_SLOTS + OUT_SLOTS) + FF_SLOTS
BASE_IN = (0, IN_SLOTS + OUT_SLOTS + FF_SLOTS)
BASE_OUT = (IN_SLOTS, BASE_IN[1] + IN_SLOTS)
BASE_FF = IN_SLOTS + OUT_SLOTS
WIDE = 512
EX_CHUNKS = DFE // WIDE
ITEM_SLOTS = 6 * EX_CHUNKS
OPEN_SLOTS = 4
BASE_MOE = DENSE_SLOTS + OPEN_SLOTS
CLOSE_SLOTS = ITEM_SLOTS - OPEN_SLOTS
MAX_OVER = 3
ITEMS = EXPERTS + MAX_OVER
SCATTER_BANKS = (7, 6, 4, 5)
MARGIN_AT = 4
LANDING = 16

assert ITEM_SLOTS % RAW == 0 and ITEM_SLOTS % SPLIT == 0
RAW_SHIFT = -BASE_MOE % RAW
SPLIT_SHIFT = -BASE_MOE % SPLIT


def raw_place(j):
    return (j + RAW_SHIFT) % RAW


def split_place(j):
    return (j + SPLIT_SHIFT) % SPLIT


def landings(j):
    return (j - (raw_place(j) - RAW_SHIFT) % RAW) // RAW + 1


def ff_slots(c):
    gate = BASE_FF if c == 0 else BASE_FF + 3 * c - 1
    down = BASE_FF + (3 * c + 4 if c < FF_CHUNKS - 1 else FF_SLOTS - 1)
    return gate, gate + 1, down


def step_slots(k, last=False):
    at = 6 * (k - 1)
    if k < EX_CHUNKS:
        return (at, at + 1), (at + 2, at + 3), (at + 4, at + 5)
    if last:
        return None, None, (at, at + 1)
    return (at, at + 1), (at + 2, at + 5), (at + 3, at + 4)


def hybrid_trunk(nc, x, g_mix, w_in, qk_gain, sinks, ln_g, ln_b, w_s, b_s, rel, g_out, w_out, g_ffn,
                 w_gate_d, w_up_d, w_down_d, w_router, w_gate_e, w_up_e, w_down_e, out):
    ctx = ExitStack()
    with ctx:
        def sb(name, shape, dt=F32):
            return ctx.enter_context(nc.sbuf_tensor(name, shape, dt))

        def sem(name):
            return ctx.enter_context(nc.semaphore(name))

        ps = ctx.enter_context(nc.psum_tensor("ps", [P, 8, 512], F32))

        raw = sb("raw", [P, RAW, SLOT])
        high = sb("high", [P, SPLIT, SLOT], F32R)
        low = sb("low", [P, SPLIT, SLOT], F32R)
        xr = sb("xr", [P, TILES, D])
        hn = sb("hn", [P, TILES, D])
        gain = sb("gain", [P, D])
        turned_h = sb("turned_h", [P, TILES * D], F32R)
        turned_l = sb("turned_l", [P, TILES * D], F32R)
        th = turned_h[:, :].rearrange("p (k n) -> p k n", k=KD)
        tl = turned_l[:, :].rearrange("p (k n) -> p k n", k=KD)
        work = sb("work", [P, 20 * P])
        S = work[:, 0:6 * SCORES].rearrange("p (h n) -> p h n", h=6)
        relb = sb("relb", [P, CH, SCORES])
        dist = sb("dist", [P, SCORES])
        PT = hn[:, 0, 0:2 * SCORES].rearrange("p (n c) -> p n c", n=2)
        paired = hn[:, 1, :].rearrange("p (t b a d) -> p t b a d", t=TILES, b=4, a=2)
        wsT = sb("wsT", [P, BG, P])
        lng = sb("lng", [P, BG * HEAD])
        lnb = sb("lnb", [P, BG * HEAD])
        small = sb("small", [P, 320])
        taken = [0]

        def cols(n):
            taken[0] += n
            assert taken[0] <= 320
            return small[:, taken[0] - n:taken[0]]

        bs = cols(BG)
        qkg = cols(4)
        sink = cols(AQ)
        ss_x = cols(2 * LAYERS * TILES)
        ms_x = cols(2 * LAYERS * TILES)
        rs_x = cols(2 * LAYERS * TILES)
        ss_q = cols(40)
        rs_q = cols(40)
        mean_b = cols(8)
        var_b = cols(8)
        rs_b = cols(8)
        mx = cols(24).rearrange("p (n t) -> p n t", t=TILES)
        nm = cols(24).rearrange("p (n t) -> p n t", t=TILES)
        total = cols(24).rearrange("p (n t) -> p n t", t=TILES)
        esink = cols(12).rearrange("p (n t) -> p n t", t=TILES)
        ss_g = cols(6)
        rs_g = cols(6)
        inv_n = cols(6)
        halves = cols(40)
        ident = sb("ident", [P, P])
        ident_r = sb("ident_r", [P, P], F32R)
        count_up = sb("count_up", [P, P])
        before = sb("before", [P, P])
        ones = sb("ones", [P, P])
        silu = work[:, 0:512]
        acted = work[:, 512:1024]
        part_h = sb("part_h", [P, 512], F32R)
        part_l = sb("part_l", [P, 512], F32R)
        wr = sb("wr", [P, KD * EXPERTS])
        wr_hl = sb("wr_hl", [P, KD, 2 * EXPERTS], F32R)
        logitsT = sb("logitsT", [2 * EXPERTS, TILES * P])
        stack = sb("stack", [2 * EXPERTS, EXPERTS])
        route = work[:, 2304:2560]
        used = [0]

        def rcols(n, **kw):
            used[0] += n
            assert used[0] <= 256
            a = route[:, used[0] - n:used[0]]
            return a.rearrange("p (t e) -> p t e", **kw) if kw else a

        logits = rcols(16, t=2)
        best = rcols(16, t=2)
        best_at = rcols(4, t=2)
        margin = rcols(2)
        emargin = rcols(2)
        gate1 = rcols(2)
        gate2 = rcols(2)
        first = rcols(16, t=2)
        second = rcols(16, t=2)
        chosen = rcols(16, t=2)
        ranks = rcols(24)
        over = rcols(8)
        over_at = rcols(8)
        pick = rcols(8)
        picked = rcols(16, t=2)
        spare = rcols(5)
        item_rank = rcols(2 * ITEMS, t=2)
        item_gate = rcols(2 * ITEMS, t=2)
        best_index = sb("best_index", [P, 2, 8], U32)
        plan = sb("plan", [P, 5], I32)
        hot = sb("hot", [P, TILES, P], F32R)
        hotT = sb("hotT", [P, TILES, P], F32R)
        item_h = sb("item_h", [P, KD, P], F32R)
        item_l = sb("item_l", [P, KD, P], F32R)

        with nc.sbuf_tensor("proj", [P, TILES, IN_WIDTH], F32) as proj, nc.sbuf_tensor("qkT", [P, 10, TILES * P], F32) as qkT:
            pass
        rows_h = sb("rows_h", [P, TILES, D], F32R)
        rows_l = sb("rows_l", [P, TILES, D], F32R)
        res_h = sb("res_h", [P, D], F32R)
        res_l = sb("res_l", [P, D], F32R)

        s = {}

        def sems(*names):
            for n in names:
                s[n] = sem(n)

        landed = [sem(f"landed{r}") for r in range(RAW)]
        sems("high_ready", "slot_split", "slot_used", "tile0_done")
        sems("x0_loaded", "x1_loaded", "gain_loaded", "param_loaded", "router_loaded")
        sems("const_made", "const_chain", "dist_made", "masked", "ident_r_made", "router_high", "router_split", "qkg_scaled")
        sems("x_squared", "x_ms", "x_rs", "hn_ready", "turned", "turned_high", "turned_ready", "x_updated")
        sems("evac_a", "evac_d", "qk_squared", "qk_sum", "qk_rs", "qk_normed", "pool_chain")
        sems("gelu_done", "b_chain", "b_var", "b_rs", "b_normed", "b_psum", "b_out")
        sems("qk_turned", "qkT_a", "qkT_d", "scored", "score_in", "max_chain", "nm_ready", "p_ready", "esink_ready")
        sems("p_turned", "PT_a", "PT_d", "pv_done", "den_chain", "o_ready", "group_squared", "group_rs")
        sems("ff_silu", "ff_acted", "ff_turned", "ff_high", "ff_ready")
        sems("logitsT_psum", "logitsT_read", "logits_psum", "route_chain", "plan_chain", "item_tables", "stack_made", "emargin_ready", "chosen_ready", "ranks_psum", "ranks_read", "rows_high", "rows_ready", "plan_ready")
        sems("hot_ready", "m_hotT_psum", "m_hotT_ready", "m_item_psum", "m_item_high", "m_item_ready")
        sems("m_silu", "m_acted", "m_turned", "m_part_high", "m_part_ready", "m_res_high", "m_res_ready", "m_scattered", "m_added")
        sems("x_stored")

        def rms_index(l, ffn):
            return 2 * l + ffn

        block = ctx.enter_context(nc.Block())

        @block.sync
        def _(sp):
            narrow = lambda w: w.rearrange("(k p) n -> p k n", p=P)
            eight = lambda r: raw[:, r, :].rearrange("p (k n) -> p k n", k=KD)
            four = lambda r: raw[:, r, :].rearrange("p (k n) -> p k n", k=4)
            two = lambda r: raw[:, r, :].rearrange("p (k n) -> p k n", k=2)

            def send(j, to, src):
                if j >= RAW:
                    sp.wait_ge(s["slot_split"], j - RAW + 1)
                sp.dma_start(to(raw_place(j)), src).then_inc(landed[raw_place(j)], LANDING)

            for t in range(TILES):
                sp.dma_start(xr[:, t, :], x[t * P:(t + 1) * P, :]).then_inc(s[f"x{t}_loaded"], LANDING)
            for l in range(LAYERS):
                for c in range(IN_SLOTS):
                    send(BASE_IN[l] + c, eight, narrow(w_in[l])[:, :, c * NARROW:(c + 1) * NARROW])
                for c in range(OUT_SLOTS):
                    send(BASE_OUT[l] + c, eight, narrow(w_out[l])[:, :, c * NARROW:(c + 1) * NARROW])
                if l == 0:
                    for c in range(FF_CHUNKS + 1):
                        if c < FF_CHUNKS:
                            cut = slice(c * NARROW, (c + 1) * NARROW)
                            send(ff_slots(c)[0], eight, narrow(w_gate_d[0])[:, :, cut])
                            send(ff_slots(c)[1], eight, narrow(w_up_d[0])[:, :, cut])
                        if c > 0:
                            send(ff_slots(c - 1)[2], two, narrow(w_down_d[0])[:, 2 * (c - 1):2 * c, :])

            up_view = lambda w: w[0].rearrange("e (k p) n -> e p k n", p=P)

            first_down = step_slots(1)[2][0]

            def put(m, i, to, src):
                j = BASE_MOE + m
                if m != first_down:
                    sp.wait_ge(s["slot_split"], i * ITEM_SLOTS + (j - RAW + (2 if m == first_down - 1 else 1)))
                sp.dma_start(to(raw_place(j)), src).then_inc(landed[raw_place(j)], LANDING)

            def put_columns(m, i, w, e, c, a):
                if isinstance(e, tuple):
                    start, e = e
                    put(m, i, four, up_view(w)[start:, :, 4 * a:4 * a + 4, c * WIDE:(c + 1) * WIDE][e])
                    return
                put(m, i, four, up_view(w)[e, :, 4 * a:4 * a + 4, c * WIDE:(c + 1) * WIDE])

            def put_down(m, i, e, c, a):
                put(m, i, two, up_view(w_down_e)[e, :, 4 * c + 2 * a:4 * c + 2 * a + 2, :])

            def send_item(i, e, e_next):
                for k in range(1, EX_CHUNKS):
                    gate, up, down = step_slots(k)
                    for a in range(2):
                        put_columns(gate[a], i, w_gate_e, e, k, a)
                    for a in range(2):
                        put_columns(up[a], i, w_up_e, e, k, a)
                    for a in range(2):
                        put_down(down[a], i, e, k - 1, a)
                gate, up, down = step_slots(EX_CHUNKS, e_next is None)
                if e_next is not None:
                    for a in range(2):
                        put_columns(gate[a], i, w_gate_e, e_next, 0, a)
                    put_columns(up[0], i, w_up_e, e_next, 0, 0)
                for a in range(2):
                    put_down(down[a], i, e, EX_CHUNKS - 1, a)
                if e_next is not None:
                    put_columns(up[1], i, w_up_e, e_next, 0, 1)

            for a in range(2):
                send(DENSE_SLOTS + a, four, up_view(w_gate_e)[0, :, 4 * a:4 * a + 4, 0:WIDE])
            for a in range(2):
                send(DENSE_SLOTS + 2 + a, four, up_view(w_up_e)[0, :, 4 * a:4 * a + 4, 0:WIDE])
            with sp.Fori(0, EXPERTS - 1) as i:
                send_item(i, i, (1, i))
            sp.wait_ge(s["plan_ready"], 1)
            extra = sp.value_load(plan[0:1, 0:1], min_val=0, max_val=MAX_OVER)
            expert_of = lambda v: sp.value_load(plan[0:1, bass.ds(v + 1, 1)], min_val=0, max_val=EXPERTS - 1)
            with sp.If(extra > 0):
                with sp.Fori(0, extra) as v:
                    send_item(v + (EXPERTS - 1), expert_of(v), expert_of(v + 1))
            send_item(extra + (EXPERTS - 1), expert_of(extra), None)
            sp.wait_ge(s["m_added"], (extra + EXPERTS) * 4 + 1)
            for t in range(TILES):
                sp.dma_start(out[t * P:(t + 1) * P, :], xr[:, t, :]).then_inc(s["x_stored"], LANDING)
            sp.wait_ge(s["x_stored"], TILES * LANDING)

        @block.gpsimd
        def _(pool):
            loads = [0]

            def load_gain(n):
                row = (g_mix, g_out, g_ffn)[n % 3][n // 3]
                pool.dma_start(gain[:, :], row.partition_broadcast(P)).then_inc(s["gain_loaded"], LANDING)

            def load_params(l):
                for to, src in ((relb[:, :, :], rel[l]), (wsT[:, :, :], w_s[l]), (bs, b_s[l]), (qkg, qk_gain[l]),
                                (lng[:, :], ln_g[l].partition_broadcast(P)), (lnb[:, :], ln_b[l].partition_broadcast(P)),
                                (sink, sinks[l].partition_broadcast(P))):
                    pool.dma_start(to, src).then_inc(s["param_loaded"], LANDING)
                    loads[0] += LANDING
                pool.wait_ge(s["param_loaded"], loads[0])
                pool.wait_ge(s["x_rs"], TILES * (2 * l + 1))
                nc.gpsimd.memset(relb[0:CHUNK, :, CHUNK:P], NEG_INF).then_inc(s["masked"], 1)
                nc.gpsimd.memset(relb[0:CHUNK, :, SCORES - CHUNK:SCORES], NEG_INF).then_inc(s["masked"], 1)
                nc.gpsimd.memset(wsT[CHUNK:P, :, 0:CHUNK], 0.0).then_inc(s["masked"], 1)
                pool.wait_ge(s["masked"], 3 * (l + 1))

            load_gain(0)
            nc.gpsimd.memset(halves, -0.5).then_inc(s["const_made"], 1)
            nc.gpsimd.memset(ident[:, :], 0.0).then_inc(s["const_chain"], 1)
            pool.wait_ge(s["const_chain"], 1)
            nc.gpsimd.affine_select(out=ident[:, :], in_=ident[:, :], compare_op=ALU.not_equal, fill=1.0, base=0,
                                    pattern=[[-1, P]], channel_multiplier=1).then_inc(s["const_made"], 1)
            nc.gpsimd.iota(count_up[:, :], [[1, P]], base=0, channel_multiplier=0,
                           allow_small_or_imprecise_dtypes=True).then_inc(s["const_made"], 1)
            nc.gpsimd.iota(before[:, :], [[1, P]], base=0, channel_multiplier=-1,
                           allow_small_or_imprecise_dtypes=True).then_inc(s["const_made"], 1)
            nc.gpsimd.iota(dist[:, 0:P], [[-1, P]], base=0, channel_multiplier=1,
                           allow_small_or_imprecise_dtypes=True).then_inc(s["const_made"], 1)
            nc.gpsimd.iota(dist[:, P:SCORES], [[-1, 2 * P]], base=P, channel_multiplier=1,
                           allow_small_or_imprecise_dtypes=True).then_inc(s["const_made"], 1)
            nc.gpsimd.memset(ones[:, :], 1.0).then_inc(s["const_made"], 1)
            for t in range(TILES):
                for g, (_, _, width) in enumerate(OUT_GROUPS):
                    nc.gpsimd.memset(inv_n[:, 3 * t + g:3 * t + g + 1], 1.0 / width).then_inc(s["const_made"], 1)
            pool.dma_start(wr[:, :], w_router).then_inc(s["router_loaded"], LANDING)
            chain = [0]

            def power(out_, ms, done):
                pool.wait_ge(s["pool_chain"], chain[0])
                nc.gpsimd.tensor_tensor(out_, ms, halves[:, 0:out_.shape[1]], ALU.pow).then_inc(s[done], 1)

            def mean_eps(to, sums, scale):
                nc.gpsimd.tensor_scalar(to, sums, scale, EPS, ALU.mult, ALU.add).then_inc(s["pool_chain"], 1)
                chain[0] += 1

            def rms_rows(n):
                for t in range(TILES):
                    c = slice(TILES * n + t, TILES * n + t + 1)
                    pool.wait_ge(s["x_squared"], TILES * n + t + 1)
                    mean_eps(ms_x[:, c], ss_x[:, c], 1.0 / D)
                    power(rs_x[:, c], ms_x[:, c], "x_rs")

            def next_gain(n):
                pool.wait_ge(s["hn_ready"], TILES * n)
                load_gain(n)

            for l in range(LAYERS):
                rms_rows(2 * l)
                load_params(l)
                next_gain(3 * l + 1)
                for part, lo, n in (("a", 0, 16), ("b", 0, 8), ("c", 16, 24)):
                    if part == "b":
                        pool.wait_ge(s["b_var"], l + 1)
                        mean_eps(var_b, var_b, 1.0 / HEAD)
                        power(rs_b, var_b, "b_rs")
                    else:
                        pool.wait_ge(s["qk_sum"], 2 * l + (1 if part == "a" else 2))
                        mean_eps(ss_q[:, lo:lo + n], ss_q[:, lo:lo + n], 1.0 / HEAD)
                        power(rs_q[:, lo:lo + n], ss_q[:, lo:lo + n], "qk_rs")
                pool.wait_ge(s["group_squared"], 6 * (l + 1))
                nc.gpsimd.tensor_tensor(ss_g, ss_g, inv_n, ALU.mult).then_inc(s["pool_chain"], 1)
                chain[0] += 1
                pool.wait_ge(s["pool_chain"], chain[0])
                mean_eps(ss_g, ss_g, 1.0)
                power(rs_g, ss_g, "group_rs")
                next_gain(3 * l + 2)
                rms_rows(2 * l + 1)
                if l + 1 < LAYERS:
                    next_gain(3 * l + 3)

            links = [0]

            def r(ins):
                links[0] += 1
                ins.then_inc(s["plan_chain"], 1)
                pool.wait_ge(s["plan_chain"], links[0])

            def sum_experts(to, v):
                for n in (4, 2):
                    r(nc.gpsimd.tensor_tensor(v[:, :, 0:n], v[:, :, 0:n], v[:, :, n:2 * n], ALU.add))
                r(nc.gpsimd.tensor_tensor(to, v[:, :, 0], v[:, :, 1], ALU.add))

            pool.wait_ge(s["item_tables"], 1)
            r(nc.gpsimd.tensor_scalar(over, ranks[:, 16:24], float(P), None, ALU.is_gt))
            r(nc.gpsimd.memset(over_at[:, 0:1], 0.0))
            for e in range(1, EXPERTS):
                r(nc.gpsimd.tensor_tensor(over_at[:, e:e + 1], over_at[:, e - 1:e], over[:, e - 1:e], ALU.add))
            r(nc.gpsimd.tensor_tensor(spare[:, 0:1], over_at[:, EXPERTS - 1:], over[:, EXPERTS - 1:], ALU.add))
            r(nc.gpsimd.memset(spare[:, 1:2], float(EXPERTS - 1)))
            for v in range(MAX_OVER):
                r(nc.gpsimd.tensor_scalar(pick, over_at, float(v), None, ALU.is_equal))
                r(nc.gpsimd.tensor_tensor(pick, pick, over, ALU.mult))
                both = pick.unsqueeze(1).broadcast_to([P, TILES, EXPERTS])
                for table, less in ((item_rank, float(P)), (item_gate, 0.0)):
                    r(nc.gpsimd.tensor_tensor(picked, table[:, :, 0:EXPERTS], both, ALU.mult))
                    col = table[:, :, EXPERTS + v]
                    sum_experts(col, picked)
                    if less:
                        r(nc.gpsimd.tensor_scalar(col, col, -less, None, ALU.add))
                r(nc.gpsimd.tensor_tensor(picked[:, 0, :], pick, count_up[:, 0:EXPERTS], ALU.mult))
                sum_experts(spare[:, 2 + v:3 + v], picked[:, 0:1, :])
            nc.gpsimd.tensor_copy(plan[:, :], spare).then_inc(s["plan_ready"], 1)

        @block.scalar
        def _(act):
            at = [0]

            def high_to(m):
                for j in range(at[0], m + 1):
                    act.wait_ge(landed[raw_place(j)], LANDING * landings(j))
                    if j >= SPLIT:
                        act.wait_ge(s["slot_used"], j - SPLIT + 1)
                    nc.scalar.activation(high[:, split_place(j), :], raw[:, raw_place(j), :], ACT.Copy)\
                        .then_inc(s["high_ready"], 1)
                at[0] = max(at[0], m + 1)

            def square_rows(n, need):
                for t in range(TILES):
                    need(t)
                    c = TILES * n + t
                    nc.scalar.activation(work[:, t * D:(t + 1) * D], xr[:, t, :], ACT.Square,
                                         accum_out=ss_x[:, c:c + 1]).then_inc(s["x_squared"], 1)

            def turn_high(u):
                t = u % TILES
                for q in range(2):
                    act.wait_ge(s["turned"], 2 * u + q + 1)
                    bank = (u % 2) * 2 + q
                    nc.scalar.activation(th[:, 4 * q:4 * q + 4, t * P:(t + 1) * P],
                                         ps[:, bank, :].rearrange("p (k n) -> p k n", k=4), ACT.Copy)\
                        .then_inc(s["turned_high"], 1)

            act.sem_inc(s["evac_a"], SPLIT)
            square_rows(0, lambda t: act.wait_ge(s[f"x{t}_loaded"], LANDING))
            act.wait_ge(s["const_made"], 13)
            nc.scalar.activation(ident_r[:, :], ident[:, :], ACT.Copy).then_inc(s["ident_r_made"], 1)

            for l in range(LAYERS):
                base, after = BASE_IN[l], BASE_OUT[l]
                high_to(base + SPLIT - 1)
                for t in range(TILES):
                    turn_high(6 * l + t)
                for c in range(IN_SLOTS):
                    high_to(base + c + SPLIT)
                    act.wait_ge(s["tile0_done"], base + c + 1)
                    nc.scalar.activation(proj[:, 0, c * NARROW:(c + 1) * NARROW], ps[:, 2 * (c % 3), 0:NARROW], ACT.Copy)\
                        .then_inc(s["evac_a"], 1)
                    if c in (2, 5, 8):
                        act.wait_ge(s["evac_a"], SPLIT + IN_SLOTS * l + c)
                        act.wait_ge(s["evac_d"], SPLIT + IN_SLOTS * l + c)
                    if c == 1 and l == 0:
                        act.wait_ge(s["router_loaded"], LANDING)
                        nc.scalar.activation(wr_hl[:, :, 0:EXPERTS], wr[:, :].rearrange("p (k e) -> p k e", k=KD), ACT.Copy)\
                            .then_inc(s["router_high"], 1)
                    if c == 2:
                        for t in range(TILES):
                            nc.scalar.activation(work[:, 512 * t:512 * t + 512], proj[:, t, COL_AQ:COL_AV], ACT.Square)\
                                .then_inc(s["qk_squared"], 1)
                    if c == 5:
                        for t in range(TILES):
                            nc.scalar.activation(proj[:, t, COL_BU:COL_CQ], proj[:, t, COL_BU:COL_CQ], ACT.Gelu)\
                                .then_inc(s["gelu_done"], 1)
                    if c == 8:
                        for t in range(TILES):
                            nc.scalar.activation(work[:, 1024 + 768 * t:1792 + 768 * t], proj[:, t, COL_CQ:COL_CV], ACT.Square)\
                                .then_inc(s["qk_squared"], 1)
                act.wait_ge(s["qkg_scaled"], l + 1)
                for bank, g in ((0, 0), (2, 2), (4, 3)):
                    act.wait_ge(s["qk_turned"], 10 * l + 2 * bank + 2)
                    nc.scalar.activation(qkT[:, 2 * bank:2 * bank + 2, :], ps[:, bank, :].rearrange("p (a n) -> p a n", a=2),
                                         ACT.Copy, scale=qkg[:, g:g + 1]).then_inc(s["qkT_a"], 1)

                def pt_copy(n):
                    act.wait_ge(s["p_turned"], 12 * l + n + 1)
                    if n >= 2:
                        act.wait_ge(s["pv_done"], 12 * l + n - 1)
                    nc.scalar.activation(PT[:, n % 2, :], ps[:, 4 + n % 2, 0:SCORES], ACT.Copy).then_inc(s["PT_a"], 1)

                for n in range(AQ + CH):
                    if n in (0, AQ):
                        act.wait_ge(s["nm_ready"], 2 * l + (1 if n == 0 else 2))
                    for t, (lo, hi) in enumerate(((0, P), (P, SCORES))):
                        e = nc.scalar.activation(S[:, n % 6, lo:hi], S[:, n % 6, lo:hi], ACT.Exp,
                                                 bias=nm[:, n, t:t + 1], accum_out=total[:, n, t:t + 1])
                    e.then_inc(s["p_ready"], 1)
                    if n == AQ - 1:
                        nc.scalar.activation(esink, esink, ACT.Exp).then_inc(s["esink_ready"], 1)
                    if n >= 2 and n % 2 == 0:
                        pt_copy(n - 2)
                pt_copy(10)
                act.wait_ge(s["b_out"], 4 * (l + 1))
                act.wait_ge(s["o_ready"], 4 * (l + 1))
                for t in range(TILES):
                    for g, (to, col, width) in enumerate(OUT_GROUPS):
                        nc.scalar.activation(work[:, t * D + to:t * D + to + width], proj[:, t, col:col + width], ACT.Square,
                                             accum_out=ss_g[:, 3 * t + g:3 * t + g + 1]).then_inc(s["group_squared"], 1)
                for t in range(TILES):
                    turn_high(6 * l + 2 + t)
                high_to(after + OUT_SLOTS + SPLIT - 1)
                done = (8 if l == 0 else 20)
                square_rows(2 * l + 1, lambda t: act.wait_ge(s["x_updated"], done - 1 + t))
                for t in range(TILES):
                    turn_high(6 * l + 4 + t)
                if l == 0:
                    def ff_silu(c):
                        up = ff_slots(c)[1]
                        for t in range(TILES):
                            act.wait_ge(s["tile0_done" if t == 0 else "slot_used"], up + 1)
                            if c > 0:
                                act.wait_ge(s["ff_acted"], 2 * (c - 1) + t + 1)
                            nc.scalar.activation(silu[:, 256 * t:256 * t + 256], ps[:, t, 0:NARROW], ACT.Silu)\
                                .then_inc(s["ff_silu"], 1)

                    def ff_high(c):
                        for t in range(TILES):
                            act.wait_ge(s["ff_turned"], 2 * c + t + 1)
                            if c > 0:
                                act.wait_ge(s["slot_used"], ff_slots(c - 1)[2] + 1)
                            nc.scalar.activation(part_h[:, 256 * t:256 * t + 256], ps[:, 6 + t, 0:256], ACT.Copy)\
                                .then_inc(s["ff_high"], 1)

                    for c in range(FF_CHUNKS):
                        if c > 0:
                            high_to(ff_slots(c)[0] + SPLIT)
                            ff_high(c - 1)
                        high_to(ff_slots(c)[1] + SPLIT)
                        ff_silu(c)
                    high_to(ff_slots(FF_CHUNKS - 1)[1] + 4)
                    ff_high(FF_CHUNKS - 1)
                    square_rows(2, lambda t: act.wait_ge(s["x_updated"], 8 + 2 * (t + 1)))

            for t in range(TILES):
                nc.scalar.activation(rows_h[:, t, :], hn[:, t, :], ACT.Copy).then_inc(s["rows_high"], 1)
            act.wait_ge(s["logitsT_psum"], 1)
            nc.scalar.activation(logitsT[:, :], ps[0:2 * EXPERTS, 7, 0:TILES * P], ACT.Copy).then_inc(s["logitsT_read"], 1)
            act.wait_ge(s["route_chain"], MARGIN_AT)
            nc.scalar.activation(emargin, margin, ACT.Exp).then_inc(s["emargin_ready"], 1)

            def item_high(i):
                for q in range(2):
                    act.wait_ge(s["m_item_psum"], i * 2 + (q + 1))
                    nc.scalar.activation(item_h[:, 4 * q:4 * q + 4, :], ps[:, 2 + q, :].rearrange("p (k n) -> p k n", k=4),
                                         ACT.Copy).then_inc(s["m_item_high"], 1)

            item_high(0)
            high_to(DENSE_SLOTS + 1 + SPLIT)
            act.wait_ge(s["slot_used"], DENSE_SLOTS + 2)
            nc.scalar.activation(silu, ps[:, 0, :], ACT.Silu).then_inc(s["m_silu"], 1)
            high_to(BASE_MOE + SPLIT - 1)

            def item_body(i, last=False):
                used = lambda m: i * ITEM_SLOTS + (BASE_MOE + m + 1)

                def high_item(m):
                    j = BASE_MOE + m
                    act.wait_ge(landed[raw_place(j)], i * (ITEM_SLOTS // RAW * LANDING) + LANDING * landings(j))
                    act.wait_ge(s["slot_used"], used(m - SPLIT))
                    nc.scalar.activation(high[:, split_place(j), :], raw[:, raw_place(j), :], ACT.Copy)\
                        .then_inc(s["high_ready"], 1)

                slots = CLOSE_SLOTS if last else ITEM_SLOTS + SPLIT
                for m in range(SPLIT, slots):
                    if not last and m == step_slots(EX_CHUNKS)[2][1] + SPLIT:
                        act.wait_ge(s["slot_used"], used(m - SPLIT))
                        for q in range(2):
                            nc.scalar.activation(res_h[:, 512 * q:512 * q + 512], ps[:, 4 + q, :], ACT.Copy)\
                                .then_inc(s["m_res_high"], 1)
                    high_item(m)
                    for k in range(1, EX_CHUNKS + 1):
                        if m == 6 * (k - 1) + 1 + SPLIT and not (last and k == EX_CHUNKS):
                            act.wait_ge(s["slot_used"], used(m - SPLIT))
                            act.wait_ge(s["m_acted"], i * EX_CHUNKS + k)
                            nc.scalar.activation(silu, ps[:, 2 * (k % EX_CHUNKS % 2), :], ACT.Silu).then_inc(s["m_silu"], 1)
                            act.wait_ge(s["m_turned"], i * EX_CHUNKS + k)
                            nc.scalar.activation(part_h[:, :], ps[:, 6, :], ACT.Copy).then_inc(s["m_part_high"], 1)
                    if m == step_slots(2)[0][0] + SPLIT:
                        act.wait_ge(s["m_hotT_psum"], i + 1)
                        nc.scalar.activation(hotT[:, :, :].rearrange("p t n -> p (t n)"), ps[:, 7, 256:512], ACT.Copy)\
                            .then_inc(s["m_hotT_ready"], 1)
                    if m == step_slots(6)[1][1] + SPLIT and not last:
                        item_high(i + 1)
                if last:
                    act.wait_ge(s["m_turned"], (i + 1) * EX_CHUNKS)
                    nc.scalar.activation(part_h[:, :], ps[:, 6, :], ACT.Copy).then_inc(s["m_part_high"], 1)
                    act.wait_ge(s["slot_used"], used(CLOSE_SLOTS - 1))
                    for q in range(2):
                        nc.scalar.activation(res_h[:, 512 * q:512 * q + 512], ps[:, 4 + q, :], ACT.Copy)\
                            .then_inc(s["m_res_high"], 1)

            with act.Fori(0, EXPERTS - 1) as i:
                item_body(i)
            act.wait_ge(s["plan_ready"], 1)
            extra = act.value_load(plan[0:1, 0:1], min_val=0, max_val=MAX_OVER)
            with act.If(extra > 0):
                with act.Fori(0, extra) as v:
                    item_body(v + (EXPERTS - 1))
            item_body(extra + (EXPERTS - 1), last=True)

        @block.vector
        def _(dve):
            at = [0]
            chains = {}

            def link(name, ins):
                chains[name] = chains.get(name, 0) + 1
                ins.then_inc(s[name], 1)
                dve.wait_ge(s[name], chains[name])

            def low_to(m):
                for j in range(at[0], m + 1):
                    dve.wait_ge(s["high_ready"], j + 1)
                    nc.vector.tensor_tensor(low[:, split_place(j), :], raw[:, raw_place(j), :],
                                            high[:, split_place(j), :].bitcast(F32), ALU.subtract)\
                        .then_inc(s["slot_split"], 1)
                at[0] = max(at[0], m + 1)

            def normed_rows(n, u, gains):
                for t in range(TILES):
                    dve.wait_ge(s["x_rs"], TILES * n + t + 1)
                    dve.wait_ge(s["gain_loaded"], LANDING * gains)
                    c = TILES * n + t
                    nc.vector.scalar_tensor_tensor(hn[:, t, :], xr[:, t, :], rs_x[:, c:c + 1], gain[:, :],
                                                   ALU.mult, ALU.mult).then_inc(s["hn_ready"], 1)

            def turn_low(u):
                t = u % TILES
                for q in range(2):
                    dve.wait_ge(s["turned_high"], 2 * u + q + 1)
                    bank = (u % 2) * 2 + q
                    cut = (slice(None), slice(4 * q, 4 * q + 4), slice(t * P, (t + 1) * P))
                    nc.vector.tensor_tensor(tl[cut], ps[:, bank, :].rearrange("p (k n) -> p k n", k=4),
                                            th[cut].bitcast(F32), ALU.subtract).then_inc(s["turned_ready"], 1)

            dve.sem_inc(s["evac_d"], SPLIT)
            for name in ("m_part_ready", "m_added"):
                dve.sem_inc(s[name], 1)
            dve.wait_ge(s["const_made"], 13)
            link("dist_made", nc.vector.scalar_tensor_tensor(dist[:, :], dist[:, :], -1.0, dist[:, :], ALU.mult, ALU.max))
            for rows, lo, hi in (((0, CHUNK), CHUNK, P), ((0, CHUNK), P, P + CHUNK), ((0, CHUNK), SCORES - CHUNK, SCORES),
                                 ((CHUNK, P), P, 2 * P)):
                link("dist_made", nc.vector.memset(dist[rows[0]:rows[1], lo:hi], FAR))
            link("dist_made", nc.vector.tensor_scalar(before[:, :], before[:, :], 0.0, None, ALU.is_gt))
            nc.vector.tensor_tensor(stack[:, :], ident[0:2 * EXPERTS, 0:EXPERTS], ident[0:2 * EXPERTS, EXPERTS:2 * EXPERTS],
                                    ALU.add).then_inc(s["stack_made"], 1)

            for l in range(LAYERS):
                base, after = BASE_IN[l], BASE_OUT[l]
                normed_rows(2 * l, 6 * l, 3 * l + 1)
                for t in range(TILES):
                    turn_low(6 * l + t)
                low_to(base + SPLIT - 1)

                def scale_a():
                    dve.wait_ge(s["qk_rs"], 2 * l + 1)
                    for t in range(TILES):
                        r = rs_q[:, 8 * t:8 * t + 8]
                        for half in range(2):
                            cut = slice(3 * half, 3 * half + 3)
                            q = proj[:, t, COL_AQ + 192 * half:COL_AQ + 192 * half + 192].rearrange("p (h d) -> p h d", d=HEAD)
                            nc.vector.tensor_tensor(paired[:, t, 0:3, half, :], q,
                                                    r[:, cut].unsqueeze(2).broadcast_to([P, 3, HEAD]), ALU.mult)
                        k = proj[:, t, COL_AK:COL_AV].rearrange("p (h d) -> p h d", d=HEAD)
                        nc.vector.tensor_tensor(paired[:, t, 3, :, :], k, r[:, AQ:].unsqueeze(2).broadcast_to([P, AKV, HEAD]),
                                                ALU.mult).then_inc(s["qk_normed"], 1)

                def scale_c():
                    dve.wait_ge(s["qk_rs"], 2 * l + 2)
                    for t in range(TILES):
                        v = proj[:, t, COL_CQ:COL_CV].rearrange("p (h d) -> p h d", d=HEAD)
                        r = rs_q[:, 16 + 12 * t:28 + 12 * t].unsqueeze(2).broadcast_to([P, 2 * CH, HEAD])
                        nc.vector.tensor_tensor(v, v, r, ALU.mult).then_inc(s["qk_normed"], 1)

                bv = proj[:, :, COL_BV:COL_CQ].rearrange("p t (g d) -> p t g d", d=HEAD)
                bsq = work[:, 1024:1536]
                for c in range(IN_SLOTS):
                    low_to(base + c + SPLIT)
                    dve.wait_ge(s["slot_used"], base + c + 1)
                    nc.vector.tensor_copy(proj[:, 1, c * NARROW:(c + 1) * NARROW], ps[:, 2 * (c % 3) + 1, 0:NARROW])\
                        .then_inc(s["evac_d"], 1)
                    if c == 1:
                        dve.wait_ge(s["param_loaded"], 7 * LANDING * (l + 1))
                        nc.vector.tensor_scalar(qkg[:, 0:4:2], qkg[:, 0:4:2], HEAD ** -0.5, None, ALU.mult)\
                            .then_inc(s["qkg_scaled"], 1)
                    if c == 2 and l == 0:
                        dve.wait_ge(s["router_high"], 1)
                        nc.vector.tensor_tensor(wr_hl[:, :, EXPERTS:], wr[:, :].rearrange("p (k e) -> p k e", k=KD),
                                                wr_hl[:, :, 0:EXPERTS].bitcast(F32), ALU.subtract)\
                            .then_inc(s["router_split"], 1)
                    if c == 3:
                        dve.wait_ge(s["qk_squared"], 4 * l + 2)
                        nc.vector.tensor_reduce(ss_q[:, 0:16], work[:, 0:1024].rearrange("p (h d) -> p h d", d=HEAD),
                                                AX_X, ALU.add).then_inc(s["qk_sum"], 1)
                    if c == 4:
                        scale_a()
                    if c == 6:
                        dve.wait_ge(s["gelu_done"], 2 * (l + 1))
                        m4 = mean_b.rearrange("p (t g) -> p t g", t=TILES)
                        link("b_chain", nc.vector.tensor_reduce(m4, bv, AX_X, ALU.add))
                        link("b_chain", nc.vector.tensor_scalar(mean_b, mean_b, 1.0 / HEAD, None, ALU.mult))
                        link("b_chain", nc.vector.tensor_tensor(bv, bv, m4.unsqueeze(3).broadcast_to([P, TILES, BG, HEAD]),
                                                                ALU.subtract))
                        b4 = bsq.rearrange("p (t g d) -> p t g d", t=TILES, d=HEAD)
                        link("b_chain", nc.vector.tensor_tensor(b4, bv, bv, ALU.mult))
                        nc.vector.tensor_reduce(var_b, bsq.rearrange("p (g d) -> p g d", d=HEAD), AX_X, ALU.add)\
                            .then_inc(s["b_var"], 1)
                    if c == 7:
                        dve.wait_ge(s["b_rs"], l + 1)
                        dve.wait_ge(s["param_loaded"], 7 * LANDING * (l + 1))
                        r4 = rs_b.rearrange("p (t g) -> p t g", t=TILES)
                        link("b_chain", nc.vector.tensor_tensor(bv, bv, r4.unsqueeze(3).broadcast_to([P, TILES, BG, HEAD]),
                                                                ALU.mult))
                        flat = proj[:, :, COL_BV:COL_CQ]
                        link("b_chain", nc.vector.tensor_tensor(flat, flat, lng[:, :].unsqueeze(1).broadcast_to([P, TILES, 256]),
                                                                ALU.mult))
                        nc.vector.tensor_tensor(flat, flat, lnb[:, :].unsqueeze(1).broadcast_to([P, TILES, 256]), ALU.add)\
                            .then_inc(s["b_normed"], 1)
                dve.wait_ge(s["qk_squared"], 4 * l + 4)
                nc.vector.tensor_reduce(ss_q[:, 16:40], work[:, 1024:2560].rearrange("p (h d) -> p h d", d=HEAD),
                                        AX_X, ALU.add).then_inc(s["qk_sum"], 1)

                def qk_copy(bank, g):
                    dve.wait_ge(s["qk_turned"], 10 * l + 2 * bank + 2)
                    for a in range(2):
                        i = nc.vector.tensor_scalar(qkT[:, 2 * bank + a, :], ps[:, bank, 256 * a:256 * a + 256],
                                                    qkg[:, g + a:g + a + 1], None, ALU.mult)
                    i.then_inc(s["qkT_d"], 1)

                dve.wait_ge(s["qkg_scaled"], l + 1)
                qk_copy(1, 0)
                scale_c()
                qk_copy(3, 2)

                def score_a(h):
                    dve.wait_ge(s["scored"], 12 * l + h + 1)
                    slope = 2.0 ** (-8.0 * (h + 1) / AQ)
                    link("max_chain", nc.vector.scalar_tensor_tensor(S[:, h, :], dist[:, :], -slope, ps[:, h % 4, 0:SCORES],
                                                                     ALU.mult, ALU.add))
                    nc.vector.tensor_reduce(mx[:, h, 0:1], S[:, h, 0:P], AX_X, ALU.max)
                    nc.vector.tensor_reduce(mx[:, h, 1:2], S[:, h, P:SCORES], AX_X, ALU.max).then_inc(s["score_in"], 1)

                def score_c(h):
                    n = AQ + h
                    dve.wait_ge(s["scored"], 12 * l + n + 1)
                    dve.wait_ge(s["p_turned"], 12 * l + h + 1)
                    for t, (lo, hi) in enumerate(((0, P), (P, SCORES))):
                        i = nc.vector.tensor_tensor_reduce(S[:, h, lo:hi], ps[:, n % 4, lo:hi], relb[:, h, lo:hi], 1.0, -3e38,
                                                           ALU.add, ALU.max, mx[:, n, t:t + 1])
                    i.then_inc(s["score_in"], 1)

                def pt_copy(n):
                    dve.wait_ge(s["p_turned"], 12 * l + n + 1)
                    if n >= 2:
                        dve.wait_ge(s["pv_done"], 12 * l + n - 1)
                    nc.vector.tensor_copy(PT[:, n % 2, :], ps[:, 4 + n % 2, 0:SCORES]).then_inc(s["PT_d"], 1)

                def weigh(n0, col, order):
                    dve.wait_ge(s["pv_done"], 12 * l + n0 + 6)
                    for t in range(TILES):
                        v = proj[:, t, col:col + 384].rearrange("p (h d) -> p h d", d=HEAD)
                        r = total[:, n0:n0 + 6, t:t + 1].broadcast_to([P, 6, HEAD])
                        nc.vector.tensor_tensor(v, ps[:, 6 + t, 0:384].rearrange("p (h d) -> p h d", d=HEAD), r, ALU.mult)\
                            .then_inc(s["o_ready"], 1)

                for h in range(AQ):
                    score_a(h)
                dve.wait_ge(s["score_in"], 12 * l + AQ)
                sinks2 = sink.unsqueeze(2).broadcast_to([P, AQ, TILES])
                link("max_chain", nc.vector.tensor_tensor(mx[:, 0:AQ, :], mx[:, 0:AQ, :], sinks2, ALU.max))
                link("max_chain", nc.vector.tensor_scalar(nm[:, 0:AQ, :], mx[:, 0:AQ, :], -1.0, None, ALU.mult))
                nc.vector.tensor_tensor(esink, sinks2, nm[:, 0:AQ, :], ALU.add).then_inc(s["nm_ready"], 1)
                dve.wait_ge(s["b_psum"], l + 1)
                for g in range(BG):
                    u = proj[:, :, COL_BU + g * HEAD:COL_BU + (g + 1) * HEAD]
                    nc.vector.scalar_tensor_tensor(u, ps[:, 5, :].rearrange("p (t c) -> p t c", t=TILES)[:, :, g * HEAD:(g + 1) * HEAD],
                                                   bs[:, g:g + 1], u, ALU.add, ALU.mult).then_inc(s["b_out"], 1)
                dve.wait_ge(s["masked"], 3 * (l + 1))
                for h in range(CH):
                    score_c(h)
                    if h in (1, 3):
                        pt_copy(h)
                dve.wait_ge(s["score_in"], 12 * (l + 1))
                nc.vector.tensor_scalar(nm[:, AQ:, :], mx[:, AQ:, :], -1.0, None, ALU.mult).then_inc(s["nm_ready"], 1)
                pt_copy(5)
                dve.wait_ge(s["esink_ready"], l + 1)
                link("den_chain", nc.vector.tensor_tensor(total[:, 0:AQ, :], total[:, 0:AQ, :], esink, ALU.add))
                link("den_chain", nc.vector.reciprocal(total[:, 0:AQ, :], total[:, 0:AQ, :]))
                weigh(0, COL_AQ, 0)
                for n in (7, 9, 11):
                    pt_copy(n)
                dve.wait_ge(s["p_ready"], 12 * (l + 1))
                link("den_chain", nc.vector.reciprocal(total[:, AQ:, :], total[:, AQ:, :]))
                weigh(AQ, COL_CQ, 1)
                dve.wait_ge(s["group_rs"], l + 1)
                dve.wait_ge(s["gain_loaded"], LANDING * (3 * l + 2))
                for t in range(TILES):
                    for g, (to, col, width) in enumerate(OUT_GROUPS):
                        i = nc.vector.scalar_tensor_tensor(hn[:, t, to:to + width], proj[:, t, col:col + width],
                                                           rs_g[:, 3 * t + g:3 * t + g + 1], gain[:, to:to + width],
                                                           ALU.mult, ALU.mult)
                    i.then_inc(s["hn_ready"], 1)
                for t in range(TILES):
                    turn_low(6 * l + 2 + t)
                for c in range(OUT_SLOTS):
                    low_to(after + c + SPLIT)
                    for t in range(TILES):
                        dve.wait_ge(s["tile0_done" if t == 0 else "slot_used"], after + c + 1)
                        v = xr[:, t, c * NARROW:(c + 1) * NARROW]
                        nc.vector.tensor_tensor(v, v, ps[:, 4 + 2 * (c % 2) + t, 0:NARROW], ALU.add)\
                            .then_inc(s["x_updated"], 1)
                normed_rows(2 * l + 1, 6 * l + 4, 3 * l + 3)
                for t in range(TILES):
                    turn_low(6 * l + 4 + t)
                if l == 0:
                    def ff_mul(c):
                        up = ff_slots(c)[1]
                        for t in range(TILES):
                            dve.wait_ge(s["tile0_done" if t == 0 else "slot_used"], up + 1)
                            dve.wait_ge(s["ff_silu"], 2 * c + t + 1)
                            if c > 0:
                                dve.wait_ge(s["ff_turned"], 2 * (c - 1) + t + 1)
                            nc.vector.tensor_tensor(acted[:, 256 * t:256 * t + 256], silu[:, 256 * t:256 * t + 256],
                                                    ps[:, t, NARROW:2 * NARROW], ALU.mult).then_inc(s["ff_acted"], 1)

                    def ff_low(c):
                        for t in range(TILES):
                            dve.wait_ge(s["ff_high"], 2 * c + t + 1)
                            nc.vector.tensor_tensor(part_l[:, 256 * t:256 * t + 256], ps[:, 6 + t, 0:256],
                                                    part_h[:, 256 * t:256 * t + 256].bitcast(F32), ALU.subtract)\
                                .then_inc(s["ff_ready"], 1)

                    for c in range(FF_CHUNKS):
                        low_to(ff_slots(c)[1] + SPLIT)
                        ff_mul(c)
                        if c + 1 < FF_CHUNKS:
                            low_to(ff_slots(c + 1)[0] + SPLIT)
                        else:
                            low_to(ff_slots(c)[1] + 4)
                        ff_low(c)
                    for t in range(TILES):
                        dve.wait_ge(s["tile0_done" if t == 0 else "slot_used"], BASE_FF + FF_SLOTS)
                        for q in range(2):
                            v = xr[:, t, 512 * q:512 * q + 512]
                            nc.vector.tensor_tensor(v, v, ps[:, 2 + 2 * t + q, :], ALU.add).then_inc(s["x_updated"], 1)

            for t in range(TILES):
                dve.wait_ge(s["rows_high"], t + 1)
                nc.vector.tensor_tensor(rows_l[:, t, :], hn[:, t, :], rows_h[:, t, :].bitcast(F32), ALU.subtract)\
                    .then_inc(s["rows_ready"], 1)

            r = lambda ins: link("route_chain", ins)
            dve.wait_ge(s["logits_psum"], 1)
            r(nc.vector.tensor_copy(logits, ps[:, 7, 256:272].rearrange("p (t e) -> p t e", t=TILES)))
            nc.vector.max(best[:, 0, :], logits[:, 0, :])
            r(nc.vector.max(best[:, 1, :], logits[:, 1, :]))
            nc.vector.max_index(best_index[:, 0, :], best[:, 0, :], logits[:, 0, :])
            r(nc.vector.max_index(best_index[:, 1, :], best[:, 1, :], logits[:, 1, :]))
            r(nc.vector.tensor_tensor(margin, best[:, :, 1], best[:, :, 0], ALU.subtract))
            assert chains["route_chain"] == MARGIN_AT
            r(nc.vector.tensor_copy(best_at, best_index[:, :, 0:2]))
            for t in range(TILES):
                for k, hit in enumerate((first, second)):
                    i = nc.vector.tensor_scalar(hit[:, t, :], count_up[:, 0:EXPERTS], best_at[:, t, k:k + 1], None, ALU.is_equal)
            r(i)
            nc.vector.tensor_tensor(chosen, first, second, ALU.add).then_inc(s["chosen_ready"], 1)
            dve.wait_ge(s["emargin_ready"], 1)
            r(nc.vector.tensor_scalar(gate1, emargin, 1.0, None, ALU.add))
            r(nc.vector.reciprocal(gate1, gate1))
            dve.wait_ge(s["ranks_psum"], 1)
            nc.vector.tensor_copy(ranks, ps[:, 7, 64:88]).then_inc(s["ranks_read"], 1)
            rank = ranks[:, 0:16].rearrange("p (t e) -> p t e", t=TILES)
            dve.wait_ge(s["ranks_read"], 1)
            r(nc.vector.scalar_tensor_tensor(item_rank[:, :, 0:EXPERTS], rank, 1.0, chosen, ALU.add, ALU.mult))
            r(nc.vector.tensor_scalar(item_rank[:, :, 0:EXPERTS], item_rank[:, :, 0:EXPERTS], -1.0, None, ALU.add))

            def make_hot(i):
                for t in range(TILES):
                    col = item_rank[:, t, 0:1] if isinstance(i, int) else item_rank[:, t, bass.ds(i, 1)]
                    h = nc.vector.tensor_scalar(hot[:, t, :], count_up[:, :], col, None, ALU.is_equal)
                h.then_inc(s["hot_ready"], 1)

            make_hot(0)
            r(nc.vector.tensor_tensor(gate2, gate1, emargin, ALU.mult))
            for t in range(TILES):
                i = nc.vector.tensor_scalar(first[:, t, :], first[:, t, :], gate1[:, t:t + 1], None, ALU.mult)
            r(i)
            for t in range(TILES):
                i = nc.vector.scalar_tensor_tensor(item_gate[:, t, 0:EXPERTS], second[:, t, :], gate2[:, t:t + 1],
                                                   first[:, t, :], ALU.mult, ALU.add)
            i.then_inc(s["item_tables"], 1)

            def item_low(i):
                for q in range(2):
                    dve.wait_ge(s["m_item_high"], i * 2 + (q + 1))
                    nc.vector.tensor_tensor(item_l[:, 4 * q:4 * q + 4, :], ps[:, 2 + q, :].rearrange("p (k n) -> p k n", k=4),
                                            item_h[:, 4 * q:4 * q + 4, :].bitcast(F32), ALU.subtract)\
                        .then_inc(s["m_item_ready"], 1)

            item_low(0)
            low_to(BASE_MOE + SPLIT - 1)
            dve.wait_ge(s["slot_used"], BASE_MOE)
            dve.wait_ge(s["m_silu"], 1)
            nc.vector.tensor_tensor(acted, silu, ps[:, 1, :], ALU.mult).then_inc(s["m_acted"], 1)

            def item_body(i, last=False):
                used = lambda m: i * ITEM_SLOTS + (BASE_MOE + m + 1)

                def low_item(m):
                    j = BASE_MOE + m
                    dve.wait_ge(s["high_ready"], i * ITEM_SLOTS + (j + 1))
                    nc.vector.tensor_tensor(low[:, split_place(j), :], raw[:, raw_place(j), :],
                                            high[:, split_place(j), :].bitcast(F32), ALU.subtract)\
                        .then_inc(s["slot_split"], 1)

                def mul_of(k):
                    dve.wait_ge(s["slot_used"], used(step_slots(k)[1][1]))
                    dve.wait_ge(s["m_silu"], i * EX_CHUNKS + (k + 1))
                    dve.wait_ge(s["m_turned"], i * EX_CHUNKS + k)
                    nc.vector.tensor_tensor(acted, silu, ps[:, 2 * (k % EX_CHUNKS % 2) + 1, :], ALU.mult)\
                        .then_inc(s["m_acted"], 1)

                def part_low(k):
                    dve.wait_ge(s["m_part_high"], i * EX_CHUNKS + k)
                    nc.vector.tensor_tensor(part_l[:, :], ps[:, 6, :], part_h[:, :].bitcast(F32), ALU.subtract)\
                        .then_inc(s["m_part_ready"], 1)

                def result_low():
                    for q in range(2):
                        dve.wait_ge(s["m_res_high"], i * 2 + (q + 1))
                        nc.vector.tensor_tensor(res_l[:, 512 * q:512 * q + 512], ps[:, 4 + q, :],
                                                res_h[:, 512 * q:512 * q + 512].bitcast(F32), ALU.subtract)\
                            .then_inc(s["m_res_ready"], 1)

                def add_result():
                    for n, (q, t) in enumerate(((0, 0), (0, 1), (1, 0), (1, 1))):
                        dve.wait_ge(s["m_scattered"], i * 4 + (n + 1))
                        v = xr[:, t, 512 * q:512 * q + 512]
                        nc.vector.scalar_tensor_tensor(v, ps[:, SCATTER_BANKS[n], :], item_gate[:, t, bass.ds(i, 1)], v,
                                                       ALU.mult, ALU.add).then_inc(s["m_added"], 1)

                slots = CLOSE_SLOTS if last else ITEM_SLOTS + SPLIT
                for m in range(SPLIT, slots):
                    if not last and m == step_slots(EX_CHUNKS)[2][1] + SPLIT:
                        result_low()
                    if m == step_slots(EX_CHUNKS)[1][1] + SPLIT:
                        mul_of(EX_CHUNKS)
                    low_item(m)
                    for k in range(1, EX_CHUNKS + 1):
                        if m == 6 * (k - 1) + 1 + SPLIT and not (last and k == EX_CHUNKS):
                            part_low(k)
                    if m == step_slots(4)[0][1] + SPLIT and not last:
                        dve.wait_ge(s["m_hotT_psum"], i + 1)
                        make_hot(i + 1)
                    if m == step_slots(6)[1][1] + SPLIT and not last:
                        item_low(i + 1)
                    for k in range(1, EX_CHUNKS):
                        if m == step_slots(k)[1][1] + SPLIT:
                            mul_of(k)
                    if m == ITEM_SLOTS + 1:
                        add_result()
                if last:
                    part_low(EX_CHUNKS)
                    result_low()
                    add_result()

            with dve.Fori(0, EXPERTS - 1) as i:
                item_body(i)
            dve.wait_ge(s["plan_ready"], 1)
            extra = dve.value_load(plan[0:1, 0:1], min_val=0, max_val=MAX_OVER)
            with dve.If(extra > 0):
                with dve.Fori(0, extra) as v:
                    item_body(v + (EXPERTS - 1))
            item_body(extra + (EXPERTS - 1), last=True)

        @block.tensor
        def _(pe):
            eight = lambda t_, j: t_[:, split_place(j), :].rearrange("p (k n) -> p k n", k=KD)
            four = lambda t_, j: t_[:, split_place(j), :].rearrange("p (k n) -> p k n", k=4)
            two = lambda t_, j: t_[:, split_place(j), :].rearrange("p (k n) -> p k n", k=2)

            def three(out_, xh, xl, wh, wl, start, stop):
                nc.tensor.matmul(out_, xh, wh, start=start, stop=False)
                nc.tensor.matmul(out_, xh, wl, start=False, stop=False)
                return nc.tensor.matmul(out_, xl, wh, start=False, stop=stop)

            def turn(u):
                pe.wait_ge(s["hn_ready"], u + 1)
                for q in range(2):
                    for k in range(4):
                        c = (4 * q + k) * P
                        m = nc.tensor.transpose(ps[:, (u % 2) * 2 + q, k * P:(k + 1) * P], hn[:, u % TILES, c:c + P], ident[:, :])
                    m.then_inc(s["turned"], 1)

            def project(j, places, free=None, counts=None):
                for t in range(TILES):
                    if counts:
                        pe.wait_ge(s[free], counts[t])
                    for k in range(KD):
                        rows = slice(t * P, (t + 1) * P)
                        m = three(places[t], th[:, k, rows], tl[:, k, rows], eight(high, j)[:, k, :], eight(low, j)[:, k, :],
                                  k == 0, k == KD - 1)
                    m.then_inc(s["tile0_done" if t == 0 else "slot_used"], 1)

            pe.wait_ge(s["const_made"], 13)
            for l in range(LAYERS):
                base, after = BASE_IN[l], BASE_OUT[l]
                for t in range(TILES):
                    turn(6 * l + t)
                pe.wait_ge(s["turned_ready"], 4 * (3 * l) + 4)
                with pe.Fori(0, IN_SLOTS // SPLIT) as trip:
                    for c in range(SPLIT):
                        pe.wait_ge(s["slot_split"], trip * SPLIT + (base + c + 1))
                        pe.wait_ge(s["evac_a"], trip * SPLIT + (IN_SLOTS * l + c + 1))
                        pe.wait_ge(s["evac_d"], trip * SPLIT + (IN_SLOTS * l + c + 1))
                        project(base + c, [ps[:, 2 * c + t, 0:NARROW] for t in range(TILES)])
                pe.wait_ge(s["evac_a"], SPLIT + IN_SLOTS * (l + 1))
                pe.wait_ge(s["evac_d"], SPLIT + IN_SLOTS * (l + 1))
                for pair in range(10):
                    pe.wait_ge(s["qk_normed"], 4 * l + (2 if pair < 4 else 4))
                    for t in range(TILES):
                        if pair < 4:
                            src = paired[:, t, pair, :, :].rearrange("p a d -> p (a d)")
                        else:
                            src = proj[:, t, COL_CQ + (pair - 4) * P:COL_CQ + (pair - 3) * P]
                        m = nc.tensor.transpose(ps[:, pair // 2, (pair % 2) * 256 + t * P:(pair % 2) * 256 + (t + 1) * P],
                                                src, ident[:, :])
                    m.then_inc(s["qk_turned"], 1)
                    if pair == 3:
                        pe.wait_ge(s["b_normed"], l + 1)
                        pe.wait_ge(s["masked"], 3 * (l + 1))
                        for t in range(TILES):
                            for g in range(BG):
                                m = nc.tensor.matmul(ps[:, 5, t * 256 + g * HEAD:t * 256 + (g + 1) * HEAD], wsT[:, g, :],
                                                     proj[:, t, COL_BV + g * HEAD:COL_BV + (g + 1) * HEAD], start=True, stop=True)
                        m.then_inc(s["b_psum"], 1)

                def score(n):
                    if n < AQ:
                        half, q, k = n // 3, n % 3, 3
                    else:
                        half, q, k = (n - AQ) % 2, 4 + (n - AQ) // 2, 7 + (n - AQ) // 2
                    pe.wait_ge(s["qkT_a"], 3 * l + (1 if n < 2 else 2 if n < AQ else 3))
                    pe.wait_ge(s["qkT_d"], 2 * l + (1 if n < 3 else 2))
                    if n >= 4:
                        pe.wait_ge(s["score_in"], 12 * l + n - 3)
                    rows = slice(half * HEAD, (half + 1) * HEAD)
                    nc.tensor.matmul(ps[:, n % 4, 0:P], qkT[rows, q, 0:P], qkT[rows, k, 0:P], start=True, stop=True)
                    nc.tensor.matmul(ps[:, n % 4, P:SCORES], qkT[rows, q, P:2 * P], qkT[rows, k, :], start=True, stop=True)\
                        .then_inc(s["scored"], 1)

                def turn_p(n):
                    pe.wait_ge(s["p_ready"], 12 * l + n + 1)
                    if n == 1:
                        pe.wait_ge(s["b_out"], 4 * (l + 1))
                    if n >= 2:
                        pe.wait_ge(s["PT_a" if n % 2 == 0 else "PT_d"], 6 * l + n // 2)
                    for b in range(3):
                        m = nc.tensor.transpose(ps[:, 4 + n % 2, b * P:(b + 1) * P], S[:, n % 6, b * P:(b + 1) * P], ident[:, :])
                    m.then_inc(s["p_turned"], 1)

                def values(n):
                    h = n if n < AQ else n - AQ
                    col = COL_AV + (h // 3) * HEAD if n < AQ else COL_CV + h * HEAD
                    if n == AQ:
                        pe.wait_ge(s["o_ready"], 4 * l + 2)
                    pe.wait_ge(s["PT_a" if n % 2 == 0 else "PT_d"], 6 * l + n // 2 + 1)
                    to = slice(h * HEAD, (h + 1) * HEAD)
                    nc.tensor.matmul(ps[:, 6, to], PT[:, n % 2, 0:P], proj[:, 0, col:col + HEAD], start=True, stop=True)
                    for b in range(2):
                        m = nc.tensor.matmul(ps[:, 7, to], PT[:, n % 2, (b + 1) * P:(b + 2) * P], proj[:, b, col:col + HEAD],
                                             start=b == 0, stop=b == 1)
                    m.then_inc(s["pv_done"], 1)

                for n in range(10):
                    score(n)
                for n in range(AQ + CH):
                    turn_p(n)
                    if n < 2:
                        score(10 + n)
                    if n >= 1:
                        values(n - 1)
                values(AQ + CH - 1)

                for t in range(TILES):
                    turn(6 * l + 2 + t)
                pe.wait_ge(s["turned_ready"], 4 * (3 * l + 1) + 4)
                for c in range(OUT_SLOTS):
                    pe.wait_ge(s["slot_split"], after + c + 1)
                    if c >= 2:
                        pe.wait_ge(s["x_updated"], 12 * l + 2 * (c - 1))
                    project(after + c, [ps[:, 4 + 2 * (c % 2) + t, 0:NARROW] for t in range(TILES)])
                for t in range(TILES):
                    turn(6 * l + 4 + t)
                pe.wait_ge(s["turned_ready"], 4 * (3 * l + 2) + 4)

                if l == 0:
                    def ff_gate(j, acted_n):
                        pe.wait_ge(s["slot_split"], j[0])
                        project(j[1], [ps[:, t, 0:NARROW] for t in range(TILES)], "ff_acted", acted_n)

                    def ff_up(j):
                        pe.wait_ge(s["slot_split"], j[0])
                        project(j[1], [ps[:, t, NARROW:2 * NARROW] for t in range(TILES)])

                    def ff_turn(acted_n, evac_n):
                        for t in range(TILES):
                            pe.wait_ge(s["ff_acted"], acted_n[t])
                            if evac_n is not None:
                                pe.wait_ge(s["ff_ready"], evac_n[t])
                            for k in range(2):
                                m = nc.tensor.transpose(ps[:, 6 + t, k * P:(k + 1) * P],
                                                        acted[:, 256 * t + k * P:256 * t + (k + 1) * P], ident[:, :])
                            m.then_inc(s["ff_turned"], 1)

                    def ff_down(j, ready_n, start, stop):
                        pe.wait_ge(s["slot_split"], j[0])
                        for t in range(TILES):
                            pe.wait_ge(s["ff_ready"], ready_n[t])
                            for q in range(2):
                                for k in range(2):
                                    rows = slice(256 * t + k * P, 256 * t + (k + 1) * P)
                                    cut = slice(512 * q, 512 * q + 512)
                                    m = three(ps[:, 2 + 2 * t + q, :], part_h[:, rows], part_l[:, rows],
                                              two(high, j[1])[:, k, cut], two(low, j[1])[:, k, cut],
                                              start and k == 0, stop and k == 1)
                            m.then_inc(s["tile0_done" if t == 0 else "slot_used"], 1)

                    g, u, _ = ff_slots(0)
                    ff_gate((g + 1, g), None)
                    ff_up((u + 1, u))
                    def ff_step(c, first):
                        const = 1
                        g, u, _ = ff_slots(const)
                        d = ff_slots(const - 1)[2]
                        away = (c - const) * 3
                        ff_gate((away + (g + 1), g), [c * 2 - 1, c * 2])
                        ff_turn([c * 2 - 1, c * 2], None if first else [(c - 1) * 2 - 1, (c - 1) * 2])
                        ff_up((away + (u + 1), u))
                        ff_down((away + (d + 1), d), [c * 2 - 1, c * 2], first, False)

                    ff_step(1, True)
                    with pe.Fori(2, FF_CHUNKS) as c:
                        ff_step(c, False)
                    last = FF_CHUNKS
                    ff_turn([2 * last - 1, 2 * last], [2 * last - 3, 2 * last - 2])
                    d = ff_slots(last - 1)[2]
                    ff_down((d + 1, d), [2 * last - 1, 2 * last], False, True)

            pe.wait_ge(s["router_split"], 1)
            pe.wait_ge(s["stack_made"], 1)
            pe.wait_ge(s["ident_r_made"], 1)
            for k in range(KD):
                nc.tensor.matmul(ps[0:2 * EXPERTS, 7, 0:TILES * P], wr_hl[:, k, :], th[:, k, :], start=k == 0, stop=False)
                m = nc.tensor.matmul(ps[0:2 * EXPERTS, 7, 0:TILES * P], wr_hl[:, k, :], tl[:, k, :], start=False, stop=k == KD - 1)
            m.then_inc(s["logitsT_psum"], 1)
            pe.wait_ge(s["logitsT_read"], 1)
            for t in range(TILES):
                m = nc.tensor.matmul(ps[:, 7, 256 + t * EXPERTS:256 + (t + 1) * EXPERTS], logitsT[:, t * P:(t + 1) * P],
                                     stack[:, :], start=True, stop=True)
            m.then_inc(s["logits_psum"], 1)
            pe.wait_ge(s["chosen_ready"], 1)
            pe.wait_ge(s["dist_made"], 6)
            nc.tensor.matmul(ps[:, 7, 64:72], before[:, :], chosen[:, 0, :], start=True, stop=True)
            nc.tensor.matmul(ps[:, 7, 72:80], before[:, :], chosen[:, 1, :], start=True, stop=False)
            nc.tensor.matmul(ps[:, 7, 72:80], ones[:, :], chosen[:, 0, :], start=False, stop=True)
            nc.tensor.matmul(ps[:, 7, 80:88], ones[:, :], chosen[:, 0, :], start=True, stop=False)
            nc.tensor.matmul(ps[:, 7, 80:88], ones[:, :], chosen[:, 1, :], start=False, stop=True).then_inc(s["ranks_psum"], 1)

            def gather(i):
                pe.wait_ge(s["hot_ready"], i + 1)
                for q in range(2):
                    for k in range(4):
                        c = slice((4 * q + k) * P, (4 * q + k + 1) * P)
                        to = ps[:, 2 + q, k * P:(k + 1) * P]
                        nc.tensor.matmul(to, rows_h[:, 0, c], hot[:, 0, :], start=True, stop=False)
                        nc.tensor.matmul(to, rows_l[:, 0, c], hot[:, 0, :], start=False, stop=False)
                        nc.tensor.matmul(to, rows_h[:, 1, c], hot[:, 1, :], start=False, stop=False)
                        m = nc.tensor.matmul(to, rows_l[:, 1, c], hot[:, 1, :], start=False, stop=True)
                    m.then_inc(s["m_item_psum"], 1)

            def turn_hot(i):
                for t in range(TILES):
                    m = nc.tensor.matmul(ps[:, 7, 256 + t * P:256 + (t + 1) * P], hot[:, t, :], ident_r[:, :], start=True, stop=True)
                m.then_inc(s["m_hotT_psum"], 1)

            def columns(slots, away, bank, halves=(0, 1)):
                for a in halves:
                    j = BASE_MOE + slots[a]
                    pe.wait_ge(s["slot_split"], away + (j + 1))
                    for k in range(4):
                        m = three(ps[:, bank, :], item_h[:, 4 * a + k, :], item_l[:, 4 * a + k, :],
                                  four(high, j)[:, k, :], four(low, j)[:, k, :], a + k == 0, a == 1 and k == 3)
                    m.then_inc(s["slot_used"], 1)

            def turn_acted(done):
                pe.wait_ge(s["m_acted"], done)
                pe.wait_ge(s["m_part_ready"], done)
                for k in range(4):
                    m = nc.tensor.transpose(ps[:, 6, k * P:(k + 1) * P], acted[:, k * P:(k + 1) * P], ident[:, :])
                m.then_inc(s["m_turned"], 1)

            def down(slots, away, done, start, stop):
                pe.wait_ge(s["m_part_ready"], done + 1)
                for a in range(2):
                    j = BASE_MOE + slots[a]
                    pe.wait_ge(s["slot_split"], away + (j + 1))
                    for k in range(2):
                        rows = slice((2 * a + k) * P, (2 * a + k + 1) * P)
                        for q in range(2):
                            cut = slice(512 * q, 512 * q + 512)
                            m = three(ps[:, 4 + q, :], part_h[:, rows], part_l[:, rows], two(high, j)[:, k, cut],
                                      two(low, j)[:, k, cut], start and a + k == 0, stop and a == 1 and k == 1)
                    m.then_inc(s["slot_used"], 1)

            pe.wait_ge(s["rows_ready"], TILES)
            gather(0)
            pe.wait_ge(s["ranks_read"], 1)
            pe.wait_ge(s["m_item_ready"], 2)
            columns((-4, -3), 0, 0)
            columns((-2, -1), 0, 1)

            def item_body(i, last=False):
                at_slot = i * ITEM_SLOTS
                first = i * EX_CHUNKS

                def step(k, away, done, start, gather_next=False):
                    gate, up, low_ = step_slots(k)
                    bank = 2 * (k % 2)
                    columns(gate, away, bank)
                    pe.wait_ge(s["m_added"], i * 4 + 1)
                    turn_acted(done)
                    columns(up, away, bank + 1)
                    if gather_next:
                        gather(i + 1)
                    down(low_, away, done, start, False)

                step(1, at_slot, first + 1, True)
                turn_hot(i)
                with pe.Fori(0, 2) as trip:
                    step(2, at_slot + trip * 12, first + trip * 2 + 2, False)
                    step(3, at_slot + trip * 12, first + trip * 2 + 3, False)
                step(6, at_slot, first + 6, False, gather_next=not last)
                gate, up, low_ = step_slots(EX_CHUNKS, last)
                if not last:
                    pe.wait_ge(s["m_item_ready"], i * 2 + 4)
                    pe.wait_ge(s["m_acted"], first + EX_CHUNKS)
                    columns(gate, at_slot, 0)
                    turn_acted(first + EX_CHUNKS)
                    columns(up, at_slot, 1, (0,))
                else:
                    turn_acted(first + EX_CHUNKS)
                down(low_, at_slot, first + EX_CHUNKS, False, True)
                if not last:
                    columns(up, at_slot, 1, (1,))
                pe.wait_ge(s["m_hotT_ready"], i + 1)
                for n, (q, t) in enumerate(((0, 0), (0, 1), (1, 0), (1, 1))):
                    if t == 0:
                        pe.wait_ge(s["m_res_ready"], i * 2 + (q + 1))
                    to = ps[:, SCATTER_BANKS[n], :]
                    cut = slice(512 * q, 512 * q + 512)
                    nc.tensor.matmul(to, hotT[:, t, :], res_h[:, cut], start=True, stop=False)
                    nc.tensor.matmul(to, hotT[:, t, :], res_l[:, cut], start=False, stop=True).then_inc(s["m_scattered"], 1)

            with pe.Fori(0, EXPERTS - 1) as i:
                item_body(i)
            pe.wait_ge(s["plan_ready"], 1)
            extra = pe.value_load(plan[0:1, 0:1], min_val=0, max_val=MAX_OVER)
            with pe.If(extra > 0):
                with pe.Fori(0, extra) as v:
                    item_body(v + (EXPERTS - 1))
            item_body(extra + (EXPERTS - 1), last=True)


def kernel(x, g_mix, w_in, qn_a, kn_a, sinks_a, ln_b_g, ln_b_b, w_s, b_s, qn_c, kn_c, rel_bias_c, g_out, w_out,
           g_ffn, w_gate_d, w_up_d, w_down_d, w_router, w_gate_e, w_up_e, w_down_e):
    import numpy as np
    import concourse.bacc as bacc
    from concourse.bass_utils import run_bass_kernel_spmd

    n = lambda a: np.ascontiguousarray(a)
    qk = np.stack([np.asarray(a) for a in (qn_a, kn_a, qn_c, kn_c)], axis=-1)
    qk = np.concatenate([qk, qk], axis=1)
    line = np.asarray(rel_bias_c)[:, :, :LAST_REL + CHUNK][:, :, ::-1]
    line = np.concatenate([line, line[:, :, -1:].repeat(CHUNK, axis=2)], axis=2)
    rel = np.stack([np.concatenate([line[:, :, LAST_REL - q:LAST_REL - q + P],
                                    line[:, :, LAST_REL - P - q:LAST_REL + P - q]], axis=2) for q in range(P)], axis=1)
    ins = {
        "x": np.asarray(x)[0], "g_mix": g_mix, "w_in": w_in, "qk_gain": qk, "sinks": sinks_a, "ln_g": ln_b_g, "ln_b": ln_b_b,
        "w_s": np.transpose(np.asarray(w_s), (0, 3, 1, 2)), "b_s": np.transpose(np.asarray(b_s), (0, 2, 1)), "rel": rel,
        "g_out": g_out, "w_out": w_out, "g_ffn": g_ffn, "w_gate_d": w_gate_d, "w_up_d": w_up_d, "w_down_d": w_down_d,
        "w_router": np.asarray(w_router)[0].reshape(KD, P, EXPERTS).transpose(1, 0, 2).reshape(P, KD * EXPERTS), "w_gate_e": w_gate_e, "w_up_e": w_up_e, "w_down_e": w_down_e,
    }
    nc = bacc.Bacc("TRN2", target_bir_lowering=False, num_devices=1)
    arrays, args = {}, {}
    for name, a in ins.items():
        arrays[f"in_{name}"] = n(a)
        args[name] = nc.dram_tensor(f"in_{name}", arrays[f"in_{name}"].shape, F32, kind="ExternalInput").ap()
    args["out"] = nc.dram_tensor("out_x", (TILES * P, D), F32, kind="ExternalOutput").ap()
    hybrid_trunk(nc, **args)
    r = run_bass_kernel_spmd(nc, [arrays], core_ids=[0])
    return r.results[0]["out_x"].reshape(1, TILES * P, D)
```

```python
from contextlib import ExitStack

import concourse.bass as bass
from concourse import mybir

F32 = mybir.dt.float32
F32R = mybir.dt.float32r
I32 = mybir.dt.int32
U32 = mybir.dt.uint32
ALU = mybir.AluOpType
ACT = mybir.ActivationFunctionType
AX_X = mybir.AxisListType.X

P = 128
TILES = 2
D = 1024
KD = D // P
CHUNK = 64
HEAD = 64
AQ, AKV, BG, CH = 6, 2, 4, 6
COL_AQ, COL_AK, COL_AV = 0, 384, 512
COL_BU, COL_BV = 640, 896
COL_CQ, COL_CK, COL_CV = 1152, 1536, 1920
IN_WIDTH = 2304
IN_BANKS = 2
HN_STEPS = 6
PIECES = 4
OUT_GROUPS = ((0, COL_AQ, 384), (384, COL_BU, 256), (640, COL_CQ, 384))
DFF = 2816
DFE = 3584
EXPERTS = 8
LAYERS = 2
EPS = 1e-6
NEG_INF = -1e30
FAR = 1e33
SCORES = 3 * P
LAST_REL = 255

SLOT = 2048
RAW = 8
EXTRA = (7, 8)
SPLIT = 3
NARROW = SLOT // KD
IN_SLOTS = IN_WIDTH // NARROW
OUT_SLOTS = D // NARROW
FF_CHUNKS = DFF // NARROW
FF_SLOTS = 3 * FF_CHUNKS
DENSE_SLOTS = LAYERS * (IN_SLOTS + OUT_SLOTS) + FF_SLOTS
BASE_IN = (0, IN_SLOTS + OUT_SLOTS + FF_SLOTS)
BASE_OUT = (IN_SLOTS, BASE_IN[1] + IN_SLOTS)
BASE_FF = IN_SLOTS + OUT_SLOTS
WIDE = 512
EX_CHUNKS = DFE // WIDE
ITEM_SLOTS = 6 * EX_CHUNKS
OPEN_SLOTS = 4
BASE_MOE = DENSE_SLOTS + OPEN_SLOTS
CLOSE_SLOTS = ITEM_SLOTS - OPEN_SLOTS
MAX_OVER = 3
ITEMS = EXPERTS + MAX_OVER
SCATTER_BANKS = (7, 6, 4, 5)
MARGIN_AT = 4
LANDING = 16

RING_SLOTS = ITEM_SLOTS - len(EXTRA)
assert RING_SLOTS % RAW == 0 and ITEM_SLOTS % SPLIT == 0
SPLIT_SHIFT = -BASE_MOE % SPLIT


def raw_place(j):
    m = j - BASE_MOE
    item, m = (divmod(m, ITEM_SLOTS) if m >= 0 else (0, m))
    if m in EXTRA:
        return RAW + EXTRA.index(m)
    return (m + item * RING_SLOTS - sum(0 <= e < m for e in EXTRA)) % RAW


def split_place(j):
    return (j + SPLIT_SHIFT) % SPLIT


def landings(j):
    return sum(raw_place(n) == raw_place(j) for n in range(j + 1))


def last_there(j):
    before = [n for n in range(j) if raw_place(n) == raw_place(j)]
    return before[-1] if before else None


def item_landings(j):
    return RING_SLOTS // RAW if raw_place(j) < RAW else 1


def ff_slots(c):
    gate = BASE_FF if c == 0 else BASE_FF + 3 * c - 1
    down = BASE_FF + (3 * c + 4 if c < FF_CHUNKS - 1 else FF_SLOTS - 1)
    return gate, gate + 1, down


def step_slots(k, last=False):
    at = 6 * (k - 1)
    if k < EX_CHUNKS:
        return (at, at + 1), (at + 2, at + 3), (at + 4, at + 5)
    if last:
        return None, None, (at, at + 1)
    return (at, at + 1), (at + 2, at + 5), (at + 3, at + 4)


def hybrid_trunk(nc, x, g_mix, w_in, qk_gain, sinks, ln_g, ln_b, w_s, b_s, rel, g_out, w_out, g_ffn,
                 w_gate_d, w_up_d, w_down_d, w_router, w_gate_e, w_up_e, w_down_e, out):
    ctx = ExitStack()
    with ctx:
        def sb(name, shape, dt=F32):
            return ctx.enter_context(nc.sbuf_tensor(name, shape, dt))

        def sem(name):
            return ctx.enter_context(nc.semaphore(name))

        ps = ctx.enter_context(nc.psum_tensor("ps", [P, 8, 512], F32))

        raw = sb("raw", [P, RAW, SLOT])
        high = sb("high", [P, SPLIT, SLOT], F32R)
        low = sb("low", [P, SPLIT, SLOT], F32R)
        xr = sb("xr", [P, TILES, D])
        hn = sb("hn", [P, TILES, D])
        gain = sb("gain", [P, D])
        turned_h = sb("turned_h", [P, TILES * D], F32R)
        turned_l = sb("turned_l", [P, TILES * D], F32R)
        th = turned_h[:, :].rearrange("p (k n) -> p k n", k=KD)
        tl = turned_l[:, :].rearrange("p (k n) -> p k n", k=KD)
        work = sb("work", [P, 20 * P])
        S = work[:, 0:6 * SCORES].rearrange("p (h n) -> p h n", h=6)
        centred = hn[:, :, 768:1024].rearrange("p t (g d) -> p t g d", d=HEAD)
        paired = hn[:, 1, :].rearrange("p (t b a d) -> p t b a d", t=TILES, b=4, a=2)
        wsT = sb("wsT", [P, BG, P])
        lng = sb("lng", [P, BG * HEAD])
        lnb = sb("lnb", [P, BG * HEAD])
        small = sb("small", [P, 320])
        taken = [0]

        def cols(n):
            taken[0] += n
            assert taken[0] <= 320
            return small[:, taken[0] - n:taken[0]]

        bs = cols(BG)
        qkg = cols(4)
        sink = cols(AQ)
        ss_x = cols(2 * LAYERS * TILES)
        ms_x = cols(2 * LAYERS * TILES)
        rs_x = cols(2 * LAYERS * TILES)
        ss_q = cols(40)
        rs_q = cols(40)
        mean_b = cols(8)
        var_b = cols(8)
        rs_b = cols(8)
        mx = cols(24).rearrange("p (n t) -> p n t", t=TILES)
        nm = cols(24).rearrange("p (n t) -> p n t", t=TILES)
        total = cols(24).rearrange("p (n t) -> p n t", t=TILES)
        esink = cols(12).rearrange("p (n t) -> p n t", t=TILES)
        ss_g = cols(6)
        rs_g = cols(6)
        halves = cols(40)
        warmth = cols(6)
        ident = sb("ident", [P, P])
        ident_r = sb("ident_r", [P, P], F32R)
        count_up = sb("count_up", [P, P])
        before = sb("before", [P, P])
        ones = sb("ones", [P, P])
        silu = work[:, 0:512]
        acted = work[:, 512:1024]
        wr = sb("wr", [P, KD * EXPERTS])
        wr_hl = sb("wr_hl", [P, KD, 2 * EXPERTS], F32R)
        logitsT = sb("logitsT", [2 * EXPERTS, TILES * P])
        stack = sb("stack", [2 * EXPERTS, EXPERTS])
        route = work[:, 2304:2560]
        used = [0]

        def rcols(n, **kw):
            used[0] += n
            assert used[0] <= 256
            a = route[:, used[0] - n:used[0]]
            return a.rearrange("p (t e) -> p t e", **kw) if kw else a

        logits = rcols(16, t=2)
        best = rcols(16, t=2)
        best_at = rcols(4, t=2)
        margin = rcols(2)
        emargin = rcols(2)
        gate1 = rcols(2)
        gate2 = rcols(2)
        first = rcols(16, t=2)
        second = rcols(16, t=2)
        chosen = rcols(16, t=2)
        ranks = rcols(24)
        over = rcols(8)
        over_at = rcols(8)
        pick = rcols(8)
        picked = rcols(16, t=2)
        spare = rcols(5)
        item_rank = rcols(2 * ITEMS, t=2)
        item_gate = rcols(2 * ITEMS, t=2)
        best_index = sb("best_index", [P, 2, 8], U32)
        plan = sb("plan", [P, 5], I32)

        with (nc.sbuf_tensor("proj", [P, TILES, IN_WIDTH], F32) as proj, nc.sbuf_tensor("qkT", [P, 10, TILES * P], F32) as qkT,
              nc.sbuf_tensor("dist", [P, SCORES], F32) as dist, nc.sbuf_tensor("relb", [P, CH, SCORES], F32) as relb):
            PT = qkT[:, 0:3, :].rearrange("p a n -> p (a n)").rearrange("p (n c) -> p n c", n=2)
        with (nc.sbuf_tensor("x2_h", [P, KD, TILES * P], F32R) as x2_h,
              nc.sbuf_tensor("x2_l", [P, KD, TILES * P], F32R) as x2_l):
            pass
        more_raw = sb("more_raw", [P, len(EXTRA), SLOT])
        part_h = sb("part_h", [P, 512], F32R)
        part_l = sb("part_l", [P, 512], F32R)
        res_h = sb("res_h", [P, D], F32R)
        res_l = sb("res_l", [P, D], F32R)
        item_h = sb("item_h", [P, KD, P], F32R)
        item_l = sb("item_l", [P, KD, P], F32R)
        item_rows = hn[:, 0, :]
        end_h = item_h[:, 0:4, :].rearrange("p k n -> p (k n)")
        end_l = item_l[:, 0:4, :].rearrange("p k n -> p (k n)")
        hot = sb("hot", [P, TILES, P], F32R)
        hotT = sb("hotT", [P, TILES, P], F32R)
        rows_h = turned_h[:, :].rearrange("p (t n) -> p t n", t=TILES)
        rows_l = turned_l[:, :].rearrange("p (t n) -> p t n", t=TILES)

        s = {}

        def sems(*names):
            for n in names:
                s[n] = sem(n)

        landed = [sem(f"landed{r}") for r in range(RAW + len(EXTRA))]

        def raw_at(j):
            r = raw_place(j)
            return raw[:, r, :] if r < RAW else more_raw[:, r - RAW, :]

        sems("high_ready", "slot_split", "slot_used", "tile0_done")
        sems("x0_loaded", "x1_loaded", "gain_loaded", "param_loaded", "router_loaded")
        sems("const_made", "const_chain", "dist_made", "masked", "ident_r_made", "router_high", "router_split", "qkg_scaled")
        sems("x_squared", "x_ms", "x_rs", "hn_ready", "turned", "turned_high", "turned_ready", "x_updated")
        sems("piece_ready", "piece_turned", "piece_high", "piece_split")
        sems("evac_a", "evac_d", "qk_squared", "qk_sum", "qk_rs", "qk_normed", "pool_chain")
        sems("gelu_done", "b_chain", "b_var", "b_rs", "b_normed", "b_psum", "b_out")
        sems("qk_turned", "qkT_a", "qkT_d", "scored", "score_in", "max_chain", "nm_ready", "p_ready", "esink_ready")
        sems("p_turned", "PT_a", "PT_d", "pv_done", "den_chain", "o_ready", "group_squared", "group_rs")
        sems("ff_silu", "ff_acted", "ff_turned", "ff_high", "ff_ready")
        sems("logitsT_psum", "logitsT_read", "logits_psum", "route_chain", "plan_chain", "item_tables", "stack_made", "emargin_ready", "chosen_ready", "ranks_psum", "ranks_read", "rows_high", "rows_ready", "plan_ready")
        sems("hot_ready", "m_hotT_psum", "m_hotT_ready", "m_rows_psum", "m_rows_copied", "m_item_psum", "m_item_high", "m_item_ready")
        sems("m_silu", "m_acted", "m_turned", "m_part_high", "m_part_ready", "m_res_high", "m_res_ready", "m_scattered", "m_added")
        sems("x_stored")

        def rms_index(l, ffn):
            return 2 * l + ffn

        block = ctx.enter_context(nc.Block())

        @block.sync
        def _(sp):
            narrow = lambda w: w.rearrange("(k p) n -> p k n", p=P)
            eight = lambda j: raw_at(j).rearrange("p (k n) -> p k n", k=KD)
            four = lambda j: raw_at(j).rearrange("p (k n) -> p k n", k=4)
            two = lambda j: raw_at(j).rearrange("p (k n) -> p k n", k=2)

            def send(j, to, src):
                if j == SPLIT:
                    sp.wait_ge(s["param_loaded"], 7 * LANDING)
                if last_there(j) is not None:
                    sp.wait_ge(s["slot_split"], last_there(j) + 1)
                sp.dma_start(to(j), src).then_inc(landed[raw_place(j)], LANDING)

            for t in range(TILES):
                sp.dma_start(xr[:, t, :], x[t * P:(t + 1) * P, :]).then_inc(s[f"x{t}_loaded"], LANDING)
            for l in range(LAYERS):
                for c in range(IN_SLOTS):
                    send(BASE_IN[l] + c, eight, narrow(w_in[l])[:, :, c * NARROW:(c + 1) * NARROW])
                for c in range(OUT_SLOTS):
                    send(BASE_OUT[l] + c, eight, narrow(w_out[l])[:, :, c * NARROW:(c + 1) * NARROW])
                if l == 0:
                    for c in range(FF_CHUNKS + 1):
                        if c < FF_CHUNKS:
                            cut = slice(c * NARROW, (c + 1) * NARROW)
                            send(ff_slots(c)[0], eight, narrow(w_gate_d[0])[:, :, cut])
                            send(ff_slots(c)[1], eight, narrow(w_up_d[0])[:, :, cut])
                        if c > 0:
                            send(ff_slots(c - 1)[2], two, narrow(w_down_d[0])[:, 2 * (c - 1):2 * c, :])

            up_view = lambda w: w[0].rearrange("e (k p) n -> e p k n", p=P)

            first_down = step_slots(1)[2][0]

            def put(m, i, to, src):
                j = BASE_MOE + m
                if m != first_down:
                    before = last_there(j + 1 if m == first_down - 1 else j)
                    if m in EXTRA:
                        sp.wait_ge(s["logitsT_psum"], 1)
                        before = j - ITEM_SLOTS
                    sp.wait_ge(s["slot_split"], i * ITEM_SLOTS + (before + 1))
                sp.dma_start(to(j), src).then_inc(landed[raw_place(j)], LANDING)

            def put_columns(m, i, w, e, c, a):
                if isinstance(e, tuple):
                    start, e = e
                    put(m, i, four, up_view(w)[start:, :, 4 * a:4 * a + 4, c * WIDE:(c + 1) * WIDE][e])
                    return
                put(m, i, four, up_view(w)[e, :, 4 * a:4 * a + 4, c * WIDE:(c + 1) * WIDE])

            def put_down(m, i, e, c, a):
                put(m, i, two, up_view(w_down_e)[e, :, 4 * c + 2 * a:4 * c + 2 * a + 2, :])

            def send_item(i, e, e_next):
                for k in range(1, EX_CHUNKS):
                    gate, up, down = step_slots(k)
                    for a in range(2):
                        put_columns(gate[a], i, w_gate_e, e, k, a)
                    for a in range(2):
                        put_columns(up[a], i, w_up_e, e, k, a)
                    for a in range(2):
                        put_down(down[a], i, e, k - 1, a)
                gate, up, down = step_slots(EX_CHUNKS, e_next is None)
                if e_next is not None:
                    for a in range(2):
                        put_columns(gate[a], i, w_gate_e, e_next, 0, a)
                    put_columns(up[0], i, w_up_e, e_next, 0, 0)
                for a in range(2):
                    put_down(down[a], i, e, EX_CHUNKS - 1, a)
                if e_next is not None:
                    put_columns(up[1], i, w_up_e, e_next, 0, 1)

            for a in range(2):
                send(DENSE_SLOTS + a, four, up_view(w_gate_e)[0, :, 4 * a:4 * a + 4, 0:WIDE])
            for a in range(2):
                send(DENSE_SLOTS + 2 + a, four, up_view(w_up_e)[0, :, 4 * a:4 * a + 4, 0:WIDE])
            with sp.Fori(0, EXPERTS - 1) as i:
                send_item(i, i, (1, i))
            sp.wait_ge(s["plan_ready"], 1)
            extra = sp.value_load(plan[0:1, 0:1], min_val=0, max_val=MAX_OVER)
            expert_of = lambda v: sp.value_load(plan[0:1, bass.ds(v + 1, 1)], min_val=0, max_val=EXPERTS - 1)
            with sp.If(extra > 0):
                with sp.Fori(0, extra) as v:
                    send_item(v + (EXPERTS - 1), expert_of(v), expert_of(v + 1))
            send_item(extra + (EXPERTS - 1), expert_of(extra), None)
            for q in range(2):
                sp.wait_ge(s["m_added"], (extra + (EXPERTS - 1)) * 4 + (2 * q + 3))
                cut = slice(512 * q, 512 * q + 512)
                sp.dma_start(out.rearrange("(t p) n -> p t n", p=P)[:, :, cut], xr[:, :, cut]).then_inc(s["x_stored"], LANDING)
            sp.wait_ge(s["x_stored"], TILES * LANDING)

        @block.gpsimd
        def _(pool):
            def load_gain(n):
                row = (g_mix, g_out, g_ffn)[n % 3][n // 3]
                pool.dma_start(gain[:, :], row.partition_broadcast(P)).then_inc(s["gain_loaded"], LANDING)

            def load_params(l):
                for to, src in ((relb[:, :, :], rel[l]), (wsT[:, :, :], w_s[l]), (bs, b_s[l]), (qkg, qk_gain[l]),
                                (lng[:, :], ln_g[l].partition_broadcast(P)), (lnb[:, :], ln_b[l].partition_broadcast(P)),
                                (sink, sinks[l].partition_broadcast(P))):
                    pool.dma_start(to, src).then_inc(s["param_loaded"], LANDING)

            def mask_params(l):
                pool.wait_ge(s["param_loaded"], 7 * LANDING * (l + 1))
                pool.wait_ge(s["x_rs"], TILES * (2 * l + 1))
                nc.gpsimd.memset(relb[0:CHUNK, :, CHUNK:P], NEG_INF).then_inc(s["masked"], 1)
                nc.gpsimd.memset(relb[0:CHUNK, :, SCORES - CHUNK:SCORES], NEG_INF).then_inc(s["masked"], 1)
                nc.gpsimd.memset(wsT[CHUNK:P, :, 0:CHUNK], 0.0).then_inc(s["masked"], 1)
                pool.wait_ge(s["masked"], 3 * (l + 1))

            load_gain(0)
            nc.gpsimd.memset(halves, -0.5).then_inc(s["const_made"], 1)
            nc.gpsimd.memset(ident[:, :], 0.0).then_inc(s["const_chain"], 1)
            pool.wait_ge(s["const_chain"], 1)
            nc.gpsimd.affine_select(out=ident[:, :], in_=ident[:, :], compare_op=ALU.not_equal, fill=1.0, base=0,
                                    pattern=[[-1, P]], channel_multiplier=1).then_inc(s["const_made"], 1)
            nc.gpsimd.iota(count_up[:, :], [[1, P]], base=0, channel_multiplier=0,
                           allow_small_or_imprecise_dtypes=True).then_inc(s["const_made"], 1)
            nc.gpsimd.iota(before[:, :], [[1, P]], base=0, channel_multiplier=-1,
                           allow_small_or_imprecise_dtypes=True).then_inc(s["const_made"], 1)
            nc.gpsimd.iota(dist[:, 0:P], [[-1, P]], base=0, channel_multiplier=1,
                           allow_small_or_imprecise_dtypes=True).then_inc(s["const_made"], 1)
            nc.gpsimd.iota(dist[:, P:SCORES], [[-1, 2 * P]], base=P, channel_multiplier=1,
                           allow_small_or_imprecise_dtypes=True).then_inc(s["const_made"], 1)
            nc.gpsimd.memset(ones[:, :], 1.0).then_inc(s["const_made"], 1)
            load_params(0)
            pool.dma_start(wr[:, :], w_router).then_inc(s["router_loaded"], LANDING)
            chain = [0]

            def power(out_, ms, done):
                pool.wait_ge(s["pool_chain"], chain[0])
                nc.gpsimd.tensor_tensor(out_, ms, halves[:, 0:out_.shape[1]], ALU.pow).then_inc(s[done], 1)

            def mean_eps(to, sums, scale):
                nc.gpsimd.tensor_scalar(to, sums, scale, EPS, ALU.mult, ALU.add).then_inc(s["pool_chain"], 1)
                chain[0] += 1

            def rms_rows(n):
                for t in range(TILES):
                    c = slice(TILES * n + t, TILES * n + t + 1)
                    pool.wait_ge(s["x_squared"], TILES * n + t + 1)
                    mean_eps(ms_x[:, c], ss_x[:, c], 1.0 / D)
                    power(rs_x[:, c], ms_x[:, c], "x_rs")

            def next_gain(n):
                if n % 3:
                    pool.wait_ge(s["hn_ready"], HN_STEPS * (n // 3) + (2 if n % 3 == 1 else HN_STEPS))
                else:
                    pool.wait_ge(s["piece_ready"], PIECES * (n // 3))
                load_gain(n)

            for l in range(LAYERS):
                rms_rows(2 * l)
                mask_params(l)
                next_gain(3 * l + 1)
                for part, lo, n in (("a", 0, 16), ("c queries", 16, 12), ("c keys", 28, 12), ("b", 0, 8)):
                    if part == "b":
                        pool.wait_ge(s["b_var"], l + 1)
                        mean_eps(var_b, var_b, 1.0 / HEAD)
                        power(rs_b, var_b, "b_rs")
                    else:
                        pool.wait_ge(s["qk_sum"], 3 * l + ("a", "c queries", "c keys").index(part) + 1)
                        mean_eps(ss_q[:, lo:lo + n], ss_q[:, lo:lo + n], 1.0 / HEAD)
                        power(rs_q[:, lo:lo + n], ss_q[:, lo:lo + n], "qk_rs")
                for groups in ((0, 1), (2,)):
                    pool.wait_ge(s["group_squared"], 6 * l + TILES * (groups[-1] + 1))
                    for g in groups:
                        cut = slice(TILES * g, TILES * (g + 1))
                        mean_eps(ss_g[:, cut], ss_g[:, cut], 1.0 / OUT_GROUPS[g][2])
                    cut = slice(TILES * groups[0], TILES * (groups[-1] + 1))
                    power(rs_g[:, cut], ss_g[:, cut], "group_rs")
                next_gain(3 * l + 2)
                if l + 1 < LAYERS:
                    load_params(l + 1)
                rms_rows(2 * l + 1)
                if l + 1 < LAYERS:
                    next_gain(3 * l + 3)

            links = [0]

            def r(ins):
                links[0] += 1
                ins.then_inc(s["plan_chain"], 1)
                pool.wait_ge(s["plan_chain"], links[0])

            def sum_experts(to, v):
                for n in (4, 2):
                    r(nc.gpsimd.tensor_tensor(v[:, :, 0:n], v[:, :, 0:n], v[:, :, n:2 * n], ALU.add))
                r(nc.gpsimd.tensor_tensor(to, v[:, :, 0], v[:, :, 1], ALU.add))

            pool.wait_ge(s["item_tables"], 1)
            r(nc.gpsimd.tensor_scalar(over, ranks[:, 16:24], float(P), None, ALU.is_gt))
            r(nc.gpsimd.memset(over_at[:, 0:1], 0.0))
            for e in range(1, EXPERTS):
                r(nc.gpsimd.tensor_tensor(over_at[:, e:e + 1], over_at[:, e - 1:e], over[:, e - 1:e], ALU.add))
            r(nc.gpsimd.tensor_tensor(spare[:, 0:1], over_at[:, EXPERTS - 1:], over[:, EXPERTS - 1:], ALU.add))
            r(nc.gpsimd.memset(spare[:, 1:2], float(EXPERTS - 1)))
            for v in range(MAX_OVER):
                r(nc.gpsimd.tensor_scalar(pick, over_at, float(v), None, ALU.is_equal))
                r(nc.gpsimd.tensor_tensor(pick, pick, over, ALU.mult))
                both = pick.unsqueeze(1).broadcast_to([P, TILES, EXPERTS])
                for table, less in ((item_rank, float(P)), (item_gate, 0.0)):
                    r(nc.gpsimd.tensor_tensor(picked, table[:, :, 0:EXPERTS], both, ALU.mult))
                    col = table[:, :, EXPERTS + v]
                    sum_experts(col, picked)
                    if less:
                        r(nc.gpsimd.tensor_scalar(col, col, -less, None, ALU.add))
                r(nc.gpsimd.tensor_tensor(picked[:, 0, :], pick, count_up[:, 0:EXPERTS], ALU.mult))
                sum_experts(spare[:, 2 + v:3 + v], picked[:, 0:1, :])
            nc.gpsimd.tensor_copy(plan[:, :], spare).then_inc(s["plan_ready"], 1)

        @block.scalar
        def _(act):
            at = [0]

            def high_to(m):
                for j in range(at[0], m + 1):
                    act.wait_ge(landed[raw_place(j)], LANDING * landings(j))
                    if j >= SPLIT:
                        act.wait_ge(s["slot_used"], j - SPLIT + 1)
                    nc.scalar.activation(high[:, split_place(j), :], raw_at(j), ACT.Copy)\
                        .then_inc(s["high_ready"], 1)
                at[0] = max(at[0], m + 1)

            def square_rows(n, need, tiles=range(TILES)):
                for t in tiles:
                    need(t)
                    c = TILES * n + t
                    nc.scalar.activation(work[:, t * D:(t + 1) * D], xr[:, t, :], ACT.Square,
                                         accum_out=ss_x[:, c:c + 1]).then_inc(s["x_squared"], 1)

            def turn_high(u, parts):
                t = u % TILES
                for q, n in parts:
                    act.wait_ge(s["turned"], n + 1)
                    bank = (u % 2) * 2 + q
                    nc.scalar.activation(th[:, 4 * q:4 * q + 4, t * P:(t + 1) * P],
                                         ps[:, bank, :].rearrange("p (k n) -> p k n", k=4), ACT.Copy)\
                        .then_inc(s["turned_high"], 1)

            act.sem_inc(s["evac_a"], IN_BANKS)
            warmed = [0]

            def warm(function):
                nc.scalar.activation(warmth[:, warmed[0]:warmed[0] + 1], halves[:, 0:1], function)
                warmed[0] += 1

            square_rows(0, lambda t: act.wait_ge(s[f"x{t}_loaded"], LANDING))
            act.wait_ge(s["const_made"], 7)
            nc.scalar.activation(ident_r[:, :], ident[:, :], ACT.Copy).then_inc(s["ident_r_made"], 1)

            for l in range(LAYERS):
                base, after = BASE_IN[l], BASE_OUT[l]
                for t in range(TILES):
                    if l > 0:
                        square_rows(2 * l, lambda t: act.wait_ge(s["x_updated"], 2 * OUT_SLOTS + 2 * (t + 1)), (t,))
                    turn_high(t, [(q, 8 * l + 2 * t + q) for q in range(2)])
                high_to(base + SPLIT - 1)
                def exps(n):
                    for t, (lo, hi) in enumerate(((0, P), (P, SCORES))):
                        e = nc.scalar.activation(S[:, n % 6, lo:hi], S[:, n % 6, lo:hi], ACT.Exp,
                                                 bias=nm[:, n, t:t + 1], accum_out=total[:, n, t:t + 1])
                    e.then_inc(s["p_ready"], 1)

                def qk_copy(bank, pair, g, turned):
                    act.wait_ge(s["qk_turned"], 10 * l + turned)
                    nc.scalar.activation(qkT[:, pair:pair + 2, :], ps[:, bank, :].rearrange("p (a n) -> p a n", a=2),
                                         ACT.Copy, scale=qkg[:, g:g + 1]).then_inc(s["qkT_a"], 1)

                def pt_copy(n):
                    act.wait_ge(s["p_turned"], 12 * l + n + 1)
                    if n >= 2:
                        act.wait_ge(s["pv_done"], 12 * l + n - 1)
                    nc.scalar.activation(PT[:, n % 2, :], ps[:, 4 + n % 2, 0:SCORES], ACT.Copy).then_inc(s["PT_a"], 1)

                def both_in(c):
                    act.wait_ge(s["evac_a"], IN_BANKS + IN_SLOTS * l + c + 1)
                    act.wait_ge(s["evac_d"], IN_BANKS + IN_SLOTS * l + c + 1)

                def square_group(g):
                    to, col, width = OUT_GROUPS[g]
                    for t in range(TILES):
                        nc.scalar.activation(hn[:, t, to:to + width], proj[:, t, col:col + width], ACT.Square,
                                             accum_out=ss_g[:, TILES * g + t:TILES * g + t + 1]).then_inc(s["group_squared"], 1)

                for c in range(IN_SLOTS):
                    act.wait_ge(s["tile0_done"], base + c + 1)
                    if c == 0:
                        act.wait_ge(s["x_rs"], 2 * TILES * l + 1)
                    nc.scalar.activation(proj[:, 0, c * NARROW:(c + 1) * NARROW], ps[:, 2 * (c % IN_BANKS), 0:NARROW], ACT.Copy,
                                         scale=rs_x[:, 2 * TILES * l:2 * TILES * l + 1])\
                        .then_inc(s["evac_a"], 1)
                    if c < IN_SLOTS - 2:
                        high_to(base + c + SPLIT)
                    if c == 1:
                        both_in(c)
                        for t in range(TILES):
                            nc.scalar.activation(hn[:, t, 0:512], proj[:, t, COL_AQ:COL_AV], ACT.Square)\
                                .then_inc(s["qk_squared"], 1)
                    if c == 2 and l == 0:
                        act.wait_ge(s["router_loaded"], LANDING)
                        nc.scalar.activation(wr_hl[:, :, 0:EXPERTS], wr[:, :].rearrange("p (k e) -> p k e", k=KD), ACT.Copy)\
                            .then_inc(s["router_high"], 1)
                    if c == 3:
                        act.wait_ge(s["qkg_scaled"], l + 1)
                        qk_copy(4, 0, 0, 2)
                    if c == 4:
                        both_in(c)
                        for t in range(TILES):
                            nc.scalar.activation(proj[:, t, COL_BU:COL_CQ], proj[:, t, COL_BU:COL_CQ], ACT.Gelu)\
                                .then_inc(s["gelu_done"], 1)
                    if c == 3:
                        warm(ACT.Gelu)
                    if c == 6:
                        warm(ACT.Exp)
                    if c in (5, 7):
                        both_in(c)
                        col = COL_CQ if c == 5 else COL_CK
                        for t in range(TILES):
                            nc.scalar.activation(hn[:, t, 0:384], proj[:, t, col:col + 384], ACT.Square)\
                                .then_inc(s["qk_squared"], 1)
                    if c == 7:
                        act.wait_ge(s["nm_ready"], 3 * l + 1)
                        for n in range(2):
                            exps(n)
                    if c == 8:
                        pt_copy(0)
                        for n in range(2, AQ):
                            exps(n)
                        nc.scalar.activation(esink, esink, ACT.Exp).then_inc(s["esink_ready"], 1)
                qk_copy(0, 4, 2, 6)
                qk_copy(2, 8, 3, 10)
                pt_copy(2)
                pt_copy(4)
                high_to(after + SPLIT - 2)
                for n in range(AQ, AQ + CH):
                    if n in (AQ, AQ + 3):
                        act.wait_ge(s["nm_ready"], 3 * l + (2 if n == AQ else 3))
                    exps(n)
                    if n >= AQ + 2 and n % 2 == 0:
                        pt_copy(n - 2)
                    if n == AQ + 4:
                        act.wait_ge(s["b_out"], 4 * (l + 1))
                        act.wait_ge(s["o_ready"], 4 * l + 2)
                        square_group(0)
                        square_group(1)
                pt_copy(10)
                first_turned = 8 * l + 4
                for t in range(TILES):
                    turn_high(6 * l + 2 + t, ((0, first_turned + t),))
                act.wait_ge(s["o_ready"], 4 * (l + 1))
                square_group(2)
                for t in range(TILES):
                    turn_high(6 * l + 2 + t, ((1, first_turned + 2 + t),))

                def piece_high(c):
                    act.wait_ge(s["piece_turned"], PIECES * l + c + 1)
                    nc.scalar.activation(x2_h[:, 2 * c:2 * c + 2, :], ps[:, c, :].rearrange("p (k n) -> p k n", k=2), ACT.Copy)\
                        .then_inc(s["piece_high"], 1)

                for c in range(OUT_SLOTS - 1):
                    high_to(after + c + SPLIT)
                    if c > 0:
                        piece_high(c - 1)
                piece_high(OUT_SLOTS - 2)
                piece_high(OUT_SLOTS - 1)
                done = (8 if l == 0 else 20)
                square_rows(2 * l + 1, lambda t: act.wait_ge(s["x_updated"], done - 1 + t))
                if l == 0:
                    warm(ACT.Silu)
                    high_to(after + OUT_SLOTS - 1 + SPLIT)
                if l == 0:
                    def ff_silu(c):
                        up = ff_slots(c)[1]
                        for t in range(TILES):
                            act.wait_ge(s["tile0_done" if t == 0 else "slot_used"], up + 1)
                            if c > 0:
                                act.wait_ge(s["ff_acted"], 2 * (c - 1) + t + 1)
                            if c == 0:
                                act.wait_ge(s["x_rs"], TILES + t + 1)
                            nc.scalar.activation(silu[:, 256 * t:256 * t + 256], ps[:, t, 0:NARROW], ACT.Silu,
                                                 scale=rs_x[:, TILES + t:TILES + t + 1])\
                                .then_inc(s["ff_silu"], 1)

                    def ff_high(c):
                        for t in range(TILES):
                            act.wait_ge(s["ff_turned"], 2 * c + t + 1)
                            if c > 0:
                                act.wait_ge(s["slot_used"], ff_slots(c - 1)[2] + 1)
                            nc.scalar.activation(part_h[:, 256 * t:256 * t + 256], ps[:, 6 + t, 0:256], ACT.Copy)\
                                .then_inc(s["ff_high"], 1)

                    for c in range(FF_CHUNKS):
                        if c > 0:
                            high_to(ff_slots(c)[0] + SPLIT)
                            ff_high(c - 1)
                        ff_silu(c)
                        high_to(ff_slots(c)[1] + SPLIT)
                    ff_high(FF_CHUNKS - 1)
                    high_to(ff_slots(FF_CHUNKS - 1)[1] + 4)

            act.wait_ge(s["logitsT_psum"], 1)
            nc.scalar.activation(logitsT[:, :], ps[0:2 * EXPERTS, 7, 0:TILES * P], ACT.Copy).then_inc(s["logitsT_read"], 1)
            for t in range(TILES):
                act.wait_ge(s["x_rs"], 3 * TILES + t + 1)
                nc.scalar.activation(rows_h[:, t, :], hn[:, t, :], ACT.Copy, scale=rs_x[:, 3 * TILES + t:3 * TILES + t + 1])\
                    .then_inc(s["rows_high"], 1)
            act.wait_ge(s["route_chain"], MARGIN_AT)
            nc.scalar.activation(emargin, margin, ACT.Exp).then_inc(s["emargin_ready"], 1)
            high_to(DENSE_SLOTS + SPLIT - 1)

            def item_high(i):
                for q in range(2):
                    act.wait_ge(s["m_item_psum"], i * 2 + (q + 1))
                    nc.scalar.activation(item_h[:, 4 * q:4 * q + 4, :], ps[:, 2 + q, :].rearrange("p (k n) -> p k n", k=4),
                                         ACT.Copy).then_inc(s["m_item_high"], 1)

            def copy_rows(i):
                for q in range(2):
                    act.wait_ge(s["m_rows_psum"], i * 2 + (q + 1))
                    nc.scalar.activation(item_rows[:, 512 * q:512 * q + 512], ps[:, 2 + q, :], ACT.Copy)\
                        .then_inc(s["m_rows_copied"], 1)

            copy_rows(0)
            item_high(0)
            high_to(DENSE_SLOTS + 1 + SPLIT)
            act.wait_ge(s["slot_used"], DENSE_SLOTS + 2)
            nc.scalar.activation(silu, ps[:, 0, :], ACT.Silu).then_inc(s["m_silu"], 1)
            high_to(BASE_MOE + SPLIT - 1)

            def item_body(i, last=False):
                used = lambda m: i * ITEM_SLOTS + (BASE_MOE + m + 1)

                def high_item(m):
                    j = BASE_MOE + m
                    act.wait_ge(landed[raw_place(j)], i * (item_landings(j) * LANDING) + LANDING * landings(j))
                    act.wait_ge(s["slot_used"], used(m - SPLIT))
                    nc.scalar.activation(high[:, split_place(j), :], raw_at(j), ACT.Copy)\
                        .then_inc(s["high_ready"], 1)

                slots = CLOSE_SLOTS if last else ITEM_SLOTS + SPLIT
                for m in range(SPLIT, slots):
                    if last and m == CLOSE_SLOTS - 1:
                        act.wait_ge(s["m_turned"], (i + 1) * EX_CHUNKS)
                        nc.scalar.activation(end_h, ps[:, 6, :], ACT.Copy).then_inc(s["m_part_high"], 1)
                    if not last and m == step_slots(EX_CHUNKS)[2][1] + SPLIT:
                        act.wait_ge(s["slot_used"], used(m - SPLIT))
                        for q in range(2):
                            nc.scalar.activation(res_h[:, 512 * q:512 * q + 512], ps[:, 4 + q, :], ACT.Copy)\
                                .then_inc(s["m_res_high"], 1)
                    high_item(m)
                    for k in range(1, EX_CHUNKS + 1):
                        if m == 6 * (k - 1) + 1 + SPLIT and not (last and k == EX_CHUNKS):
                            act.wait_ge(s["slot_used"], used(m - SPLIT))
                            act.wait_ge(s["m_acted"], i * EX_CHUNKS + k)
                            nc.scalar.activation(silu, ps[:, 2 * (k % EX_CHUNKS % 2), :], ACT.Silu).then_inc(s["m_silu"], 1)
                            act.wait_ge(s["m_turned"], i * EX_CHUNKS + k)
                            nc.scalar.activation(part_h[:, :], ps[:, 6, :], ACT.Copy).then_inc(s["m_part_high"], 1)
                    if m == step_slots(2)[0][0] + SPLIT:
                        act.wait_ge(s["m_hotT_psum"], i + 1)
                        nc.scalar.activation(hotT[:, :, :].rearrange("p t n -> p (t n)"), ps[:, 7, 256:512], ACT.Copy)\
                            .then_inc(s["m_hotT_ready"], 1)
                    if m == step_slots(6)[1][1] + SPLIT and not last:
                        copy_rows(i + 1)
                    if m == step_slots(6)[1][1] + SPLIT + 1 and not last:
                        item_high(i + 1)
                if last:
                    act.wait_ge(s["slot_used"], used(CLOSE_SLOTS - 1))
                    for q in range(2):
                        nc.scalar.activation(res_h[:, 512 * q:512 * q + 512], ps[:, 4 + q, :], ACT.Copy)\
                            .then_inc(s["m_res_high"], 1)

            with act.Fori(0, EXPERTS - 1) as i:
                item_body(i)
            act.wait_ge(s["plan_ready"], 1)
            extra = act.value_load(plan[0:1, 0:1], min_val=0, max_val=MAX_OVER)
            with act.If(extra > 0):
                with act.Fori(0, extra) as v:
                    item_body(v + (EXPERTS - 1))
            item_body(extra + (EXPERTS - 1), last=True)

        @block.vector
        def _(dve):
            at = [0]
            chains = {}

            def link(name, ins):
                chains[name] = chains.get(name, 0) + 1
                ins.then_inc(s[name], 1)
                dve.wait_ge(s[name], chains[name])

            def low_to(m):
                for j in range(at[0], m + 1):
                    dve.wait_ge(s["high_ready"], j + 1)
                    nc.vector.tensor_tensor(low[:, split_place(j), :], raw_at(j),
                                            high[:, split_place(j), :].bitcast(F32), ALU.subtract)\
                        .then_inc(s["slot_split"], 1)
                at[0] = max(at[0], m + 1)

            def weighed_rows(l, tiles=range(TILES)):
                dve.wait_ge(s["gain_loaded"], LANDING * (3 * l + 1))
                for t in tiles:
                    if l == 0:
                        dve.wait_ge(s[f"x{t}_loaded"], LANDING)
                    else:
                        dve.wait_ge(s["x_updated"], 2 * OUT_SLOTS + 2 * (t + 1))
                    nc.vector.tensor_tensor(hn[:, t, :], xr[:, t, :], gain[:, :], ALU.mult).then_inc(s["hn_ready"], 1)

            def turn_low(u, parts):
                t = u % TILES
                for q, n in parts:
                    dve.wait_ge(s["turned_high"], n + 1)
                    bank = (u % 2) * 2 + q
                    cut = (slice(None), slice(4 * q, 4 * q + 4), slice(t * P, (t + 1) * P))
                    nc.vector.tensor_tensor(tl[cut], ps[:, bank, :].rearrange("p (k n) -> p k n", k=4),
                                            th[cut].bitcast(F32), ALU.subtract).then_inc(s["turned_ready"], 1)

            dve.sem_inc(s["evac_d"], IN_BANKS)
            for name in ("m_part_ready", "m_added"):
                dve.sem_inc(s[name], 1)
            dve.wait_ge(s["const_made"], 7)
            link("dist_made", nc.vector.scalar_tensor_tensor(dist[:, :], dist[:, :], -1.0, dist[:, :], ALU.mult, ALU.max))
            for rows, lo, hi in (((0, CHUNK), CHUNK, P), ((0, CHUNK), P, P + CHUNK), ((0, CHUNK), SCORES - CHUNK, SCORES),
                                 ((CHUNK, P), P, 2 * P)):
                link("dist_made", nc.vector.memset(dist[rows[0]:rows[1], lo:hi], FAR))
            link("dist_made", nc.vector.tensor_scalar(before[:, :], before[:, :], 0.0, None, ALU.is_gt))
            nc.vector.tensor_tensor(stack[:, :], ident[0:2 * EXPERTS, 0:EXPERTS], ident[0:2 * EXPERTS, EXPERTS:2 * EXPERTS],
                                    ALU.add).then_inc(s["stack_made"], 1)

            for l in range(LAYERS):
                base, after = BASE_IN[l], BASE_OUT[l]
                if l == 0:
                    weighed_rows(l)
                for t in range(TILES):
                    turn_low(t, [(q, 8 * l + 2 * t + q) for q in range(2)])
                low_to(base + SPLIT - 1)

                def scale_a():
                    dve.wait_ge(s["qk_rs"], 3 * l + 1)
                    for t in range(TILES):
                        r = rs_q[:, 8 * t:8 * t + 8]
                        for half in range(2):
                            cut = slice(3 * half, 3 * half + 3)
                            q = proj[:, t, COL_AQ + 192 * half:COL_AQ + 192 * half + 192].rearrange("p (h d) -> p h d", d=HEAD)
                            nc.vector.tensor_tensor(paired[:, t, 0:3, half, :], q,
                                                    r[:, cut].unsqueeze(2).broadcast_to([P, 3, HEAD]), ALU.mult)
                        k = proj[:, t, COL_AK:COL_AV].rearrange("p (h d) -> p h d", d=HEAD)
                        nc.vector.tensor_tensor(paired[:, t, 3, :, :], k, r[:, AQ:].unsqueeze(2).broadcast_to([P, AKV, HEAD]),
                                                ALU.mult).then_inc(s["qk_normed"], 1)

                def scale_c(keys):
                    dve.wait_ge(s["qk_rs"], 3 * l + 2 + keys)
                    for t in range(TILES):
                        col = COL_CK if keys else COL_CQ
                        v = proj[:, t, col:col + 384].rearrange("p (h d) -> p h d", d=HEAD)
                        first = (28 if keys else 16) + CH * t
                        r = rs_q[:, first:first + CH].unsqueeze(2).broadcast_to([P, CH, HEAD])
                        nc.vector.tensor_tensor(v, v, r, ALU.mult).then_inc(s["qk_normed"], 1)

                bv = proj[:, :, COL_BV:COL_CQ].rearrange("p t (g d) -> p t g d", d=HEAD)

                def sum_squares(first, n):
                    nc.vector.tensor_reduce(ss_q[:, first:first + TILES * n].rearrange("p (t h) -> p t h", t=TILES),
                                            hn[:, :, 0:n * HEAD].rearrange("p t (h d) -> p t h d", d=HEAD),
                                            AX_X, ALU.add).then_inc(s["qk_sum"], 1)

                def qk_copy(bank, pair, g, turned):
                    dve.wait_ge(s["qk_turned"], 10 * l + turned)
                    for a in range(2):
                        i = nc.vector.tensor_scalar(qkT[:, pair + a, :], ps[:, bank, 256 * a:256 * a + 256],
                                                    qkg[:, g + a:g + a + 1], None, ALU.mult)
                    i.then_inc(s["qkT_d"], 1)

                def score_a(h):
                    dve.wait_ge(s["scored"], 12 * l + h + 1)
                    slope = 2.0 ** (-8.0 * (h + 1) / AQ)
                    link("max_chain", nc.vector.scalar_tensor_tensor(S[:, h, :], dist[:, :], -slope, ps[:, 4 + h % 4, 0:SCORES],
                                                                     ALU.mult, ALU.add))
                    nc.vector.tensor_reduce(mx[:, h, 0:1], S[:, h, 0:P], AX_X, ALU.max)
                    nc.vector.tensor_reduce(mx[:, h, 1:2], S[:, h, P:SCORES], AX_X, ALU.max).then_inc(s["score_in"], 1)

                def score_c(h):
                    n = AQ + h
                    dve.wait_ge(s["scored"], 12 * l + n + 1)
                    dve.wait_ge(s["p_turned"], 12 * l + h + 1)
                    for t, (lo, hi) in enumerate(((0, P), (P, SCORES))):
                        i = nc.vector.tensor_tensor_reduce(S[:, h, lo:hi], ps[:, h % 4, lo:hi], relb[:, h, lo:hi], 1.0, -3e38,
                                                           ALU.add, ALU.max, mx[:, n, t:t + 1])
                    i.then_inc(s["score_in"], 1)

                def minus_max(first):
                    dve.wait_ge(s["score_in"], 12 * l + first + 3)
                    nc.vector.tensor_scalar(nm[:, first:first + 3, :], mx[:, first:first + 3, :], -1.0, None, ALU.mult)\
                        .then_inc(s["nm_ready"], 1)

                def pt_copy(n):
                    dve.wait_ge(s["p_turned"], 12 * l + n + 1)
                    if n >= 2:
                        dve.wait_ge(s["pv_done"], 12 * l + n - 1)
                    nc.vector.tensor_copy(PT[:, n % 2, :], ps[:, 4 + n % 2, 0:SCORES]).then_inc(s["PT_d"], 1)

                def weigh(n0, col):
                    dve.wait_ge(s["pv_done"], 12 * l + n0 + 6)
                    for t in range(TILES):
                        v = proj[:, t, col:col + 384].rearrange("p (h d) -> p h d", d=HEAD)
                        r = total[:, n0:n0 + 6, t:t + 1].broadcast_to([P, 6, HEAD])
                        nc.vector.tensor_tensor(v, ps[:, 6 + t, 0:384].rearrange("p (h d) -> p h d", d=HEAD), r, ALU.mult)\
                            .then_inc(s["o_ready"], 1)

                def norm_groups(groups, done):
                    dve.wait_ge(s["group_rs"], 2 * l + done)
                    dve.wait_ge(s["gain_loaded"], LANDING * (3 * l + 2))
                    for t in range(TILES):
                        for g in groups:
                            to, col, width = OUT_GROUPS[g]
                            i = nc.vector.scalar_tensor_tensor(hn[:, t, to:to + width], proj[:, t, col:col + width],
                                                               rs_g[:, TILES * g + t:TILES * g + t + 1], gain[:, to:to + width],
                                                               ALU.mult, ALU.mult)
                        i.then_inc(s["hn_ready"], 1)

                for c in range(IN_SLOTS):
                    dve.wait_ge(s["slot_used"], base + c + 1)
                    if c == 0:
                        dve.wait_ge(s["x_rs"], 2 * TILES * l + 2)
                    nc.vector.tensor_scalar(proj[:, 1, c * NARROW:(c + 1) * NARROW], ps[:, 2 * (c % IN_BANKS) + 1, 0:NARROW],
                                            rs_x[:, 2 * TILES * l + 1:2 * TILES * l + 2], None, ALU.mult)\
                        .then_inc(s["evac_d"], 1)
                    if c < IN_SLOTS - 3:
                        low_to(base + c + SPLIT)
                    if c == 1:
                        dve.wait_ge(s["param_loaded"], 7 * LANDING * (l + 1))
                        nc.vector.tensor_scalar(qkg[:, 0:4:2], qkg[:, 0:4:2], HEAD ** -0.5, None, ALU.mult)\
                            .then_inc(s["qkg_scaled"], 1)
                        dve.wait_ge(s["qk_squared"], 6 * l + 2)
                        sum_squares(0, 8)
                    if c == 2:
                        scale_a()
                    if c == 3:
                        dve.wait_ge(s["qkg_scaled"], l + 1)
                        qk_copy(5, 2, 0, 4)
                        if l == 0:
                            dve.wait_ge(s["router_high"], 1)
                            nc.vector.tensor_tensor(wr_hl[:, :, EXPERTS:], wr[:, :].rearrange("p (k e) -> p k e", k=KD),
                                                    wr_hl[:, :, 0:EXPERTS].bitcast(F32), ALU.subtract)\
                                .then_inc(s["router_split"], 1)
                    if c in (4, 5, 6):
                        score_a(2 * (c - 4))
                        score_a(2 * (c - 4) + 1)
                    if c == 6:
                        dve.wait_ge(s["score_in"], 12 * l + AQ)
                        sinks2 = sink.unsqueeze(2).broadcast_to([P, AQ, TILES])
                        link("max_chain", nc.vector.tensor_tensor(mx[:, 0:AQ, :], mx[:, 0:AQ, :], sinks2, ALU.max))
                        link("max_chain", nc.vector.tensor_scalar(nm[:, 0:AQ, :], mx[:, 0:AQ, :], -1.0, None, ALU.mult))
                        nc.vector.tensor_tensor(esink, sinks2, nm[:, 0:AQ, :], ALU.add).then_inc(s["nm_ready"], 1)
                        low_to(base + c + SPLIT)
                    if c == 5:
                        dve.wait_ge(s["qk_squared"], 6 * l + 4)
                        sum_squares(16, CH)
                    if c == 7:
                        dve.wait_ge(s["qk_squared"], 6 * l + 6)
                        sum_squares(28, CH)
                        scale_c(0)
                pt_copy(1)
                scale_c(1)
                qk_copy(1, 6, 2, 8)
                dve.wait_ge(s["gelu_done"], 2 * (l + 1))
                m4 = mean_b.rearrange("p (t g) -> p t g", t=TILES)
                link("b_chain", nc.vector.tensor_reduce(m4, bv, AX_X, ALU.add))
                link("b_chain", nc.vector.tensor_scalar(mean_b, mean_b, 1.0 / HEAD, None, ALU.mult))
                link("b_chain", nc.vector.tensor_tensor(bv, bv, m4.unsqueeze(3).broadcast_to([P, TILES, BG, HEAD]),
                                                        ALU.subtract))
                link("b_chain", nc.vector.tensor_tensor(centred, bv, bv, ALU.mult))
                nc.vector.tensor_reduce(var_b.rearrange("p (t g) -> p t g", t=TILES), centred, AX_X, ALU.add)\
                    .then_inc(s["b_var"], 1)
                pt_copy(3)
                dve.wait_ge(s["masked"], 3 * (l + 1))
                score_c(0)
                score_c(1)
                pt_copy(5)
                score_c(2)
                minus_max(AQ)
                dve.wait_ge(s["b_rs"], l + 1)
                r4 = rs_b.rearrange("p (t g) -> p t g", t=TILES)
                link("b_chain", nc.vector.tensor_tensor(bv, bv, r4.unsqueeze(3).broadcast_to([P, TILES, BG, HEAD]), ALU.mult))
                flat = proj[:, :, COL_BV:COL_CQ]
                link("b_chain", nc.vector.tensor_tensor(flat, flat, lng[:, :].unsqueeze(1).broadcast_to([P, TILES, 256]),
                                                        ALU.mult))
                nc.vector.tensor_tensor(flat, flat, lnb[:, :].unsqueeze(1).broadcast_to([P, TILES, 256]), ALU.add)\
                    .then_inc(s["b_normed"], 1)
                score_c(3)
                dve.wait_ge(s["esink_ready"], l + 1)
                link("den_chain", nc.vector.tensor_tensor(total[:, 0:AQ, :], total[:, 0:AQ, :], esink, ALU.add))
                link("den_chain", nc.vector.reciprocal(total[:, 0:AQ, :], total[:, 0:AQ, :]))
                weigh(0, COL_AQ)
                score_c(4)
                score_c(5)
                minus_max(AQ + 3)
                dve.wait_ge(s["b_psum"], l + 1)
                for g in range(BG):
                    u = proj[:, :, COL_BU + g * HEAD:COL_BU + (g + 1) * HEAD]
                    nc.vector.scalar_tensor_tensor(u, ps[:, 2, :].rearrange("p (t c) -> p t c", t=TILES)[:, :, g * HEAD:(g + 1) * HEAD],
                                                   bs[:, g:g + 1], u, ALU.add, ALU.mult).then_inc(s["b_out"], 1)
                pt_copy(7)
                pt_copy(9)
                norm_groups((0, 1), 1)
                dve.wait_ge(s["p_ready"], 12 * (l + 1))
                link("den_chain", nc.vector.reciprocal(total[:, AQ:, :], total[:, AQ:, :]))
                pt_copy(11)
                first_turned = 8 * l + 4
                for t in range(TILES):
                    turn_low(6 * l + 2 + t, ((0, first_turned + t),))
                weigh(AQ, COL_CQ)
                low_to(after + SPLIT - 2)
                norm_groups((2,), 2)
                for t in range(TILES):
                    turn_low(6 * l + 2 + t, ((1, first_turned + 2 + t),))

                def piece_low(c):
                    dve.wait_ge(s["piece_high"], PIECES * l + c + 1)
                    nc.vector.tensor_tensor(x2_l[:, 2 * c:2 * c + 2, :], ps[:, c, :].rearrange("p (k n) -> p k n", k=2),
                                            x2_h[:, 2 * c:2 * c + 2, :].bitcast(F32), ALU.subtract)\
                        .then_inc(s["piece_split"], 1)

                for c in range(OUT_SLOTS):
                    cut = slice(c * NARROW, (c + 1) * NARROW)
                    for t in range(TILES):
                        dve.wait_ge(s["tile0_done" if t == 0 else "slot_used"], after + c + 1)
                        nc.vector.tensor_tensor(xr[:, t, cut], xr[:, t, cut], ps[:, 4 + 2 * (c % 2) + t, 0:NARROW], ALU.add)\
                            .then_inc(s["x_updated"], 1)
                    dve.wait_ge(s["gain_loaded"], LANDING * (3 * l + 3))
                    dve.wait_ge(s["x_updated"], 12 * l + TILES * (c + 1))
                    nc.vector.tensor_tensor(hn[:, :, cut], xr[:, :, cut], gain[:, cut].unsqueeze(1).broadcast_to([P, TILES, NARROW]),
                                            ALU.mult).then_inc(s["piece_ready"], 1)
                    if c < OUT_SLOTS - 1:
                        low_to(after + c + SPLIT)
                    if c > 0:
                        piece_low(c - 1)
                piece_low(OUT_SLOTS - 1)
                if l == 0:
                    low_to(after + OUT_SLOTS - 1 + SPLIT)
                if l == 0:
                    def ff_mul(c):
                        up = ff_slots(c)[1]
                        for t in range(TILES):
                            dve.wait_ge(s["tile0_done" if t == 0 else "slot_used"], up + 1)
                            dve.wait_ge(s["ff_silu"], 2 * c + t + 1)
                            if c > 0:
                                dve.wait_ge(s["ff_turned"], 2 * (c - 1) + t + 1)
                            nc.vector.scalar_tensor_tensor(acted[:, 256 * t:256 * t + 256], ps[:, t, NARROW:2 * NARROW],
                                                           rs_x[:, TILES + t:TILES + t + 1], silu[:, 256 * t:256 * t + 256],
                                                           ALU.mult, ALU.mult).then_inc(s["ff_acted"], 1)

                    def ff_low(c):
                        for t in range(TILES):
                            dve.wait_ge(s["ff_high"], 2 * c + t + 1)
                            nc.vector.tensor_tensor(part_l[:, 256 * t:256 * t + 256], ps[:, 6 + t, 0:256],
                                                    part_h[:, 256 * t:256 * t + 256].bitcast(F32), ALU.subtract)\
                                .then_inc(s["ff_ready"], 1)

                    for c in range(FF_CHUNKS):
                        ff_mul(c)
                        low_to(ff_slots(c)[1] + SPLIT)
                        if c + 1 < FF_CHUNKS:
                            low_to(ff_slots(c + 1)[0] + SPLIT)
                            ff_low(c)
                        else:
                            ff_low(c)
                            low_to(ff_slots(c)[1] + 4)
                    for t in range(TILES):
                        dve.wait_ge(s["tile0_done" if t == 0 else "slot_used"], BASE_FF + FF_SLOTS)
                        for q in range(2):
                            v = xr[:, t, 512 * q:512 * q + 512]
                            nc.vector.tensor_tensor(v, v, ps[:, 2 + 2 * t + q, :], ALU.add).then_inc(s["x_updated"], 1)
                        weighed_rows(1, (t,))

            r = lambda ins: link("route_chain", ins)
            dve.wait_ge(s["logits_psum"], 1)
            dve.wait_ge(s["x_rs"], 4 * TILES)
            for t in range(TILES):
                i = nc.vector.tensor_scalar(logits[:, t, :], ps[:, 7, 256 + EXPERTS * t:256 + EXPERTS * (t + 1)],
                                            rs_x[:, 3 * TILES + t:3 * TILES + t + 1], None, ALU.mult)
            r(i)
            nc.vector.max(best[:, 0, :], logits[:, 0, :])
            r(nc.vector.max(best[:, 1, :], logits[:, 1, :]))
            nc.vector.max_index(best_index[:, 0, :], best[:, 0, :], logits[:, 0, :])
            r(nc.vector.max_index(best_index[:, 1, :], best[:, 1, :], logits[:, 1, :]))
            r(nc.vector.tensor_tensor(margin, best[:, :, 1], best[:, :, 0], ALU.subtract))
            assert chains["route_chain"] == MARGIN_AT
            r(nc.vector.tensor_copy(best_at, best_index[:, :, 0:2]))
            for t in range(TILES):
                for k, hit in enumerate((first, second)):
                    i = nc.vector.tensor_scalar(hit[:, t, :], count_up[:, 0:EXPERTS], best_at[:, t, k:k + 1], None, ALU.is_equal)
            r(i)
            nc.vector.tensor_tensor(chosen, first, second, ALU.add).then_inc(s["chosen_ready"], 1)
            for t in range(TILES):
                dve.wait_ge(s["rows_high"], t + 1)
                nc.vector.scalar_tensor_tensor(rows_l[:, t, :], hn[:, t, :], rs_x[:, 3 * TILES + t:3 * TILES + t + 1],
                                               rows_h[:, t, :].bitcast(F32), ALU.mult, ALU.subtract).then_inc(s["rows_ready"], 1)
            dve.wait_ge(s["ranks_psum"], 1)
            nc.vector.tensor_copy(ranks, ps[:, 7, 64:88]).then_inc(s["ranks_read"], 1)
            rank = ranks[:, 0:16].rearrange("p (t e) -> p t e", t=TILES)
            dve.wait_ge(s["ranks_read"], 1)
            r(nc.vector.scalar_tensor_tensor(item_rank[:, :, 0:EXPERTS], rank, 1.0, chosen, ALU.add, ALU.mult))
            r(nc.vector.tensor_scalar(item_rank[:, :, 0:EXPERTS], item_rank[:, :, 0:EXPERTS], -1.0, None, ALU.add))

            def make_hot(i):
                for t in range(TILES):
                    col = item_rank[:, t, 0:1] if isinstance(i, int) else item_rank[:, t, bass.ds(i, 1)]
                    h = nc.vector.tensor_scalar(hot[:, t, :], count_up[:, :], col, None, ALU.is_equal)
                h.then_inc(s["hot_ready"], 1)

            make_hot(0)
            low_to(DENSE_SLOTS + SPLIT - 1)
            dve.wait_ge(s["emargin_ready"], 1)
            r(nc.vector.tensor_scalar(gate1, emargin, 1.0, None, ALU.add))
            r(nc.vector.reciprocal(gate1, gate1))
            r(nc.vector.tensor_tensor(gate2, gate1, emargin, ALU.mult))
            for t in range(TILES):
                i = nc.vector.tensor_scalar(first[:, t, :], first[:, t, :], gate1[:, t:t + 1], None, ALU.mult)
            r(i)
            for t in range(TILES):
                i = nc.vector.scalar_tensor_tensor(item_gate[:, t, 0:EXPERTS], second[:, t, :], gate2[:, t:t + 1],
                                                   first[:, t, :], ALU.mult, ALU.add)
            i.then_inc(s["item_tables"], 1)

            def item_low(i):
                for q in range(2):
                    dve.wait_ge(s["m_item_high"], i * 2 + (q + 1))
                    nc.vector.tensor_tensor(item_l[:, 4 * q:4 * q + 4, :], ps[:, 2 + q, :].rearrange("p (k n) -> p k n", k=4),
                                            item_h[:, 4 * q:4 * q + 4, :].bitcast(F32), ALU.subtract)\
                        .then_inc(s["m_item_ready"], 1)

            item_low(0)
            low_to(BASE_MOE + SPLIT - 1)
            dve.wait_ge(s["slot_used"], BASE_MOE)
            dve.wait_ge(s["m_silu"], 1)
            nc.vector.tensor_tensor(acted, silu, ps[:, 1, :], ALU.mult).then_inc(s["m_acted"], 1)

            def item_body(i, last=False):
                used = lambda m: i * ITEM_SLOTS + (BASE_MOE + m + 1)

                def low_item(m):
                    j = BASE_MOE + m
                    dve.wait_ge(s["high_ready"], i * ITEM_SLOTS + (j + 1))
                    nc.vector.tensor_tensor(low[:, split_place(j), :], raw_at(j),
                                            high[:, split_place(j), :].bitcast(F32), ALU.subtract)\
                        .then_inc(s["slot_split"], 1)

                def mul_of(k):
                    dve.wait_ge(s["slot_used"], used(step_slots(k)[1][1]))
                    dve.wait_ge(s["m_silu"], i * EX_CHUNKS + (k + 1))
                    dve.wait_ge(s["m_turned"], i * EX_CHUNKS + k)
                    nc.vector.tensor_tensor(acted, silu, ps[:, 2 * (k % EX_CHUNKS % 2) + 1, :], ALU.mult)\
                        .then_inc(s["m_acted"], 1)

                def part_low(k, low_=part_l[:, :], high_=part_h[:, :]):
                    dve.wait_ge(s["m_part_high"], i * EX_CHUNKS + k)
                    nc.vector.tensor_tensor(low_, ps[:, 6, :], high_.bitcast(F32), ALU.subtract)\
                        .then_inc(s["m_part_ready"], 1)

                def result_low():
                    for q in range(2):
                        dve.wait_ge(s["m_res_high"], i * 2 + (q + 1))
                        nc.vector.tensor_tensor(res_l[:, 512 * q:512 * q + 512], ps[:, 4 + q, :],
                                                res_h[:, 512 * q:512 * q + 512].bitcast(F32), ALU.subtract)\
                            .then_inc(s["m_res_ready"], 1)

                def add_result():
                    for n, (q, t) in enumerate(((0, 0), (0, 1), (1, 0), (1, 1))):
                        dve.wait_ge(s["m_scattered"], i * 4 + (n + 1))
                        v = xr[:, t, 512 * q:512 * q + 512]
                        nc.vector.scalar_tensor_tensor(v, ps[:, SCATTER_BANKS[n], :], item_gate[:, t, bass.ds(i, 1)], v,
                                                       ALU.mult, ALU.add).then_inc(s["m_added"], 1)

                slots = CLOSE_SLOTS if last else ITEM_SLOTS + SPLIT
                for m in range(SPLIT, slots):
                    if last and m == CLOSE_SLOTS - 1:
                        part_low(EX_CHUNKS, end_l, end_h)
                    if not last and m == step_slots(EX_CHUNKS)[2][1] + SPLIT:
                        result_low()
                    if m == step_slots(EX_CHUNKS)[1][1] + SPLIT:
                        mul_of(EX_CHUNKS)
                    if last and m == CLOSE_SLOTS - 2:
                        mul_of(EX_CHUNKS - 1)
                    if not last and m == step_slots(6)[1][1] + SPLIT + 1:
                        item_low(i + 1)
                    low_item(m)
                    for k in range(1, EX_CHUNKS + 1):
                        if m == 6 * (k - 1) + 1 + SPLIT and not (last and k == EX_CHUNKS):
                            part_low(k)
                    if m == step_slots(4)[0][1] + SPLIT and not last:
                        dve.wait_ge(s["m_hotT_psum"], i + 1)
                        make_hot(i + 1)
                    for k in range(1, EX_CHUNKS - 1 if last else EX_CHUNKS):
                        if m == step_slots(k)[1][1] + SPLIT:
                            mul_of(k)
                    if m == ITEM_SLOTS + 1:
                        add_result()
                if last:
                    result_low()
                    add_result()

            with dve.Fori(0, EXPERTS - 1) as i:
                item_body(i)
            dve.wait_ge(s["plan_ready"], 1)
            extra = dve.value_load(plan[0:1, 0:1], min_val=0, max_val=MAX_OVER)
            with dve.If(extra > 0):
                with dve.Fori(0, extra) as v:
                    item_body(v + (EXPERTS - 1))
            item_body(extra + (EXPERTS - 1), last=True)

        @block.tensor
        def _(pe):
            eight = lambda t_, j: t_[:, split_place(j), :].rearrange("p (k n) -> p k n", k=KD)
            four = lambda t_, j: t_[:, split_place(j), :].rearrange("p (k n) -> p k n", k=4)
            two = lambda t_, j: t_[:, split_place(j), :].rearrange("p (k n) -> p k n", k=2)

            def three(out_, xh, xl, wh, wl, start, stop):
                nc.tensor.matmul(out_, xh, wh, start=start, stop=False)
                nc.tensor.matmul(out_, xh, wl, start=False, stop=False)
                return nc.tensor.matmul(out_, xl, wh, start=False, stop=stop)

            def turn(u, ready, parts=(0, 1)):
                pe.wait_ge(s["hn_ready"], ready)
                for q in parts:
                    for k in range(4):
                        c = (4 * q + k) * P
                        m = nc.tensor.transpose(ps[:, (u % 2) * 2 + q, k * P:(k + 1) * P], hn[:, u % TILES, c:c + P],
                                                ident[:, :])
                    m.then_inc(s["turned"], 1)

            def project(j, places, free=None, counts=None, x=(th, tl), part=(0, KD)):
                for t in range(TILES):
                    if counts:
                        pe.wait_ge(s[free], counts[t])
                    for k in range(*part):
                        rows = slice(t * P, (t + 1) * P)
                        m = three(places[t], x[0][:, k, rows], x[1][:, k, rows], eight(high, j)[:, k, :], eight(low, j)[:, k, :],
                                  k == 0, k == KD - 1)
                    if part[1] == KD:
                        m.then_inc(s["tile0_done" if t == 0 else "slot_used"], 1)

            pe.wait_ge(s["const_made"], 7)
            for l in range(LAYERS):
                base, after = BASE_IN[l], BASE_OUT[l]
                for t in range(TILES):
                    turn(t, HN_STEPS * l + t + 1)
                pe.wait_ge(s["turned_ready"], 8 * l + 4)

                def turn_pairs(pairs, bank):
                    for n, pair in enumerate(pairs):
                        for t in range(TILES):
                            if pair < 4:
                                src = paired[:, t, pair, :, :].rearrange("p a d -> p (a d)")
                            else:
                                src = proj[:, t, COL_CQ + (pair - 4) * P:COL_CQ + (pair - 3) * P]
                            to = (n % 2) * 256 + t * P
                            m = nc.tensor.transpose(ps[:, bank + n // 2, to:to + P], src, ident[:, :])
                        m.then_inc(s["qk_turned"], 1)

                def score(n):
                    if n < AQ:
                        half, q, k = n // 3, n % 3, 3
                    else:
                        half, q, k = (n - AQ) % 2, 4 + (n - AQ) // 2, 7 + (n - AQ) // 2
                    pe.wait_ge(s["qkT_a"], 3 * l + (1 if n < AQ else 3))
                    pe.wait_ge(s["qkT_d"], 2 * l + (1 if n < AQ else 2))
                    h = n if n < AQ else n - AQ
                    if h >= 4:
                        pe.wait_ge(s["score_in"], 12 * l + n - 3)
                    bank = h % 4 + (4 if n < AQ else 0)
                    rows = slice(half * HEAD, (half + 1) * HEAD)
                    nc.tensor.matmul(ps[:, bank, 0:P], qkT[rows, q, 0:P], qkT[rows, k, 0:P], start=True, stop=True)
                    nc.tensor.matmul(ps[:, bank, P:SCORES], qkT[rows, q, P:2 * P], qkT[rows, k, :], start=True, stop=True)\
                        .then_inc(s["scored"], 1)

                def turn_p(n):
                    pe.wait_ge(s["p_ready"], 12 * l + n + 1)
                    if n >= 2:
                        pe.wait_ge(s["PT_a" if n % 2 == 0 else "PT_d"], 6 * l + n // 2)
                    for b in range(3):
                        m = nc.tensor.transpose(ps[:, 4 + n % 2, b * P:(b + 1) * P], S[:, n % 6, b * P:(b + 1) * P], ident[:, :])
                    m.then_inc(s["p_turned"], 1)

                def values(n):
                    h = n if n < AQ else n - AQ
                    col = COL_AV + (h // 3) * HEAD if n < AQ else COL_CV + h * HEAD
                    if n == AQ:
                        pe.wait_ge(s["o_ready"], 4 * l + 2)
                    pe.wait_ge(s["PT_a" if n % 2 == 0 else "PT_d"], 6 * l + n // 2 + 1)
                    to = slice(h * HEAD, (h + 1) * HEAD)
                    nc.tensor.matmul(ps[:, 6, to], PT[:, n % 2, 0:P], proj[:, 0, col:col + HEAD], start=True, stop=True)
                    for b in range(2):
                        m = nc.tensor.matmul(ps[:, 7, to], PT[:, n % 2, (b + 1) * P:(b + 2) * P], proj[:, b, col:col + HEAD],
                                             start=b == 0, stop=b == 1)
                    m.then_inc(s["pv_done"], 1)

                for c in range(IN_SLOTS):
                    pe.wait_ge(s["slot_split"], base + c + 1)
                    pe.wait_ge(s["evac_a"], IN_SLOTS * l + c + 1)
                    pe.wait_ge(s["evac_d"], IN_SLOTS * l + c + 1)
                    project(base + c, [ps[:, 2 * (c % IN_BANKS) + t, 0:NARROW] for t in range(TILES)])
                    if c == 3:
                        pe.wait_ge(s["qk_normed"], 6 * l + 2)
                        turn_pairs(range(0, 4), 4)
                    if c == 4:
                        for n in range(4):
                            score(n)
                    if c == 5:
                        score(4)
                        score(5)
                turn_p(0)
                turn_p(1)
                values(0)
                pe.wait_ge(s["evac_a"], IN_BANKS + IN_SLOTS * (l + 1))
                pe.wait_ge(s["evac_d"], IN_BANKS + IN_SLOTS * (l + 1))
                pe.wait_ge(s["qk_normed"], 6 * (l + 1))
                turn_pairs(range(4, 10), 0)
                turn_p(2)
                values(1)
                turn_p(3)
                values(2)
                for h in range(4):
                    score(AQ + h)
                turn_p(4)
                values(3)
                turn_p(5)
                values(4)
                values(5)
                score(AQ + 4)
                score(AQ + 5)
                pe.wait_ge(s["b_normed"], l + 1)
                pe.wait_ge(s["masked"], 3 * (l + 1))
                pe.wait_ge(s["score_in"], 12 * l + AQ + 3)
                for t in range(TILES):
                    for g in range(BG):
                        m = nc.tensor.matmul(ps[:, 2, t * 256 + g * HEAD:t * 256 + (g + 1) * HEAD], wsT[:, g, :],
                                             proj[:, t, COL_BV + g * HEAD:COL_BV + (g + 1) * HEAD], start=True, stop=True)
                m.then_inc(s["b_psum"], 1)
                for n in range(AQ, AQ + CH):
                    turn_p(n)
                    if n > AQ:
                        values(n - 1)
                    if n == AQ + CH - 1:
                        for t in range(TILES):
                            turn(6 * l + 2 + t, HN_STEPS * l + 3 + t, (0,))
                values(AQ + CH - 1)
                pe.wait_ge(s["slot_split"], after + 1)
                pe.wait_ge(s["turned_ready"], 8 * l + 6)
                out_banks = lambda c: [ps[:, 4 + 2 * (c % 2) + t, 0:NARROW] for t in range(TILES)]
                project(after, out_banks(0), part=(0, KD // 2))
                for t in range(TILES):
                    turn(6 * l + 2 + t, HN_STEPS * l + 5 + t, (1,))
                pe.wait_ge(s["turned_ready"], 8 * l + 8)

                def turn_piece(c):
                    pe.wait_ge(s["piece_ready"], PIECES * l + c + 1)
                    for k in range(2):
                        for t in range(TILES):
                            col = (2 * c + k) * P
                            to = (2 * k + t) * P
                            m = nc.tensor.transpose(ps[:, c, to:to + P], hn[:, t, col:col + P], ident[:, :])
                    m.then_inc(s["piece_turned"], 1)

                for c in range(OUT_SLOTS):
                    pe.wait_ge(s["slot_split"], after + c + 1)
                    if c >= 2:
                        pe.wait_ge(s["x_updated"], 12 * l + 2 * (c - 1))
                    project(after + c, out_banks(c), part=(KD // 2 if c == 0 else 0, KD))
                    if c > 0:
                        turn_piece(c - 1)
                turn_piece(OUT_SLOTS - 1)
                pe.wait_ge(s["piece_split"], PIECES * (l + 1))

                if l == 0:
                    def ff_gate(j, acted_n):
                        pe.wait_ge(s["slot_split"], j[0])
                        project(j[1], [ps[:, t, 0:NARROW] for t in range(TILES)], "ff_acted", acted_n, (x2_h, x2_l))

                    def ff_up(j):
                        pe.wait_ge(s["slot_split"], j[0])
                        project(j[1], [ps[:, t, NARROW:2 * NARROW] for t in range(TILES)], x=(x2_h, x2_l))

                    def ff_turn(acted_n, evac_n):
                        for t in range(TILES):
                            pe.wait_ge(s["ff_acted"], acted_n[t])
                            if evac_n is not None:
                                pe.wait_ge(s["ff_ready"], evac_n[t])
                            for k in range(2):
                                m = nc.tensor.transpose(ps[:, 6 + t, k * P:(k + 1) * P],
                                                        acted[:, 256 * t + k * P:256 * t + (k + 1) * P], ident[:, :])
                            m.then_inc(s["ff_turned"], 1)

                    def ff_down(j, ready_n, start, stop):
                        pe.wait_ge(s["slot_split"], j[0])
                        for t in range(TILES):
                            pe.wait_ge(s["ff_ready"], ready_n[t])
                            for q in range(2):
                                for k in range(2):
                                    rows = slice(256 * t + k * P, 256 * t + (k + 1) * P)
                                    cut = slice(512 * q, 512 * q + 512)
                                    m = three(ps[:, 2 + 2 * t + q, :], part_h[:, rows], part_l[:, rows],
                                              two(high, j[1])[:, k, cut], two(low, j[1])[:, k, cut],
                                              start and k == 0, stop and k == 1)
                            m.then_inc(s["tile0_done" if t == 0 else "slot_used"], 1)

                    g, u, _ = ff_slots(0)
                    ff_gate((g + 1, g), None)
                    ff_up((u + 1, u))
                    def ff_step(c, first):
                        const = 1
                        g, u, _ = ff_slots(const)
                        d = ff_slots(const - 1)[2]
                        away = (c - const) * 3
                        ff_gate((away + (g + 1), g), [c * 2 - 1, c * 2])
                        ff_turn([c * 2 - 1, c * 2], None if first else [(c - 1) * 2 - 1, (c - 1) * 2])
                        ff_up((away + (u + 1), u))
                        ff_down((away + (d + 1), d), [c * 2 - 1, c * 2], first, False)

                    ff_step(1, True)
                    with pe.Fori(2, FF_CHUNKS) as c:
                        ff_step(c, False)
                    last = FF_CHUNKS
                    ff_turn([2 * last - 1, 2 * last], [2 * last - 3, 2 * last - 2])
                    d = ff_slots(last - 1)[2]
                    ff_down((d + 1, d), [2 * last - 1, 2 * last], False, True)

            pe.wait_ge(s["router_split"], 1)
            pe.wait_ge(s["stack_made"], 1)
            pe.wait_ge(s["ident_r_made"], 1)
            for k in range(KD):
                nc.tensor.matmul(ps[0:2 * EXPERTS, 7, 0:TILES * P], wr_hl[:, k, :], x2_h[:, k, :], start=k == 0, stop=False)
                m = nc.tensor.matmul(ps[0:2 * EXPERTS, 7, 0:TILES * P], wr_hl[:, k, :], x2_l[:, k, :], start=False, stop=k == KD - 1)
            m.then_inc(s["logitsT_psum"], 1)
            pe.wait_ge(s["logitsT_read"], 1)
            for t in range(TILES):
                m = nc.tensor.matmul(ps[:, 7, 256 + t * EXPERTS:256 + (t + 1) * EXPERTS], logitsT[:, t * P:(t + 1) * P],
                                     stack[:, :], start=True, stop=True)
            m.then_inc(s["logits_psum"], 1)
            pe.wait_ge(s["chosen_ready"], 1)
            pe.wait_ge(s["dist_made"], 6)
            nc.tensor.matmul(ps[:, 7, 64:72], before[:, :], chosen[:, 0, :], start=True, stop=True)
            nc.tensor.matmul(ps[:, 7, 72:80], before[:, :], chosen[:, 1, :], start=True, stop=False)
            nc.tensor.matmul(ps[:, 7, 72:80], ones[:, :], chosen[:, 0, :], start=False, stop=True)
            nc.tensor.matmul(ps[:, 7, 80:88], ones[:, :], chosen[:, 0, :], start=True, stop=False)
            nc.tensor.matmul(ps[:, 7, 80:88], ones[:, :], chosen[:, 1, :], start=False, stop=True).then_inc(s["ranks_psum"], 1)

            def gather(i):
                pe.wait_ge(s["hot_ready"], i + 1)
                for q in range(2):
                    cut = slice(512 * q, 512 * q + 512)
                    for n, (t, rows) in enumerate(((0, rows_h), (0, rows_l), (1, rows_h), (1, rows_l))):
                        m = nc.tensor.matmul(ps[:, 2 + q, :], hot[:, t, :], rows[:, t, cut], start=n == 0, stop=n == 3)
                    m.then_inc(s["m_rows_psum"], 1)

            def turn_item(i):
                for q in range(2):
                    pe.wait_ge(s["m_rows_copied"], i * 2 + (q + 1))
                    for k in range(4):
                        c = (4 * q + k) * P
                        m = nc.tensor.transpose(ps[:, 2 + q, k * P:(k + 1) * P], item_rows[:, c:c + P], ident[:, :])
                    m.then_inc(s["m_item_psum"], 1)

            def turn_hot(i):
                for t in range(TILES):
                    m = nc.tensor.matmul(ps[:, 7, 256 + t * P:256 + (t + 1) * P], hot[:, t, :], ident_r[:, :], start=True, stop=True)
                m.then_inc(s["m_hotT_psum"], 1)

            def columns(slots, away, bank, halves=(0, 1)):
                for a in halves:
                    j = BASE_MOE + slots[a]
                    pe.wait_ge(s["slot_split"], away + (j + 1))
                    for k in range(4):
                        m = three(ps[:, bank, :], item_h[:, 4 * a + k, :], item_l[:, 4 * a + k, :],
                                  four(high, j)[:, k, :], four(low, j)[:, k, :], a + k == 0, a == 1 and k == 3)
                    m.then_inc(s["slot_used"], 1)

            def turn_acted(done):
                pe.wait_ge(s["m_acted"], done)
                pe.wait_ge(s["m_part_ready"], done)
                for k in range(4):
                    m = nc.tensor.transpose(ps[:, 6, k * P:(k + 1) * P], acted[:, k * P:(k + 1) * P], ident[:, :])
                m.then_inc(s["m_turned"], 1)

            def down(slots, away, done, start, stop, halves=(0, 1), x=(part_h, part_l)):
                pe.wait_ge(s["m_part_ready"], done + 1)
                for a in halves:
                    j = BASE_MOE + slots[a]
                    pe.wait_ge(s["slot_split"], away + (j + 1))
                    for k in range(2):
                        rows = slice((2 * a + k) * P, (2 * a + k + 1) * P)
                        for q in range(2):
                            cut = slice(512 * q, 512 * q + 512)
                            m = three(ps[:, 4 + q, :], x[0][:, rows], x[1][:, rows], two(high, j)[:, k, cut],
                                      two(low, j)[:, k, cut], start and a + k == 0, stop and a == 1 and k == 1)
                    m.then_inc(s["slot_used"], 1)

            pe.wait_ge(s["rows_ready"], TILES)
            gather(0)
            turn_item(0)
            pe.wait_ge(s["ranks_read"], 1)
            pe.wait_ge(s["m_item_ready"], 2)
            columns((-4, -3), 0, 0)
            columns((-2, -1), 0, 1)

            def item_body(i, last=False):
                at_slot = i * ITEM_SLOTS
                first = i * EX_CHUNKS

                def step(k, away, done, start, gather_next=False):
                    gate, up, low_ = step_slots(k)
                    bank = 2 * (k % 2)
                    columns(gate, away, bank)
                    pe.wait_ge(s["m_added"], i * 4 + 1)
                    turn_acted(done)
                    columns(up, away, bank + 1)
                    if gather_next:
                        gather(i + 1)
                        down(low_, away, done, start, False, (0,))
                        turn_item(i + 1)
                        down(low_, away, done, start, False, (1,))
                    elif last and k == EX_CHUNKS - 1:
                        down(low_, away, done, start, False, (0,))
                        turn_acted(done + 1)
                        down(low_, away, done, start, False, (1,))
                    else:
                        down(low_, away, done, start, False)

                step(1, at_slot, first + 1, True)
                turn_hot(i)
                with pe.Fori(0, 2) as trip:
                    step(2, at_slot + trip * 12, first + trip * 2 + 2, False)
                    step(3, at_slot + trip * 12, first + trip * 2 + 3, False)
                step(6, at_slot, first + 6, False, gather_next=not last)
                gate, up, low_ = step_slots(EX_CHUNKS, last)
                if not last:
                    pe.wait_ge(s["m_item_ready"], i * 2 + 4)
                    pe.wait_ge(s["m_acted"], first + EX_CHUNKS)
                    columns(gate, at_slot, 0)
                    turn_acted(first + EX_CHUNKS)
                    columns(up, at_slot, 1, (0,))
                down(low_, at_slot, first + EX_CHUNKS, False, True, x=(end_h, end_l) if last else (part_h, part_l))
                if not last:
                    columns(up, at_slot, 1, (1,))
                pe.wait_ge(s["m_hotT_ready"], i + 1)
                for n, (q, t) in enumerate(((0, 0), (0, 1), (1, 0), (1, 1))):
                    if t == 0:
                        pe.wait_ge(s["m_res_ready"], i * 2 + (q + 1))
                    to = ps[:, SCATTER_BANKS[n], :]
                    cut = slice(512 * q, 512 * q + 512)
                    nc.tensor.matmul(to, hotT[:, t, :], res_h[:, cut], start=True, stop=False)
                    nc.tensor.matmul(to, hotT[:, t, :], res_l[:, cut], start=False, stop=True).then_inc(s["m_scattered"], 1)

            with pe.Fori(0, EXPERTS - 1) as i:
                item_body(i)
            pe.wait_ge(s["plan_ready"], 1)
            extra = pe.value_load(plan[0:1, 0:1], min_val=0, max_val=MAX_OVER)
            with pe.If(extra > 0):
                with pe.Fori(0, extra) as v:
                    item_body(v + (EXPERTS - 1))
            item_body(extra + (EXPERTS - 1), last=True)


def kernel(x, g_mix, w_in, qn_a, kn_a, sinks_a, ln_b_g, ln_b_b, w_s, b_s, qn_c, kn_c, rel_bias_c, g_out, w_out,
           g_ffn, w_gate_d, w_up_d, w_down_d, w_router, w_gate_e, w_up_e, w_down_e):
    import numpy as np
    import concourse.bacc as bacc
    from concourse.bass_utils import run_bass_kernel_spmd

    n = lambda a: np.ascontiguousarray(a)
    qk = np.stack([np.asarray(a) for a in (qn_a, kn_a, qn_c, kn_c)], axis=-1)
    qk = np.concatenate([qk, qk], axis=1)
    line = np.asarray(rel_bias_c)[:, :, :LAST_REL + CHUNK][:, :, ::-1]
    line = np.concatenate([line, line[:, :, -1:].repeat(CHUNK, axis=2)], axis=2)
    rel = np.stack([np.concatenate([line[:, :, LAST_REL - q:LAST_REL - q + P],
                                    line[:, :, LAST_REL - P - q:LAST_REL + P - q]], axis=2) for q in range(P)], axis=1)
    ins = {
        "x": np.asarray(x)[0], "g_mix": g_mix, "w_in": w_in, "qk_gain": qk, "sinks": sinks_a, "ln_g": ln_b_g, "ln_b": ln_b_b,
        "w_s": np.transpose(np.asarray(w_s), (0, 3, 1, 2)), "b_s": np.transpose(np.asarray(b_s), (0, 2, 1)), "rel": rel,
        "g_out": g_out, "w_out": w_out, "g_ffn": g_ffn, "w_gate_d": w_gate_d, "w_up_d": w_up_d, "w_down_d": w_down_d,
        "w_router": np.asarray(w_router)[0].reshape(KD, P, EXPERTS).transpose(1, 0, 2).reshape(P, KD * EXPERTS), "w_gate_e": w_gate_e, "w_up_e": w_up_e, "w_down_e": w_down_e,
    }
    nc = bacc.Bacc("TRN2", target_bir_lowering=False, num_devices=1)
    arrays, args = {}, {}
    for name, a in ins.items():
        arrays[f"in_{name}"] = n(a)
        args[name] = nc.dram_tensor(f"in_{name}", arrays[f"in_{name}"].shape, F32, kind="ExternalInput").ap()
    args["out"] = nc.dram_tensor("out_x", (TILES * P, D), F32, kind="ExternalOutput").ap()
    hybrid_trunk(nc, **args)
    r = run_bass_kernel_spmd(nc, [arrays], core_ids=[0])
    return r.results[0]["out_x"].reshape(1, TILES * P, D)
```
